# Optimizing a Trainium2 kernel written in Bass

```python
import math
import jax, jax.numpy as jnp
from jax import lax
import numpy as np

D_MODEL = 1024
BATCH = 1
SEQ = 2048
DEPTH = 1

N_GROUPS_A = 4
GROUP_DIM_A = 64
W_A = N_GROUPS_A * GROUP_DIM_A
CONV_WIDTH = 3
N_HEADS_B = 4
HEAD_DIM_B = 64
W_B = N_HEADS_B * HEAD_DIM_B
Q_BLOCK = 128
K_BLOCK = 128
N_GROUPS_C = 4
GROUP_DIM_C = 64
W_C = N_GROUPS_C * GROUP_DIM_C
CHUNK = 128
N_BRANCH = 3
BRANCH_W = W_A
SPLIT_SIZES = (W_A, W_A, W_A, W_B, W_B, W_B, W_C, W_C, N_BRANCH * D_MODEL)
IN_COLS = 3 * W_A + 3 * W_B + 2 * W_C + N_BRANCH * D_MODEL
N_EXPERTS = 16
N_EXPERT_GROUPS = 4
EXPERTS_PER_GROUP = N_EXPERTS // N_EXPERT_GROUPS
TOP_K = 2
D_FF_EXPERT = 128
DEEPNORM_ALPHA = (2 * DEPTH) ** 0.25
DEEPNORM_BETA = (8 * DEPTH) ** -0.25
LN_EPS = 1e-5

kernel_name = "hybrid_conv_stickbreak_gmlp_grouped_moe_deepnorm"

def layer_norm(x, g, b):
    xf = x.astype(jnp.float32)
    mu = jnp.mean(xf, axis=-1, keepdims=True)
    var = jnp.mean(jnp.square(xf - mu), axis=-1, keepdims=True)
    y = (xf - mu) * lax.rsqrt(var + LN_EPS) * g.astype(jnp.float32) + b.astype(jnp.float32)
    return y.astype(x.dtype)

def short_conv_mixer(h, bg, cg, conv_w):
    u = cg * h
    y = lax.conv_general_dilated(
        u, conv_w[:, None, :], window_strides=(1,),
        padding=[(CONV_WIDTH - 1, 0)],
        dimension_numbers=("NWC", "WIO", "NWC"),
        feature_group_count=W_A)
    return bg * y

def stick_breaking_attention(q, k, v):
    b, s, h, dh = q.shape
    nb = s // Q_BLOCK
    scale = dh ** -0.5
    tri_in = (jnp.arange(K_BLOCK)[:, None] > jnp.arange(K_BLOCK)[None, :]).astype(jnp.float32)
    outs = []
    for i in range(nb):
        kv_len = (i + 1) * Q_BLOCK
        nk = kv_len // K_BLOCK
        q_blk = q[:, i * Q_BLOCK:(i + 1) * Q_BLOCK]
        z = jnp.einsum("bqhd,bkhd->bhqk", q_blk, k[:, :kv_len],
                       preferred_element_type=jnp.float32) * scale
        q_pos = i * Q_BLOCK + jnp.arange(Q_BLOCK)
        strict = jnp.arange(kv_len)[None, :] < q_pos[:, None]
        log_not = jnp.where(strict, -jax.nn.softplus(z), 0.0)
        ln_blk = log_not.reshape(b, h, Q_BLOCK, nk, K_BLOCK)
        within = jnp.einsum("bhqmj,js->bhqms", ln_blk, tri_in)
        tri_blk = (jnp.arange(nk)[:, None] > jnp.arange(nk)[None, :]).astype(jnp.float32)
        blk_after = jnp.einsum("bhqn,nm->bhqm", ln_blk.sum(-1), tri_blk)
        after = (within + blk_after[..., None]).reshape(b, h, Q_BLOCK, kv_len)
        a = jnp.where(strict, jnp.exp(jax.nn.log_sigmoid(z) + after), 0.0)
        outs.append(jnp.einsum("bhqk,bkhd->bqhd", a.astype(v.dtype), v[:, :kv_len]))
    out = jnp.concatenate(outs, axis=1)
    return out.reshape(b, s, h * dh)

def spatial_gating_mixer(u, v, w_s, b_s, ln_g, ln_b):
    b, s, _ = u.shape
    v = layer_norm(v, ln_g, ln_b)
    vc = v.reshape(b, s // CHUNK, CHUNK, N_GROUPS_C, GROUP_DIM_C)
    w = w_s * jnp.tril(jnp.ones((CHUNK, CHUNK), w_s.dtype))
    f = jnp.einsum("gts,bnsgc->bntgc", w, vc) + b_s.T[None, None, :, :, None]
    return u * f.reshape(b, s, W_C)

def hybrid_mixer(x, w_in, b_gate, conv_w, sg_w, sg_b, sg_ln_g, sg_ln_b, w_br, w_o):
    b, s, d = x.shape
    proj = x @ w_in
    offsets = np.cumsum(SPLIT_SIZES)[:-1].tolist()
    h_a, bg_a, cg_a, q, k, v, u_c, v_c, gate_logits = jnp.split(proj, offsets, axis=-1)
    y_a = short_conv_mixer(h_a, bg_a, cg_a, conv_w)
    y_b = stick_breaking_attention(q.reshape(b, s, N_HEADS_B, HEAD_DIM_B),
                                   k.reshape(b, s, N_HEADS_B, HEAD_DIM_B),
                                   v.reshape(b, s, N_HEADS_B, HEAD_DIM_B))
    y_c = spatial_gating_mixer(jax.nn.gelu(u_c), jax.nn.gelu(v_c), sg_w, sg_b, sg_ln_g, sg_ln_b)
    gates = jax.nn.sigmoid(gate_logits.reshape(b, s, N_BRANCH, d) + b_gate)
    branches = (y_a, y_b, y_c)
    merged = gates[:, :, 0] * (branches[0] @ w_br[0])
    for i in range(1, N_BRANCH):
        merged = merged + gates[:, :, i] * (branches[i] @ w_br[i])
    return merged @ w_o

def moe_ffn(x, w_router, router_bias, w_gate, w_up, w_down):
    b, s, d = x.shape
    xt = x.reshape(-1, d)
    n_tok = xt.shape[0]
    scores = jax.nn.sigmoid((xt @ w_router).astype(jnp.float32))
    sel = scores + router_bias.astype(jnp.float32)
    sel_g = sel.reshape(n_tok, N_EXPERT_GROUPS, EXPERTS_PER_GROUP)
    group_score = lax.top_k(sel_g, TOP_K)[0].sum(-1)
    best_group = jnp.argmax(group_score, axis=-1)
    group_mask = jax.nn.one_hot(best_group, N_EXPERT_GROUPS, dtype=jnp.bool_)
    masked_sel = jnp.where(group_mask[:, :, None], sel_g, -jnp.inf).reshape(n_tok, N_EXPERTS)
    _, top_idx = lax.top_k(masked_sel, TOP_K)
    top_s = jnp.take_along_axis(scores, top_idx, axis=-1)
    top_w = top_s / jnp.sum(top_s, axis=-1, keepdims=True)
    dense_w = jnp.sum(jax.nn.one_hot(top_idx, N_EXPERTS, dtype=jnp.float32) * top_w[..., None], axis=1)
    dense_w = dense_w.astype(xt.dtype)
    hidden = jax.nn.silu(jnp.einsum("td,edf->tef", xt, w_gate)) * jnp.einsum("td,edf->tef", xt, w_up)
    y = jnp.einsum("tef,efd->td", hidden * dense_w[:, :, None], w_down)
    return y.reshape(b, s, d)

def setup_inputs(seed: int = 0) -> dict:
    key = jax.random.key(seed)
    ks = jax.random.split(key, 24)
    f32 = jnp.float32
    nrm = lambda k, shape, sc: jax.random.normal(k, shape, f32) * sc
    return {
        "x": nrm(ks[0], (BATCH, SEQ, D_MODEL), 1.0),
        "ln_in_g": 1.0 + nrm(ks[1], (D_MODEL,), 0.05),
        "ln_in_b": nrm(ks[2], (D_MODEL,), 0.02),
        "w_in": nrm(ks[3], (DEPTH, D_MODEL, IN_COLS), D_MODEL ** -0.5),
        "b_gate": nrm(ks[4], (DEPTH, N_BRANCH, D_MODEL), 0.1),
        "conv_w": nrm(ks[5], (DEPTH, CONV_WIDTH, W_A), CONV_WIDTH ** -0.5),
        "sg_w": nrm(ks[6], (DEPTH, N_GROUPS_C, CHUNK, CHUNK), CHUNK ** -0.5),
        "sg_b": 1.0 + nrm(ks[7], (DEPTH, N_GROUPS_C, CHUNK), 0.1),
        "sg_ln_g": 1.0 + nrm(ks[8], (DEPTH, W_C), 0.05),
        "sg_ln_b": nrm(ks[9], (DEPTH, W_C), 0.02),
        "w_br": nrm(ks[10], (DEPTH, N_BRANCH, BRANCH_W, D_MODEL), (BRANCH_W ** -0.5) * DEEPNORM_BETA),
        "w_o": nrm(ks[11], (DEPTH, D_MODEL, D_MODEL), (D_MODEL ** -0.5) * DEEPNORM_BETA),
        "ln_mix_g": 1.0 + nrm(ks[12], (DEPTH, D_MODEL), 0.05),
        "ln_mix_b": nrm(ks[13], (DEPTH, D_MODEL), 0.02),
        "w_router": nrm(ks[14], (D_MODEL, N_EXPERTS), D_MODEL ** -0.5),
        "router_bias": nrm(ks[15], (N_EXPERTS,), 0.01),
        "w_gate": nrm(ks[16], (DEPTH, N_EXPERTS, D_MODEL, D_FF_EXPERT), D_MODEL ** -0.5),
        "w_up": nrm(ks[17], (DEPTH, N_EXPERTS, D_MODEL, D_FF_EXPERT), D_MODEL ** -0.5),
        "w_down": nrm(ks[18], (DEPTH, N_EXPERTS, D_FF_EXPERT, D_MODEL), (D_FF_EXPERT ** -0.5) * DEEPNORM_BETA),
        "ln_ffn_g": 1.0 + nrm(ks[19], (DEPTH, D_MODEL), 0.05),
        "ln_ffn_b": nrm(ks[20], (DEPTH, D_MODEL), 0.02),
    }

def reference(x, ln_in_g, ln_in_b, w_in, b_gate, conv_w, sg_w, sg_b, sg_ln_g, sg_ln_b,
              w_br, w_o, ln_mix_g, ln_mix_b, w_router, router_bias, w_gate, w_up, w_down,
              ln_ffn_g, ln_ffn_b):
    h = layer_norm(x, ln_in_g, ln_in_b)
    for l in range(DEPTH):
        mix = hybrid_mixer(h, w_in[l], b_gate[l], conv_w[l], sg_w[l], sg_b[l],
                           sg_ln_g[l], sg_ln_b[l], w_br[l], w_o[l])
        h = layer_norm(DEEPNORM_ALPHA * h + mix, ln_mix_g[l], ln_mix_b[l])
        ffn = moe_ffn(h, w_router, router_bias, w_gate[l], w_up[l], w_down[l])
        h = layer_norm(DEEPNORM_ALPHA * h + ffn, ln_ffn_g[l], ln_ffn_b[l])
    return h


_drawn_inputs = setup_inputs


def setup_inputs(seed=0):
    import zlib

    import numpy as np

    out = dict(_drawn_inputs(seed))
    spreads = {}
    factors = {'b_gate': 2.735, 'sg_ln_g': 4.643, 'sg_ln_b': 7.88, 'ln_ffn_b': 2.95}
    for name, (base, spread) in spreads.items():
        noise = np.random.default_rng([zlib.crc32(name.encode()), seed]).standard_normal(out[name].shape)
        drawn = base * np.exp(spread * noise) if base else spread * noise
        out[name] = __import__('jax').numpy.asarray(drawn.astype(out[name].dtype))
    for name, factor in factors.items():
        out[name] = (out[name] * factor).astype(out[name].dtype)
    return out
```

```python
from contextlib import ExitStack

import concourse.bass as bass
from concourse import mybir

ALU = mybir.AluOpType
ACT = mybir.ActivationFunctionType
AX_X = mybir.AxisListType.X
F32 = mybir.dt.float32
F32R = mybir.dt.float32r
U32 = mybir.dt.uint32

P = 128
D = 1024
KT = D // P
S = 2048
TILES = S // P
NT = 512
TT = S // NT
H, DH = 4, 64
G_C, CHUNK = 4, 128
W = 256
EPS = 1e-5
ALPHA = 2.0 ** 0.25

HA, BG, CG, Q, K, V, U_C, V_C, GATES = 0, 2, 4, 6, 8, 10, 12, 14, 16
COLS = 40


def f32(ap):
    return ap.bitcast(F32)


def input_norm(nc, sem, x, ln_g, ln_b, h_dram, hT_hi, hT_lo, ident):
    with ExitStack() as ctx:
        sb = lambda n, s, dt=F32: ctx.enter_context(nc.sbuf_tensor(n, s, dt))
        ps = lambda n, s, dt=F32: ctx.enter_context(nc.psum_tensor(n, s, dt))
        xt = sb("in_x", [P, 2, D])
        xn = sb("in_xn", [P, 2, D])
        hn = sb("in_h", [P, 2, D])
        g_row = sb("in_g", [P, D])
        b_row = sb("in_b", [P, D])
        stats = sb("in_stats", [P, 2, 12])
        mv = sb("in_mv", [P, 2, 4])
        half = sb("in_half", [P, 1])
        tp = ps("in_tp", [P, 2, KT, P])
        rows_loaded = sem("in_rows_loaded")
        x_loaded = [sem(f"in_x_loaded{b}") for b in range(2)]
        aggr_done = sem("in_aggr_done")
        stat_chain = sem("in_stat_chain")
        rstd_done = sem("in_rstd_done")
        normed = sem("in_normed")
        scaled = sem("in_scaled")
        h_done = sem("in_h_done")
        consts = sem("in_consts")
        h_stored = [sem(f"in_h_stored{b}") for b in range(2)]
        transposed = sem("in_transposed")
        hi_done = sem("in_hi_done")
        lo_done = sem("in_lo_done")
        x_t = x.rearrange("(t p) d -> t p d", p=P)
        h_t = h_dram.rearrange("(t p) d -> t p d", p=P)

        with nc.Block() as block:

            @block.sync
            def _(sp):
                sp.dma_start(xt[:, 0], x_t[0]).then_inc(x_loaded[0], 16)
                sp.dma_start(xt[:, 1], x_t[1]).then_inc(x_loaded[1], 16)
                sp.dma_start(g_row[:], ln_g.partition_broadcast(P)).then_inc(rows_loaded, 16)
                sp.dma_start(b_row[:], ln_b.partition_broadcast(P)).then_inc(rows_loaded, 16)
                for t in range(TILES):
                    b = t % 2
                    if t + 2 < TILES:
                        sp.wait_ge(normed, t + 1)
                        sp.dma_start(xt[:, b], x_t[t + 2]).then_inc(x_loaded[b], 16)
                    sp.wait_ge(h_done, t + 1)
                    sp.dma_start(h_t[t], hn[:, b]).then_inc(h_stored[b], 16)
                for b in range(2):
                    sp.wait_ge(h_stored[b], 16 * (TILES // 2))

            @block.gpsimd
            def _(pool):
                nc.gpsimd.memset(ident[:], 0.0).then_inc(consts, 1)
                pool.wait_ge(consts, 1)
                nc.gpsimd.affine_select(out=ident[:], in_=ident[:], compare_op=ALU.not_equal, fill=1.0, base=0,
                                        pattern=[[-1, P]], channel_multiplier=1).then_inc(consts, 1)
                nc.gpsimd.memset(half[:], -0.5).then_inc(consts, 1)
                pool.wait_ge(consts, 3)
                pool.wait_ge(rows_loaded, 32)
                for t in range(TILES):
                    b = t % 2
                    pool.wait_ge(aggr_done, t + 1)
                    nc.gpsimd.tensor_tensor(mv[:, b, 3:4], mv[:, b, 2:3], half[:], ALU.pow).then_inc(rstd_done, 1)
                    pool.wait_ge(normed, t + 1)
                    if t >= 2:
                        pool.wait_ge(h_stored[b], 16 * (t // 2))
                        pool.wait_ge(transposed, t - 1)
                    nc.gpsimd.tensor_tensor(hn[:, b], xn[:, b], g_row[:], ALU.mult).then_inc(scaled, 1)
                    pool.wait_ge(scaled, t + 1)
                    nc.gpsimd.tensor_tensor(hn[:, b], hn[:, b], b_row[:], ALU.add).then_inc(h_done, 1)

            @block.vector
            def _(dve):
                def statistics(t):
                    b = t % 2
                    dve.wait_ge(x_loaded[b], 16 * (t // 2 + 1))
                    for c in range(2):
                        nc.vector.bn_stats(stats[:, b, 6 * c:6 * c + 6], xt[:, b, 512 * c:512 * c + 512]
                                           ).then_inc(stat_chain, 1)
                    dve.wait_ge(stat_chain, 3 * t + 2)
                    nc.vector.bn_aggr(mv[:, b, 0:2], stats[:, b]).then_inc(stat_chain, 1)
                    dve.wait_ge(stat_chain, 3 * t + 3)
                    nc.vector.tensor_scalar(mv[:, b, 2:3], mv[:, b, 1:2], EPS, None, ALU.add).then_inc(aggr_done, 1)

                def low_part(t):
                    dve.wait_ge(hi_done, t + 1)
                    cols = slice(t * P, (t + 1) * P)
                    nc.vector.tensor_tensor(hT_lo[:, :, cols], tp[:, t % 2], f32(hT_hi[:, :, cols]),
                                            ALU.subtract).then_inc(lo_done, 1)

                statistics(0)
                for t in range(TILES):
                    b = t % 2
                    if t + 1 < TILES:
                        statistics(t + 1)
                    dve.wait_ge(rstd_done, t + 1)
                    if t >= 2:
                        dve.wait_ge(scaled, t - 1)
                    nc.vector.tensor_scalar(xn[:, b], xt[:, b], mv[:, b, 0:1], mv[:, b, 3:4],
                                            ALU.subtract, ALU.mult).then_inc(normed, 1)
                    if t >= 2:
                        low_part(t - 2)
                low_part(TILES - 2)
                low_part(TILES - 1)

            @block.tensor
            def _(pe):
                for t in range(TILES):
                    pe.wait_ge(h_done, t + 1)
                    if t >= 2:
                        pe.wait_ge(lo_done, t - 1)
                    for k in range(KT):
                        last = nc.tensor.transpose(tp[:, t % 2, k], hn[:, t % 2, k * P:(k + 1) * P], ident[:])
                    last.then_inc(transposed, 1)

            @block.scalar
            def _(act):
                for t in range(TILES):
                    act.wait_ge(transposed, t + 1)
                    nc.scalar.copy(hT_hi[:, :, t * P:(t + 1) * P], tp[:, t % 2]).then_inc(hi_done, 1)


def project(nc, sem, w_tiles, b_gate, projT, hT_hi, hT_lo):
    with ExitStack() as ctx:
        sb = lambda n, s, dt=F32: ctx.enter_context(nc.sbuf_tensor(n, s, dt))
        w_raw = sb("pj_w_raw", [P, 2, KT * P])
        w_hi = sb("pj_w_hi", [P, 2, KT * P], F32R)
        w_lo = sb("pj_w_lo", [P, 2, KT * P], F32R)
        ot = sb("pj_out", [P, 2, S])
        bg = sb("pj_bg", [P, COLS - GATES])
        acc = ctx.enter_context(nc.psum_tensor("pj_acc", [P, 2 * TT, NT], F32))
        w_loaded = [sem(f"pj_w_loaded{b}") for b in range(2)]
        bias_loaded = sem("pj_bias_loaded")
        passed = sem("pj_passed")
        hi_done = sem("pj_hi_done")
        lo_done = sem("pj_lo_done")
        product_done = sem("pj_product_done")
        evacuated = sem("pj_evacuated")
        stored = [sem(f"pj_stored{b}") for b in range(2)]

        with nc.Block() as block:

            @block.sync
            def _(sp):
                sp.dma_start(w_raw[:, 0], w_tiles[0]).then_inc(w_loaded[0], 16)
                sp.dma_start(w_raw[:, 1], w_tiles[1]).then_inc(w_loaded[1], 16)
                sp.dma_start(bg[:], b_gate).then_inc(bias_loaded, 16)

                def tile(m, b, load):
                    if load:
                        sp.wait_ge(lo_done, m + 1)
                        sp.dma_start(w_raw[:, b], w_tiles[bass.ds(m + 2, 1)].rearrange("o p n -> p (o n)")
                                     ).then_inc(w_loaded[b], 16)
                    sp.wait_ge(evacuated, TT * m + TT)
                    sp.dma_start(projT[bass.ds(m, 1)].rearrange("o p n -> p (o n)"), ot[:, b]
                                 ).then_inc(stored[b], 16)

                with sp.Fori(0, COLS // 2 - 1) as j:
                    tile(2 * j, 0, True)
                    tile(2 * j + 1, 1, True)
                tile(COLS - 2, 0, False)
                tile(COLS - 1, 1, False)
                for b in range(2):
                    sp.wait_ge(stored[b], 16 * (COLS // 2))

            @block.scalar
            def _(act):
                def high_part(n, b, m_half):
                    act.wait_ge(w_loaded[b], 16 * m_half)
                    nc.scalar.copy(w_hi[:, b], w_raw[:, b]).then_inc(hi_done, 1)

                def tile(m, b, half, gate, first, last):
                    if not last:
                        high_part(m + 1, 1 - b, half + 1 + b)
                    if not first:
                        act.wait_ge(stored[b], 16 * half)
                    for t in range(TT):
                        act.wait_ge(product_done, TT * m + t + 1)
                        act.sem_inc(passed, 1)
                        o, a = ot[:, b, t * NT:(t + 1) * NT], acc[:, b * TT + t]
                        if gate:
                            done = nc.scalar.activation(o, a, ACT.Sigmoid, bias=bg[:, bass.ds(m - GATES, 1)])
                        else:
                            done = nc.scalar.copy(o, a)
                        done.then_inc(evacuated, 1)

                high_part(0, 0, 1)
                tile(0, 0, 0, False, True, False)
                tile(1, 1, 0, False, True, False)
                with act.Fori(1, GATES // 2) as j:
                    tile(2 * j, 0, j, False, False, False)
                    tile(2 * j + 1, 1, j, False, False, False)
                act.wait_ge(bias_loaded, 16)
                with act.Fori(GATES // 2, COLS // 2 - 1) as j:
                    tile(2 * j, 0, j, True, False, False)
                    tile(2 * j + 1, 1, j, True, False, False)
                tile(COLS - 2, 0, COLS // 2 - 1, True, False, False)
                tile(COLS - 1, 1, COLS // 2 - 1, True, False, True)

            @block.vector
            def _(dve):
                with dve.Fori(0, COLS, 2) as i:
                    for b in range(2):
                        dve.wait_ge(hi_done, i + b + 1)
                        nc.vector.tensor_tensor(w_lo[:, b], w_raw[:, b], f32(w_hi[:, b]),
                                                ALU.subtract).then_inc(lo_done, 1)

            @block.tensor
            def _(pe):
                with pe.Fori(0, COLS, 2) as i:
                    for b in range(2):
                        pe.wait_ge(lo_done, i + b + 1)
                        for t in range(TT):
                            cols = slice(t * NT, (t + 1) * NT)
                            for k in range(KT):
                                w = slice(k * P, (k + 1) * P)
                                out = acc[:, b * TT + t]
                                nc.tensor.matmul(out, w_hi[:, b, w], hT_hi[:, k, cols], start=k == 0, stop=False)
                                nc.tensor.matmul(out, w_hi[:, b, w], hT_lo[:, k, cols], start=False, stop=False)
                                last = nc.tensor.matmul(out, w_lo[:, b, w], hT_hi[:, k, cols],
                                                        start=False, stop=k == KT - 1)
                            last.then_inc(product_done, 1)



def local_mixers(nc, sem, projT, conv_w, sg_w, sg_b, sg_g, sg_bb, v_nat, yT, ident):
    CW = 3
    NCH = S // CHUNK
    with ExitStack() as ctx:
        sb = lambda n, s, dt=F32: ctx.enter_context(nc.sbuf_tensor(n, s, dt))
        ps = lambda n, s, dt=F32: ctx.enter_context(nc.psum_tensor(n, s, dt))
        ha = sb("lm_ha", [P, 2, S])
        bgt = sb("lm_bg", [P, 2, S])
        cg = sb("lm_cg", [P, 2, S])
        vT = sb("lm_vT", [P, 2, S])
        uT = sb("lm_uT", [P, 2, S])
        vcT = sb("lm_vcT", [P, 2, S])
        ya = sb("lm_ya", [P, 2, S])
        cw = sb("lm_cw", [P, 2, CW])
        wsT = sb("lm_wsT", [P, G_C, CHUNK])
        bias = sb("lm_bias", [P, 2, CHUNK])
        g_row = sb("lm_g", [P, W])
        b_row = sb("lm_b", [P, W])
        half = sb("lm_half", [P, 1])
        stats = sb("lm_stats", [P, 2, 6])
        mv = sb("lm_mv", [P, 2, 4])
        vn = sb("lm_vn", [P, 2, W])
        vs = sb("lm_v", [P, 2, W])
        fb = sb("lm_fb", [P, 2, W])
        tp = ps("lm_tp", [P, 2, 4, P])
        fT = ps("lm_fT", [P, 2, 4, P])
        v_loaded = sem("lm_v_loaded")
        vc_loaded = sem("lm_vc_loaded")
        u_loaded = sem("lm_u_loaded")
        conv_loaded = sem("lm_conv_loaded")
        small_loaded = sem("lm_small_loaded")
        consts = sem("lm_consts")
        ws_masked = sem("lm_ws_masked")
        vc_gelu = sem("lm_vc_gelu")
        u_gelu = sem("lm_u_gelu")
        turned = sem("lm_turned")
        stat_chain = sem("lm_stat_chain")
        rstd_done = sem("lm_rstd_done")
        normed = sem("lm_normed")
        scaled = sem("lm_scaled")
        vn_done = sem("lm_vn_done")
        v_copied = sem("lm_v_copied")
        v_stored = [sem(f"lm_v_stored{b}") for b in range(2)]
        mixed = sem("lm_mixed")
        biased = sem("lm_biased")
        yc_done = sem("lm_yc_done")
        conv_chain = sem("lm_conv_chain")
        y_stored = sem("lm_y_stored")
        cols2 = lambda m: projT[m:m + 2].rearrange("m p s -> p m s")
        v_t = v_nat.rearrange("(n p) c -> n p c", p=P)

        with nc.Block() as block:

            @block.sync
            def _(sp):
                sp.dma_start(vcT[:], cols2(V_C)).then_inc(vc_loaded, 16)
                sp.dma_start(vT[:], cols2(V)).then_inc(v_loaded, 16)
                sp.dma_start(wsT[:], sg_w).then_inc(small_loaded, 16)
                for g in range(G_C):
                    sp.dma_start(bias[64 * (g % 2):64 * (g % 2) + 64, g // 2], sg_b[g].partition_broadcast(64)
                                 ).then_inc(small_loaded, 16)
                sp.dma_start(g_row[:], sg_g.partition_broadcast(P)).then_inc(small_loaded, 16)
                sp.dma_start(b_row[:], sg_bb.partition_broadcast(P)).then_inc(small_loaded, 16)
                sp.dma_start(cw[:], conv_w).then_inc(conv_loaded, 16)
                sp.dma_start(ha[:], cols2(HA)).then_inc(conv_loaded, 16)
                sp.dma_start(cg[:], cols2(CG)).then_inc(conv_loaded, 16)
                sp.dma_start(bgt[:], cols2(BG)).then_inc(conv_loaded, 16)
                sp.dma_start(uT[:], cols2(U_C)).then_inc(u_loaded, 16)
                for n in range(NCH):
                    sp.wait_ge(v_copied, n + 1)
                    sp.dma_start(v_t[n], vs[:, n % 2]).then_inc(v_stored[n % 2], 16)
                sp.wait_ge(conv_chain, 10)
                sp.dma_start(yT[:, 0:2], ya[:]).then_inc(y_stored, 16)
                sp.wait_ge(yc_done, NCH)
                sp.dma_start(yT[:, 4:6], uT[:]).then_inc(y_stored, 16)
                for b in range(2):
                    sp.wait_ge(v_stored[b], 16 * (NCH // 2))
                sp.wait_ge(y_stored, 32)

            @block.gpsimd
            def _(pool):
                nc.gpsimd.memset(half[:], -0.5).then_inc(consts, 1)
                pool.wait_ge(small_loaded, 7 * 16)
                nc.gpsimd.affine_select(out=wsT[:], in_=wsT[:], compare_op=ALU.is_ge, fill=0.0, base=0,
                                        pattern=[[0, G_C], [1, CHUNK]], channel_multiplier=-1
                                        ).then_inc(ws_masked, 1)
                pool.wait_ge(consts, 1)
                for n in range(NCH):
                    b = n % 2
                    pool.wait_ge(stat_chain, 3 * n + 3)
                    nc.gpsimd.tensor_tensor(mv[:, b, 3:4], mv[:, b, 2:3], half[:], ALU.pow).then_inc(rstd_done, 1)
                    pool.wait_ge(normed, n + 1)
                    nc.gpsimd.tensor_tensor(vn[:, b], vn[:, b], g_row[:], ALU.mult).then_inc(scaled, 1)
                    pool.wait_ge(scaled, n + 1)
                    nc.gpsimd.tensor_tensor(vn[:, b], vn[:, b], b_row[:], ALU.add).then_inc(vn_done, 1)

            @block.scalar
            def _(act):
                act.wait_ge(vc_loaded, 16)
                for q in range(4):
                    s = vcT[:, :, q * NT:(q + 1) * NT]
                    nc.scalar.activation(s, s, ACT.Gelu_apprx_tanh).then_inc(vc_gelu, 1)
                act.wait_ge(u_loaded, 16)
                for q in range(4):
                    s = uT[:, :, q * NT:(q + 1) * NT]
                    nc.scalar.activation(s, s, ACT.Gelu_apprx_tanh).then_inc(u_gelu, 1)
                for n in range(NCH):
                    b = n % 2
                    act.wait_ge(normed, n + 1)
                    if n >= 2:
                        act.wait_ge(v_stored[b], 16 * (n // 2))
                    nc.scalar.copy(vs[:, b], tp[:, b, 2:4].rearrange("p c t -> p (c t)")).then_inc(v_copied, 1)

            @block.tensor
            def _(pe):
                def mix(n):
                    pe.wait_ge(vn_done, n + 1)
                    if n >= 2:
                        pe.wait_ge(biased, n - 1)
                    for g in range(G_C):
                        r = 64 * (g % 2)
                        last = nc.tensor.matmul(fT[r:r + 64, n % 2, g // 2], vn[:, n % 2, g * 64:(g + 1) * 64],
                                                wsT[:, g], start=True, stop=True)
                    last.then_inc(mixed, 1)

                pe.wait_ge(v_loaded, 16)
                pe.wait_ge(ws_masked, 1)
                for n in range(NCH):
                    pe.wait_ge(vc_gelu, n // 4 + 1)
                    if n >= 2:
                        pe.wait_ge(v_copied, n - 1)
                    cols = slice(n * CHUNK, (n + 1) * CHUNK)
                    for c in range(2):
                        nc.tensor.transpose(tp[:, n % 2, c], vcT[:, c, cols], ident[:])
                        last = nc.tensor.transpose(tp[:, n % 2, 2 + c], vT[:, c, cols], ident[:])
                    last.then_inc(turned, 1)
                    if n >= 1:
                        mix(n - 1)
                mix(NCH - 1)

            @block.vector
            def _(dve):
                def statistics(n):
                    b = n % 2
                    dve.wait_ge(turned, n + 1)
                    if n >= 2:
                        dve.wait_ge(rstd_done, n - 1)
                    vc = tp[:, b, 0:2].rearrange("p c t -> p (c t)")
                    nc.vector.bn_stats(stats[:, b], vc).then_inc(stat_chain, 1)
                    dve.wait_ge(stat_chain, 3 * n + 1)
                    nc.vector.bn_aggr(mv[:, b, 0:2], stats[:, b]).then_inc(stat_chain, 1)
                    dve.wait_ge(stat_chain, 3 * n + 2)
                    nc.vector.tensor_scalar(mv[:, b, 2:3], mv[:, b, 1:2], EPS, None, ALU.add).then_inc(stat_chain, 1)

                def normalise(n):
                    b = n % 2
                    dve.wait_ge(rstd_done, n + 1)
                    if n >= 2:
                        dve.wait_ge(mixed, n - 1)
                    nc.vector.tensor_scalar(vn[:, b], tp[:, b, 0:2].rearrange("p c t -> p (c t)"), mv[:, b, 0:1],
                                            mv[:, b, 3:4], ALU.subtract, ALU.mult).then_inc(normed, 1)

                def gate(n):
                    b = n % 2
                    dve.wait_ge(mixed, n + 1)
                    if n >= 2:
                        dve.wait_ge(yc_done, n - 1)
                    f = fb[:, b].rearrange("p (c t) -> p c t", c=2)
                    nc.vector.tensor_tensor(f, fT[:, b, 0:2], bias[:], ALU.add).then_inc(biased, 1)
                    dve.wait_ge(biased, n + 1)
                    dve.wait_ge(u_gelu, n // 4 + 1)
                    u = uT[:, :, n * CHUNK:(n + 1) * CHUNK]
                    nc.vector.tensor_tensor(u, u, f, ALU.mult).then_inc(yc_done, 1)

                def convolve(i):
                    c, step = divmod(i, 5)
                    u, y = ha[:, c], ya[:, c]
                    dve.wait_ge(conv_loaded, 64)
                    if i:
                        dve.wait_ge(conv_chain, i)
                    if step == 0:
                        op = nc.vector.tensor_tensor(u, cg[:, c], u, ALU.mult)
                    elif step == 1:
                        op = nc.vector.tensor_scalar(y, u, cw[:, c, 2:3], None, ALU.mult)
                    elif step in (2, 3):
                        d = step - 1
                        op = nc.vector.scalar_tensor_tensor(out=y[:, d:S], in0=u[:, 0:S - d], scalar=cw[:, c, 2 - d:3 - d],
                                                            in1=y[:, d:S], op0=ALU.mult, op1=ALU.add)
                    else:
                        op = nc.vector.tensor_tensor(y, y, bgt[:, c], ALU.mult)
                    op.then_inc(conv_chain, 1)

                dve.wait_ge(small_loaded, 7 * 16)
                for n in range(NCH + 2):
                    if n < NCH:
                        statistics(n)
                    if n >= 2:
                        gate(n - 2)
                    if n < NCH:
                        normalise(n)
                    if 4 <= n < 14:
                        convolve(n - 4)


def attention(nc, sem, projT, v_nat, yT):
    SCALE = DH ** -0.5
    R = 8
    RZ = 4
    HEADS = 2
    SP_CAP = 44.0

    LN, SP, HI, OWN, SUM, REST, EXP, MASK, AV, OUT = 1, 2, 3, 4, 5, 6, 6, 7, 8, 9

    chain = [[], []]
    for c, tiles in enumerate(((3, 0), (2, 1))):
        for qt in tiles:
            blocks = list(range(4 * qt + 3, -1, -1))
            for kb in blocks:
                d = kb - 4 * qt
                chain[c].append((c, qt, kb, d, min(P * max(d, 0), NT // 2), kb == blocks[0], kb == 0))
    head_items = [x for pair in zip(*chain) for x in pair]
    PER_HEAD = len(head_items)
    items = [(s,) + x for s in range(HEADS) for x in head_items]
    N = len(items)

    with ExitStack() as ctx:
        sb = lambda n, s, dt=F32: ctx.enter_context(nc.sbuf_tensor(n, s, dt))
        ps = lambda n, s, dt=F32: ctx.enter_context(nc.psum_tensor(n, s, dt))
        q_raw = sb("at_q_raw", [P, S])
        k_raw = sb("at_k_raw", [P, S])
        q_hi = sb("at_q_hi", [P, HEADS, S], F32R)
        q_lo = sb("at_q_lo", [P, HEADS, S], F32R)
        k_st = sb("at_k", [P, HEADS, S], F32R)
        v_sb = sb("at_v", [P, HEADS, TILES, DH])
        neg_own = sb("at_neg_own", [P, P], F32R)
        neg_rest = sb("at_neg_rest", [P, P], F32R)
        z_sb = sb("at_z", [P, R, NT])
        e_sb = sb("at_e", [P, R, NT])
        sp_sb = sb("at_sp", [P, R, NT])
        sp_hi = sb("at_sp_hi", [P, R, NT], F32R)
        sp_lo = sb("at_sp_lo", [P, R, NT], F32R)
        t_sb = sb("at_t", [P, R, NT])
        a_sb = sb("at_a", [P, R, NT])
        y_sb = sb("at_y", [DH, 2, NT])
        z_ps = ps("at_z_ps", [P, RZ, NT])
        sum_ps = ps("at_sum_ps", [P, 2, NT])
        y_ps = ps("at_y_ps", [P, 2, NT])

        consts = sem("at_consts")
        passed = sem("at_passed")
        q_loaded = sem("at_q_loaded")
        k_loaded = sem("at_k_loaded")
        v_loaded = sem("at_v_loaded")
        prep = sem("at_prep")
        z_done = sem("at_z_done")
        z_copied = sem("at_z_copied")
        e_done = sem("at_e_done")
        l_done = sem("at_l_done")
        sp_done = sem("at_sp_done")
        masked = sem("at_masked")
        hi_done = sem("at_hi_done")
        lo_done = sem("at_lo_done")
        own_done = sem("at_own_done")
        t_done = sem("at_t_done")
        rest_done = sem("at_rest_done")
        a_done = sem("at_a_done")
        a_masked = sem("at_a_masked")
        av_done = sem("at_av_done")
        y_done = sem("at_y_done")
        y_stored = [sem(f"at_y_stored{c}") for c in range(2)]

        proj_rows = projT.rearrange("m p s -> (m p) s")
        v_heads = v_nat.rearrange("(n p) (h d) -> p n h d", p=P, d=DH)
        y_heads = yT[:, 2:4].rearrange("(r p) m s -> m r p s", p=DH)
        diag_before = [sum(1 for x in items[:n] if x[4] >= 0) for n in range(N + 1)]
        last_before = [sum(1 for x in items[:n] if x[7]) for n in range(N + 1)]
        DIAG, LASTS = diag_before[N], last_before[N]
        lasts = [n for n in range(N) if items[n][7]]
        chain_tile = lambda n: sum(1 for m in lasts if m < n and items[m][1] == items[n][1])

        def tile_before(n):
            own = [x for x, m in enumerate(lasts) if items[m][1] == items[n][1]]
            k = chain_tile(n)
            return own[k - 1] if k else own[-1] - LASTS

        PARTS = S // NT
        PREP = 4 * PARTS

        ringed = dict(act=(z_copied, e_done, l_done, a_done, y_done), dve=(sp_done, hi_done, lo_done, t_done), pe=(z_done, own_done, av_done))
        done = lambda n: R + n + 1
        freed = lambda n: n + 1

        with nc.Block() as block:

            @block.sync
            def _(sp):
                def load(h, slot, first):
                    for half in range(2):
                        r = slice(half * DH, half * DH + DH)
                        sp.dma_start(q_raw[r], proj_rows[bass.ds(Q * P + h * DH, DH)]).then_inc(q_loaded, 16)
                        sp.dma_start(k_raw[r], proj_rows[bass.ds(K * P + h * DH, DH)]).then_inc(k_loaded, 16)
                    sp.dma_start(v_sb[:, slot], v_heads[:, :, bass.ds(h, 1)].rearrange("p n o d -> p n (o d)")
                                 ).then_inc(v_loaded, 16)

                def store(n, count, pair):
                    slot, c, qt = items[n][0:3]
                    sp.wait_ge(y_done, count)
                    sp.dma_start(y_heads[bass.ds(pair, 1), slot, :, qt * NT:(qt + 1) * NT
                                         ].rearrange("o p s -> p (o s)"), y_sb[:, c]).then_inc(y_stored[c], 16)

                for c in range(2):
                    sp.sem_inc(y_stored[c], 16)
                load(0, 0, True)
                with sp.Fori(0, H // HEADS) as j:
                    sp.wait_ge(prep, PREP * (HEADS * j + 1))
                    load(HEADS * j + 1, 1, False)
                    for x, n in enumerate(lasts):
                        if x == LASTS // 2:
                            sp.wait_ge(prep, PREP * (HEADS * j + 2))
                            load((HEADS * j + 2) % H, 0, False)
                        store(n, j * LASTS + done(x), j)
                for c in range(2):
                    sp.wait_ge(y_stored[c], 16 * (H // HEADS) * (LASTS // 2) + 16)

            @block.gpsimd
            def _(pool):
                nc.gpsimd.memset(e_sb[:, 0, 0:P], -1.0).then_inc(consts, 1)
                pool.wait_ge(consts, 1)
                nc.gpsimd.affine_select(out=z_sb[:, 0, 0:P], in_=e_sb[:, 0, 0:P], compare_op=ALU.is_ge, fill=0.0,
                                        base=0, pattern=[[-1, P]], channel_multiplier=1).then_inc(consts, 1)
                nc.gpsimd.affine_select(out=z_sb[:, 0, P:2 * P], in_=e_sb[:, 0, 0:P], compare_op=ALU.is_gt, fill=0.0,
                                        base=0, pattern=[[1, P]], channel_multiplier=-1).then_inc(consts, 1)

                def causal(tile, d, c0):
                    return nc.gpsimd.affine_select(out=tile, in_=tile, compare_op=ALU.is_gt, fill=0.0,
                                                   base=c0 - d * P, pattern=[[1, NT - c0]], channel_multiplier=-1)

                with pool.Fori(0, H // HEADS) as j:
                    for s in range(N + MASK):
                        if SP <= s < N + SP:
                            n = s - SP
                            slot, c, qt, kb, d, c0, first, last = items[n]
                            tile = sp_sb[:, n % R, c0:NT]
                            if d >= 0:
                                pool.wait_ge(sp_done, j * N + done(n))
                                pool.sem_inc(passed, 1)
                                causal(tile, d, c0).then_inc(masked, 1)
                        if MASK <= s + 1 < N + MASK and items[s + 1 - MASK][4] >= 0:
                            n = s + 1 - MASK
                            slot, c, qt, kb, d, c0, first, last = items[n]
                            pool.wait_ge(a_done, j * N + done(n))
                            pool.sem_inc(passed, 1)
                            causal(a_sb[:, n % R, c0:NT], d, c0).then_inc(a_masked, 1)

            @block.scalar
            def _(act):
                for s in ringed["act"]:
                    act.sem_inc(s, R)
                nc.scalar.preload_act_table_set("natural_log_exp_and_others")
                act.wait_ge(consts, 5)
                with act.Fori(0, H // HEADS) as j:
                    for s in range(N + OUT):
                        if s < N:
                            n = s
                            c0 = items[n][5]
                            z = z_ps[:, n % RZ, c0:NT]
                            act.wait_ge(z_done, j * N + done(n))
                            act.wait_ge(t_done, j * N + freed(n))
                            nc.scalar.copy(z_sb[:, n % R, c0:NT], z).then_inc(z_copied, 1)
                        if LN <= s < N + LN:
                            n = s - LN
                            e = e_sb[:, n % R, items[n][5]:NT]
                            act.wait_ge(e_done, j * N + done(n))
                            nc.scalar.activation(e, e, ACT.Ln, bias=1.0).then_inc(l_done, 1)
                        if s < N:
                            n = s
                            c0 = items[n][5]
                            act.wait_ge(sp_done, j * N + freed(n))
                            nc.scalar.activation(e_sb[:, n % R, c0:NT], z_ps[:, n % RZ, c0:NT], ACT.Exp
                                                 ).then_inc(e_done, 1)
                        if EXP <= s < N + EXP:
                            n = s - EXP
                            c0 = items[n][5]
                            act.wait_ge(t_done, j * N + done(n))
                            act.wait_ge(av_done, j * N + freed(n))
                            nc.scalar.activation(a_sb[:, n % R, c0:NT], t_sb[:, n % R, c0:NT], ACT.Exp
                                                 ).then_inc(a_done, 1)
                        if s >= OUT and items[s - OUT][7]:
                            n = s - OUT
                            c = items[n][1]
                            act.wait_ge(av_done, j * N + done(n))
                            act.wait_ge(y_stored[c], 16 * (j * (LASTS // 2) + chain_tile(n) + 1))
                            nc.scalar.copy(y_sb[:, c], y_ps[0:DH, c]).then_inc(y_done, 1)

            @block.tensor
            def _(pe):
                for s in ringed["pe"]:
                    pe.sem_inc(s, R)
                pe.sem_inc(rest_done, R)
                pe.wait_ge(consts, 5)
                with pe.Fori(0, H // HEADS) as j:
                    for s in range(-1, N + AV):
                        if s + 1 < N:
                            n = s + 1
                            slot, c, qt, kb, d, c0, first, last = items[n]
                            if n % PER_HEAD == 0:
                                pe.wait_ge(prep, PREP * (HEADS * j + slot + 1))
                            pe.wait_ge(e_done, j * N + done(n - RZ))
                            qs = slice(qt * NT + c0, (qt + 1) * NT)
                            out = z_ps[:, n % RZ, c0:NT]
                            kw = k_st[:, slot, kb * P:(kb + 1) * P]
                            nc.tensor.matmul(out, kw, q_hi[:, slot, qs], start=True, stop=False)
                            nc.tensor.matmul(out, kw, q_lo[:, slot, qs], start=False, stop=True).then_inc(z_done, 1)
                        if REST <= s < N + REST:
                            n = s - REST
                            slot, c, qt, kb, d, c0, first, last = items[n]
                            out = sum_ps[:, c, c0:NT]
                            pe.wait_ge(t_done, j * N + done(n))
                            for part in (sp_hi, sp_lo):
                                mm = nc.tensor.matmul(out, neg_rest[:], part[:, n % R, c0:NT], start=False,
                                                      stop=last and part is sp_lo, skip_group_check=True)
                            mm.then_inc(rest_done, 1)
                        if OWN <= s < N + OWN:
                            n = s - OWN
                            slot, c, qt, kb, d, c0, first, last = items[n]
                            out = sum_ps[:, c, c0:NT]
                            pe.wait_ge(lo_done, j * N + done(n))
                            for part in (sp_hi, sp_lo):
                                mm = nc.tensor.matmul(out, neg_own[:], part[:, n % R, c0:NT],
                                                      start=first and part is sp_hi, stop=False,
                                                      skip_group_check=True)
                            mm.then_inc(own_done, 1)
                        if AV <= s < N + AV:
                            n = s - AV
                            slot, c, qt, kb, d, c0, first, last = items[n]
                            pe.wait_ge(a_done, j * N + done(n))
                            if d >= 0:
                                pe.wait_ge(a_masked, j * DIAG + diag_before[n] + 1)
                            if first:
                                pe.wait_ge(y_done, j * LASTS + done(tile_before(n)))
                            nc.tensor.matmul(y_ps[0:DH, c, c0:NT], v_sb[:, slot, kb], a_sb[:, n % R, c0:NT],
                                             start=first, stop=last, skip_group_check=True).then_inc(av_done, 1)

            @block.vector
            def _(dve):
                for s in ringed["dve"]:
                    dve.sem_inc(s, R)
                dve.wait_ge(consts, 3)
                nc.vector.tensor_copy(neg_own[:], z_sb[:, 0, 0:P]).then_inc(consts, 1)
                nc.vector.tensor_copy(neg_rest[:], z_sb[:, 0, P:2 * P]).then_inc(consts, 1)

                def split(i, head, slot):
                    part, step = divmod(i, 4)
                    x = slice(part * NT, (part + 1) * NT)
                    lower = slice(DH, P)
                    if i == 0:
                        dve.wait_ge(q_loaded, 32 * (head + 1))
                        dve.wait_ge(k_loaded, 32 * (head + 1))
                        dve.wait_ge(v_loaded, 16 * (head + 1))
                    if step == 0:
                        op = nc.vector.tensor_scalar(q_hi[:, slot, x], q_raw[:, x], SCALE, None, ALU.mult)
                    elif step == 1:
                        op = nc.vector.tensor_copy(k_st[:, slot, x], k_raw[:, x])
                    elif step == 2:
                        dve.wait_ge(prep, PREP * head + 4 * part + 1)
                        op = nc.vector.scalar_tensor_tensor(out=q_lo[:, slot, x], in0=q_raw[:, x], scalar=SCALE,
                                                            in1=f32(q_hi[:, slot, x]), op0=ALU.mult,
                                                            op1=ALU.subtract)
                    else:
                        dve.wait_ge(prep, PREP * head + 4 * part + 2)
                        op = nc.vector.tensor_tensor(k_st[lower, slot, x], k_raw[lower, x],
                                                     f32(k_st[lower, slot, x]), ALU.subtract)
                    op.then_inc(prep, 1)

                for i in range(PREP):
                    split(i, 0, 0)
                with dve.Fori(0, H // HEADS) as j:
                    for s in range(N + SUM):
                        if HI <= s < N + HI:
                            n = s - HI
                            d, c0 = items[n][4:6]
                            if d >= 0:
                                dve.wait_ge(masked, j * DIAG + diag_before[n] + 1)
                            dve.wait_ge(sp_done, j * N + done(n))
                            dve.wait_ge(rest_done, j * N + freed(n))
                            nc.vector.tensor_copy(sp_hi[:, n % R, c0:NT], sp_sb[:, n % R, c0:NT]
                                                  ).then_inc(hi_done, 1)
                        if SP <= s < N + SP:
                            n = s - SP
                            c0 = items[n][5]
                            dve.wait_ge(l_done, j * N + done(n))
                            dve.wait_ge(z_copied, j * N + done(n))
                            dve.wait_ge(lo_done, j * N + freed(n))
                            nc.vector.scalar_tensor_tensor(out=sp_sb[:, n % R, c0:NT], in0=e_sb[:, n % R, c0:NT],
                                                           scalar=SP_CAP, in1=z_sb[:, n % R, c0:NT], op0=ALU.min,
                                                           op1=ALU.max).then_inc(sp_done, 1)
                        if HI <= s < N + HI:
                            n = s - HI
                            c0 = items[n][5]
                            dve.wait_ge(hi_done, j * N + done(n))
                            nc.vector.tensor_tensor(sp_lo[:, n % R, c0:NT], sp_sb[:, n % R, c0:NT],
                                                    f32(sp_hi[:, n % R, c0:NT]), ALU.subtract).then_inc(lo_done, 1)
                        if SUM <= s < N + SUM:
                            n = s - SUM
                            slot, c, qt, kb, d, c0, first, last = items[n]
                            dve.wait_ge(own_done, j * N + done(n))
                            dve.wait_ge(a_done, j * N + freed(n))
                            nc.vector.tensor_tensor(t_sb[:, n % R, c0:NT], sum_ps[:, c, c0:NT],
                                                    z_sb[:, n % R, c0:NT], ALU.add).then_inc(t_done, 1)
                        for slot in range(HEADS):
                            i = s - slot * PER_HEAD - 16
                            if 0 <= i < PREP:
                                split(i, HEADS * j + slot + 1, 1 - slot)


E = 16


def merge_branches(nc, sem, projT, yT, w_br, mergedT):
    B = 3
    KB = W // P
    with ExitStack() as ctx:
        sb = lambda n, s, dt=F32: ctx.enter_context(nc.sbuf_tensor(n, s, dt))
        w_raw = sb("mb_w_raw", [P, B * KB, D])
        w_hi = sb("mb_w_hi", [P, B * KB, D], F32R)
        w_lo = sb("mb_w_lo", [P, B * KB, D], F32R)
        y_raw = sb("mb_y_raw", [P, B * KB, NT])
        y_hi = sb("mb_y_hi", [P, 2, B * KB, NT], F32R)
        y_lo = sb("mb_y_lo", [P, 2, B * KB, NT], F32R)
        gate = sb("mb_gate", [P, 4, B, NT])
        part = sb("mb_part", [P, 2, B, NT])
        acc = ctx.enter_context(nc.psum_tensor("mb_acc", [P, 2, B, NT], F32))
        w_loaded = [sem(f"mb_w_loaded{i}") for i in range(B)]
        y_loaded = sem("mb_y_loaded")
        gate_loaded = [sem(f"mb_gate_loaded{b}") for b in range(4)]
        w_hi_done = sem("mb_w_hi_done")
        w_lo_done = sem("mb_w_lo_done")
        y_hi_done = sem("mb_y_hi_done")
        y_lo_done = sem("mb_y_lo_done")
        product_done = sem("mb_product_done")
        gated = sem("mb_gated")
        summed = sem("mb_summed")
        stored = [sem(f"mb_stored{b}") for b in range(2)]
        gates_dram = projT[GATES:COLS].rearrange("(i m) p s -> m p i s", i=B)
        n_items = TT * KT

        with nc.Block() as block:

            @block.sync
            def _(sp):
                def load_y(t):
                    sp.dma_start(y_raw[:], yT[:, :, bass.ds(t * NT, NT)]).then_inc(y_loaded, 16)

                def load_gates(t, m):
                    sp.dma_start(gate[:, m % 4], gates_dram[m, :, :, bass.ds(t * NT, NT)]
                                 ).then_inc(gate_loaded[m % 4], 16)

                load_y(0)
                for i in range(B):
                    r = slice(i * KB, (i + 1) * KB)
                    sp.dma_start(w_raw[:, r], w_br[:, r]).then_inc(w_loaded[i], 16)
                for m in range(4):
                    load_gates(0, m)
                for b in range(2):
                    sp.sem_inc(stored[b], 16)
                with sp.Fori(0, TT // 2) as j:
                    for b in range(2):
                        t = 2 * j + b
                        for m in range(KT):
                            n = t * KT + m
                            if m == 0:
                                sp.wait_ge(y_lo_done, t + 1)
                                load_y((t + 1) % TT)
                            sp.wait_ge(summed, 2 * n + 2)
                            sp.dma_start(mergedT[m, :, bass.ds(t * NT, NT)], part[:, m % 2, 0]
                                         ).then_inc(stored[m % 2], 16)
                            ahead = t if m < KT - 4 else (t + 1) % TT
                            load_gates(ahead, (m + 4) % KT)
                for b in range(2):
                    sp.wait_ge(stored[b], 16 * (n_items // 2) + 16)
                for b in range(4):
                    sp.wait_ge(gate_loaded[b], 16 * (n_items // 4 + 1))
                sp.wait_ge(y_loaded, 16 * (TT + 1))

            @block.scalar
            def _(act):
                def y_high(t, b):
                    act.wait_ge(y_loaded, 16 * (t + 1))
                    nc.scalar.copy(y_hi[:, b], y_raw[:]).then_inc(y_hi_done, 1)

                y_high(0, 0)
                for i in range(B):
                    r = slice(i * KB, (i + 1) * KB)
                    act.wait_ge(w_loaded[i], 16)
                    nc.scalar.copy(w_hi[:, r], w_raw[:, r]).then_inc(w_hi_done, 1)
                with act.Fori(0, TT // 2) as j:
                    for b in range(2):
                        t = 2 * j + b
                        act.wait_ge(product_done, t * KT + 1)
                        y_high(t + 1, 1 - b)

            @block.vector
            def _(dve):
                def y_low(t, b):
                    dve.wait_ge(y_hi_done, t + 1)
                    nc.vector.tensor_tensor(y_lo[:, b], y_raw[:], f32(y_hi[:, b]), ALU.subtract
                                            ).then_inc(y_lo_done, 1)

                dve.sem_inc(gated, 2 * B)
                y_low(0, 0)
                for i in range(B):
                    r = slice(i * KB, (i + 1) * KB)
                    dve.wait_ge(w_hi_done, i + 1)
                    nc.vector.tensor_tensor(w_lo[:, r], w_raw[:, r], f32(w_hi[:, r]), ALU.subtract
                                            ).then_inc(w_lo_done, 1)
                with dve.Fori(0, TT // 2) as j:
                    for b in range(2):
                        t = 2 * j + b
                        for m in range(KT):
                            n = t * KT + m
                            if m == 3:
                                y_low(t + 1, 1 - b)
                            dve.wait_ge(gate_loaded[m % 4], 16 * (t * (KT // 4) + m // 4 + 1))
                            dve.wait_ge(product_done, n + 2)
                            dve.wait_ge(stored[m % 2], 16 * (t * (KT // 2) + m // 2 + 1))
                            for i in range(B):
                                nc.vector.tensor_tensor(part[:, m % 2, i], acc[:, m % 2, i], gate[:, m % 4, i],
                                                        ALU.mult).then_inc(gated, 1)
                            for i in range(1, B):
                                dve.wait_ge(gated, B * (n + 2) + i + 1)
                                if i > 1:
                                    dve.wait_ge(summed, 2 * n + 1)
                                nc.vector.tensor_tensor(part[:, m % 2, 0], part[:, m % 2, 0], part[:, m % 2, i],
                                                        ALU.add).then_inc(summed, 1)

            @block.tensor
            def _(pe):
                pe.sem_inc(product_done, 1)
                pe.wait_ge(w_lo_done, B)
                with pe.Fori(0, TT // 2) as j:
                    for b in range(2):
                        t = 2 * j + b
                        pe.wait_ge(y_lo_done, t + 1)
                        for m in range(KT):
                            n = t * KT + m
                            pe.wait_ge(gated, B * n + B)
                            for i in range(B):
                                for k in range(KB):
                                    ik = i * KB + k
                                    out, c = acc[:, m % 2, i], slice(m * P, (m + 1) * P)
                                    nc.tensor.matmul(out, w_hi[:, ik, c], y_hi[:, b, ik], start=k == 0, stop=False)
                                    nc.tensor.matmul(out, w_hi[:, ik, c], y_lo[:, b, ik], start=False, stop=False)
                                    last = nc.tensor.matmul(out, w_lo[:, ik, c], y_hi[:, b, ik],
                                                            start=False, stop=k == KB - 1)
                            last.then_inc(product_done, 1)


def mix_out(nc, sem, mergedT, w_o, h_dram, ln_g, ln_b, w_router, h2_dram, logits, ident):
    with ExitStack() as ctx:
        sb = lambda n, s, dt=F32: ctx.enter_context(nc.sbuf_tensor(n, s, dt))
        ps = lambda n, s, dt=F32: ctx.enter_context(nc.psum_tensor(n, s, dt))
        w_raw = sb("mo_w_raw", [P, 2, D])
        w_hi = sb("mo_w_hi", [P, KT, D], F32R)
        w_lo = sb("mo_w_lo", [P, KT, D], F32R)
        wr = sb("mo_w_router", [P, KT, E])
        m_raw = sb("mo_m_raw", [P, 2, KT, P])
        m_hi = sb("mo_m_hi", [P, 2, KT, P], F32R)
        m_lo = sb("mo_m_lo", [P, 2, KT, P], F32R)
        h = sb("mo_h", [P, 2, D])
        g_row = sb("mo_g", [P, D])
        b_row = sb("mo_b", [P, D])
        x2 = sb("mo_x2", [P, 2, D])
        h2 = sb("mo_h2", [P, 2, D])
        h2T = sb("mo_h2T", [P, KT, P])
        zeros = sb("mo_zeros", [P, D])
        stats = sb("mo_stats", [P, 2, 12])
        mv = sb("mo_mv", [P, 2, 4])
        half = sb("mo_half", [P, 1])
        out = ps("mo_out", [P, 2, 2, NT])
        tp = ps("mo_tp", [P, KT, P])
        lg = ps("mo_lg", [P, 2, NT])
        w_loaded = [sem(f"mo_w_loaded{b}") for b in range(2)]
        rows_loaded = sem("mo_rows_loaded")
        m_loaded = [sem(f"mo_m_loaded{b}") for b in range(2)]
        h_loaded = [sem(f"mo_h_loaded{b}") for b in range(2)]
        w_hi_done = sem("mo_w_hi_done")
        w_lo_done = sem("mo_w_lo_done")
        m_hi_done = sem("mo_m_hi_done")
        m_lo_done = sem("mo_m_lo_done")
        product_done = sem("mo_product_done")
        residual = sem("mo_residual")
        stat_chain = sem("mo_stat_chain")
        consts = sem("mo_consts")
        rstd_done = sem("mo_rstd_done")
        normed = sem("mo_normed")
        scaled = sem("mo_scaled")
        h2_done = sem("mo_h2_done")
        h2_stored = [sem(f"mo_h2_stored{b}") for b in range(2)]
        pad_stored = sem("mo_pad_stored")
        turned = sem("mo_turned")
        h2T_done = sem("mo_h2T_done")
        logit_done = sem("mo_logit_done")
        logits_copied = sem("mo_logits_copied")
        m_t = mergedT.rearrange("m p (t c) -> t p m c", c=P)
        h_t = h_dram.rearrange("(t p) d -> t p d", p=P)
        h2_t = h2_dram.rearrange("(t p) d -> t p d", p=P)

        with nc.Block() as block:

            @block.sync
            def _(sp):
                def load(t, b):
                    sp.dma_start(m_raw[:, b], m_t[t]).then_inc(m_loaded[b], 16)
                    sp.dma_start(h[:, b], h_t[t]).then_inc(h_loaded[b], 16)

                for k in range(2):
                    sp.dma_start(w_raw[:, k], w_o[:, k]).then_inc(w_loaded[k], 16)
                load(0, 0)
                for k in range(2, KT):
                    sp.wait_ge(w_lo_done, k - 1)
                    sp.dma_start(w_raw[:, k % 2], w_o[:, k]).then_inc(w_loaded[k % 2], 16)
                load(1, 1)
                sp.dma_start(g_row[:], ln_g.partition_broadcast(P)).then_inc(rows_loaded, 16)
                sp.dma_start(b_row[:], ln_b.partition_broadcast(P)).then_inc(rows_loaded, 16)
                sp.dma_start(wr[:], w_router).then_inc(rows_loaded, 16)
                sp.wait_ge(consts, 2)
                sp.dma_start(h2_t[TILES], zeros[:]).then_inc(pad_stored, 16)
                for t in range(TILES):
                    if t + 2 < TILES:
                        sp.wait_ge(residual, 2 * t + 2)
                        load(t + 2, t % 2)
                    sp.wait_ge(h2_done, t + 1)
                    sp.dma_start(h2_t[t], h2[:, t % 2]).then_inc(h2_stored[t % 2], 16)
                for b in range(2):
                    sp.wait_ge(h2_stored[b], 16 * (TILES // 2))
                sp.wait_ge(pad_stored, 16)

            @block.gpsimd
            def _(pool):
                nc.gpsimd.memset(half[:], -0.5).then_inc(consts, 1)
                nc.gpsimd.memset(zeros[:], 0.0).then_inc(consts, 1)
                pool.wait_ge(consts, 2)
                pool.wait_ge(rows_loaded, 48)
                for t in range(TILES):
                    b = t % 2
                    pool.wait_ge(stat_chain, 4 * t + 4)
                    nc.gpsimd.tensor_tensor(mv[:, b, 3:4], mv[:, b, 2:3], half[:], ALU.pow).then_inc(rstd_done, 1)
                    pool.wait_ge(normed, t + 1)
                    if t >= 2:
                        pool.wait_ge(h2_stored[b], 16 * (t // 2))
                        pool.wait_ge(turned, t - 1)
                    nc.gpsimd.tensor_tensor(h2[:, b], x2[:, b], g_row[:], ALU.mult).then_inc(scaled, 1)
                    pool.wait_ge(scaled, t + 1)
                    nc.gpsimd.tensor_tensor(h2[:, b], h2[:, b], b_row[:], ALU.add).then_inc(h2_done, 1)

            @block.scalar
            def _(act):
                def m_high(t):
                    b = t % 2
                    act.wait_ge(m_loaded[b], 16 * (t // 2 + 1))
                    if t >= 2:
                        act.wait_ge(product_done, 2 * t - 2)
                    nc.scalar.copy(m_hi[:, b], m_raw[:, b]).then_inc(m_hi_done, 1)

                def turn(t):
                    act.wait_ge(turned, t + 1)
                    if t >= 1:
                        act.wait_ge(logit_done, t)
                    nc.scalar.copy(h2T[:], tp[:]).then_inc(h2T_done, 1)

                for k in range(KT):
                    act.wait_ge(w_loaded[k % 2], 16 * (k // 2 + 1))
                    nc.scalar.copy(w_hi[:, k], w_raw[:, k % 2]).then_inc(w_hi_done, 1)
                m_high(0)
                m_high(1)
                for t in range(TILES):
                    if t + 2 < TILES:
                        m_high(t + 2)
                    if t >= 1:
                        turn(t - 1)
                turn(TILES - 1)
                act.wait_ge(logit_done, TILES)
                for b in range(2):
                    nc.scalar.copy(logits[:, b::2], lg[:, b, 0:TILES // 2 * E].rearrange("p (t e) -> p t e", e=E)
                                   ).then_inc(logits_copied, 1)

            @block.vector
            def _(dve):
                def m_low(t):
                    b = t % 2
                    dve.wait_ge(m_hi_done, t + 1)
                    nc.vector.tensor_tensor(m_lo[:, b], m_raw[:, b], f32(m_hi[:, b]), ALU.subtract
                                            ).then_inc(m_lo_done, 1)

                for k in range(KT):
                    dve.wait_ge(w_hi_done, k + 1)
                    nc.vector.tensor_tensor(w_lo[:, k], w_raw[:, k % 2], f32(w_hi[:, k]), ALU.subtract
                                            ).then_inc(w_lo_done, 1)
                m_low(0)
                m_low(1)
                for t in range(TILES):
                    b = t % 2
                    dve.wait_ge(h_loaded[b], 16 * (t // 2 + 1))
                    if t >= 2:
                        dve.wait_ge(scaled, t - 1)
                    for c in range(2):
                        x = slice(c * NT, (c + 1) * NT)
                        dve.wait_ge(product_done, 2 * t + c + 1)
                        nc.vector.scalar_tensor_tensor(out=x2[:, b, x], in0=h[:, b, x], scalar=ALPHA,
                                                       in1=out[:, b, c], op0=ALU.mult, op1=ALU.add
                                                       ).then_inc(residual, 1)
                    for c in range(2):
                        dve.wait_ge(residual, 2 * t + c + 1)
                        nc.vector.bn_stats(stats[:, b, 6 * c:6 * c + 6], x2[:, b, c * NT:(c + 1) * NT]
                                           ).then_inc(stat_chain, 1)
                    dve.wait_ge(stat_chain, 4 * t + 2)
                    nc.vector.bn_aggr(mv[:, b, 0:2], stats[:, b]).then_inc(stat_chain, 1)
                    dve.wait_ge(stat_chain, 4 * t + 3)
                    nc.vector.tensor_scalar(mv[:, b, 2:3], mv[:, b, 1:2], EPS, None, ALU.add).then_inc(stat_chain, 1)
                    if t + 2 < TILES:
                        m_low(t + 2)
                    dve.wait_ge(rstd_done, t + 1)
                    nc.vector.tensor_scalar(x2[:, b], x2[:, b], mv[:, b, 0:1], mv[:, b, 3:4],
                                            ALU.subtract, ALU.mult).then_inc(normed, 1)

            @block.tensor
            def _(pe):
                def route(t):
                    pe.wait_ge(h2_done, t + 1)
                    if t >= 1:
                        pe.wait_ge(h2T_done, t)
                    for k in range(KT):
                        last = nc.tensor.transpose(tp[:, k], h2[:, t % 2, k * P:(k + 1) * P], ident[:])
                    last.then_inc(turned, 1)

                def logit(t):
                    pe.wait_ge(h2T_done, t + 1)
                    cols = slice(t // 2 * E, (t // 2 + 1) * E)
                    for k in range(KT):
                        last = nc.tensor.matmul(lg[:, t % 2, cols], h2T[:, k], wr[:, k], start=k == 0,
                                                stop=k == KT - 1, skip_group_check=True)
                    last.then_inc(logit_done, 1)

                pe.wait_ge(w_lo_done, KT)
                for t in range(TILES):
                    b = t % 2
                    pe.wait_ge(m_lo_done, t + 1)
                    for c in range(2):
                        if t >= 2:
                            pe.wait_ge(residual, 2 * (t - 2) + c + 1)
                        for k in range(KT):
                            o, x = out[:, b, c], slice(c * NT, (c + 1) * NT)
                            nc.tensor.matmul(o, m_hi[:, b, k], w_hi[:, k, x], start=k == 0, stop=False)
                            nc.tensor.matmul(o, m_lo[:, b, k], w_hi[:, k, x], start=False, stop=False)
                            last = nc.tensor.matmul(o, m_hi[:, b, k], w_lo[:, k, x], start=False, stop=k == KT - 1)
                        last.then_inc(product_done, 1)
                        if c == 0 and t >= 2:
                            logit(t - 2)
                    if t >= 1:
                        route(t - 1)
                logit(TILES - 2)
                route(TILES - 1)
                logit(TILES - 1)


EG = 4
FF = 128
GUC, DNC = KT, EG
E_TILES = TILES + EG - 1
META = 8


def dispatch(nc, sem, logits, router_bias, order, meta, table, gu_w, dn_w, gu_raw, dn_raw, gu_loaded, dn_loaded):
    with ExitStack() as ctx:
        sb = lambda n, s, dt=F32: ctx.enter_context(nc.sbuf_tensor(n, s, dt))
        TG = TILES * EG
        bias = sb("dp_bias", [P, E])
        score = sb("dp_score", [P, TG, EG])
        sel = sb("dp_sel", [P, TG, EG])
        rank = sb("dp_rank", [P, TG, EG])
        cmp = sb("dp_cmp", [P, TG])
        taken = sb("dp_taken", [P, TG, EG])
        g_score = sb("dp_g_score", [P, TG])
        g_rank = sb("dp_g_rank", [P, TG])
        best = sb("dp_best", [P, TG])
        before = sb("dp_before", [P, P])
        ones = sb("dp_ones", [P, P])
        tile_sum = sb("dp_tile_sum", [P, TG])
        upto = sb("dp_upto", [P, TG])
        place = sb("dp_place", [P, TG])
        slot = sb("dp_slot", [P, TILES])
        slot_u = sb("dp_slot_u", [P, TILES], U32)
        denom = sb("dp_denom", [P, TILES])
        rdenom = sb("dp_rdenom", [P, TILES])
        weight = sb("dp_weight", [P, TILES, EG])
        steps = sb("dp_steps", [P, TILES])
        over = sb("dp_over", [P, EG, TILES])
        g_tiles = sb("dp_g_tiles", [P, EG])
        start = sb("dp_start", [P, EG])
        tile_no = sb("dp_tile_no", [P, E_TILES])
        past = sb("dp_past", [P, 3, E_TILES])
        group = sb("dp_group", [P, E_TILES])
        need = sb("dp_need", [P, 4])
        pad = sb("dp_pad", [P, E_TILES, META])
        row = sb("dp_row", [P, TILES, META])
        ps = ctx.enter_context(nc.psum_tensor("dp_ps", [P, 2, NT], F32))
        loaded = sem("dp_loaded")
        consts = sem("dp_consts")
        scored = sem("dp_scored")
        chain = sem("dp_chain")
        counted = sem("dp_counted")
        padded = sem("dp_padded")
        row_done = sem("dp_row_done")
        scattered = sem("dp_scattered")
        meta_loaded = sem("dp_meta_loaded")
        order_t = order.rearrange("(t p) w -> p t w", p=P)

        with nc.Block() as block:

            @block.sync
            def _(sp):
                sp.dma_start(bias[:], router_bias.partition_broadcast(P)).then_inc(loaded, 16)
                sp.dma_start(gu_raw[:, 0], gu_w[0]).then_inc(gu_loaded, 16)
                sp.dma_start(dn_raw[:, 0], dn_w[0]).then_inc(dn_loaded, 16)
                sp.wait_ge(consts, 6)
                sp.dma_start(order_t, pad[:]).then_inc(padded, 16)
                sp.wait_ge(scattered, 16 * TILES)
                sp.dma_start(meta[:], order_t).then_inc(meta_loaded, 16)
                sp.wait_ge(meta_loaded, 16)

            @block.gpsimd
            def _(pool):
                nc.gpsimd.memset(pad[:], 0.0).then_inc(consts, 1)
                nc.gpsimd.memset(row[:], 0.0).then_inc(consts, 1)
                nc.gpsimd.memset(ones[:], 1.0).then_inc(consts, 1)
                pool.wait_ge(consts, 3)
                nc.gpsimd.affine_select(out=before[:], in_=ones[:], compare_op=ALU.is_gt, fill=0.0, base=0,
                                        pattern=[[1, P]], channel_multiplier=-1).then_inc(consts, 1)
                nc.gpsimd.iota(pad[:, :, 0].bitcast(U32), [[0, E_TILES]], base=S, channel_multiplier=1
                               ).then_inc(consts, 1)
                nc.gpsimd.iota(row[:, :, 0].bitcast(U32), [[P, TILES]], base=0, channel_multiplier=1
                               ).then_inc(consts, 1)
                nc.gpsimd.iota(steps[:], [[P, TILES]], base=0, channel_multiplier=0,
                               allow_small_or_imprecise_dtypes=True).then_inc(consts, 1)
                nc.gpsimd.iota(tile_no[:], [[1, E_TILES]], base=0, channel_multiplier=0,
                               allow_small_or_imprecise_dtypes=True).then_inc(consts, 1)
                pool.wait_ge(padded, 16)
                pool.wait_ge(row_done, 2)
                for t in range(TILES):
                    nc.gpsimd.indirect_dma_start(out=order, out_offset=bass.IndirectOffsetOnAxis(slot_u[:, t:t + 1], 0),
                                                 in_=row[:, t], in_offset=None).then_inc(scattered, 16)

            @block.scalar
            def _(act):
                nc.scalar.activation(score[:].rearrange("p (t g) e -> p t (g e)", g=EG), logits[:], ACT.Sigmoid
                                     ).then_inc(scored, 1)

            @block.tensor
            def _(pe):
                pe.wait_ge(consts, 4)
                pe.wait_ge(counted, 1)
                nc.tensor.matmul(ps[:, 0, 0:TG], before[:], best[:], start=True, stop=True)
                nc.tensor.matmul(ps[:, 1, 0:TG], ones[:], best[:], start=True, stop=True).then_inc(counted, 1)

            @block.vector
            def _(dve):
                count = [0]

                def link(op):
                    count[0] += 1
                    op.then_inc(chain, 1)
                    dve.wait_ge(chain, count[0])

                def ranks(out, x, n):
                    for i in range(n):
                        for j in [j for j in range(n) if j != i]:
                            first = j == (0 if i else 1)
                            op = ALU.is_gt if j > i else ALU.is_ge
                            if first:
                                link(nc.vector.tensor_tensor(out[:, :, i], x[:, :, j], x[:, :, i], op))
                            else:
                                tmp = cmp[:, 0:x.shape[1]]
                                link(nc.vector.tensor_tensor(tmp, x[:, :, j], x[:, :, i], op))
                                link(nc.vector.tensor_tensor(out[:, :, i], out[:, :, i], tmp, ALU.add))

                by_token = lambda a: a.rearrange("p (t g) e -> p t (g e)", g=EG)
                by_group = lambda a: a.rearrange("p (t g) -> p t g", g=EG)
                dve.wait_ge(loaded, 16)
                dve.wait_ge(scored, 1)
                link(nc.vector.tensor_tensor(by_token(sel[:]), by_token(score[:]),
                                             bias[:].unsqueeze(1).to_broadcast([P, TILES, E]), ALU.add))
                ranks(rank[:], sel[:], EG)
                link(nc.vector.tensor_scalar(taken[:], rank[:], 2.0, None, ALU.is_lt))
                link(nc.vector.tensor_tensor(rank[:], sel[:], taken[:], ALU.mult))
                link(nc.vector.tensor_reduce(g_score[:], rank[:], AX_X, ALU.add))
                ranks(by_group(g_rank[:]), by_group(g_score[:]), EG)
                nc.vector.tensor_scalar(best[:], g_rank[:], 1.0, None, ALU.is_lt).then_inc(counted, 1)
                dve.wait_ge(counted, 1)
                link(nc.vector.tensor_tensor(taken[:], taken[:], score[:], ALU.mult))
                link(nc.vector.tensor_tensor(taken[:], taken[:], best[:].unsqueeze(2).to_broadcast([P, TG, EG]),
                                             ALU.mult))
                link(nc.vector.tensor_reduce(denom[:], by_token(taken[:]), AX_X, ALU.add))
                link(nc.vector.reciprocal(rdenom[:], denom[:]))
                link(nc.vector.tensor_reduce(weight[:], taken[:].rearrange("p (t g) e -> p t e g", g=EG),
                                             AX_X, ALU.add))
                dve.wait_ge(consts, 8)
                nc.vector.tensor_tensor(row[:, :, 1:1 + EG], weight[:],
                                        rdenom[:].unsqueeze(2).to_broadcast([P, TILES, EG]), ALU.mult
                                        ).then_inc(row_done, 1)
                dve.wait_ge(counted, 2)
                link(nc.vector.tensor_copy(tile_sum[:], ps[:, 1, 0:TG]))
                for g in range(EG):
                    x = by_group(tile_sum[:])[:, :, g]
                    link(nc.vector.tensor_tensor_scan(by_group(upto[:])[:, :, g], ones[:, 0:TILES], x, 0.0,
                                                      ALU.mult, ALU.add))
                link(nc.vector.tensor_tensor(place[:], upto[:], tile_sum[:], ALU.subtract))
                link(nc.vector.tensor_tensor(place[:], place[:], ps[:, 0, 0:TG], ALU.add))
                total = by_group(upto[:])[:, TILES - 1]
                link(nc.vector.tensor_tensor(over[:], total.unsqueeze(2).to_broadcast([P, EG, TILES]),
                                             steps[:].unsqueeze(1).to_broadcast([P, EG, TILES]), ALU.is_gt))
                link(nc.vector.tensor_reduce(g_tiles[:], over[:], AX_X, ALU.add))
                link(nc.vector.memset(start[:, 0:1], 0.0))
                for g in range(1, EG):
                    link(nc.vector.tensor_tensor(start[:, g:g + 1], start[:, g - 1:g], g_tiles[:, g - 1:g], ALU.add))
                link(nc.vector.scalar_tensor_tensor(out=by_group(place[:]),
                                                    in0=start[:].unsqueeze(1).to_broadcast([P, TILES, EG]),
                                                    scalar=float(P), in1=by_group(place[:]), op0=ALU.mult, op1=ALU.add))
                link(nc.vector.tensor_tensor(place[:], place[:], best[:], ALU.mult))
                link(nc.vector.tensor_reduce(slot[:], by_group(place[:]), AX_X, ALU.add))
                nc.vector.tensor_copy(slot_u[:], slot[:]).then_inc(row_done, 1)
                link(nc.vector.tensor_tensor(past[:], tile_no[:].unsqueeze(1).to_broadcast([P, 3, E_TILES]),
                                             start[:, 1:EG].unsqueeze(2).to_broadcast([P, 3, E_TILES]), ALU.is_ge))
                link(nc.vector.tensor_reduce(group[:], past[:].rearrange("p g t -> p t g"), AX_X, ALU.add))
                link(nc.vector.tensor_copy(table[:, 0:E_TILES], group[0:1, :]))
                for c, a_tile in enumerate((GUC, 1)):
                    link(nc.vector.tensor_scalar(need[:, 2 * c:2 * c + 2], start[:, 1:3], float(a_tile), 1.0,
                                                 ALU.mult, ALU.add))
                link(nc.vector.tensor_copy(table[:, E_TILES:E_TILES + 4], need[0:1, :]))


def experts(nc, sem, h2_dram, meta, table, gu_w, dn_w, gu_raw, dn_raw, gu_loaded, dn_loaded, ln_g, ln_b, out, ident):
    RING = 4
    XR = 4
    with ExitStack() as ctx:
        sb = lambda n, s, dt=F32: ctx.enter_context(nc.sbuf_tensor(n, s, dt))
        ps = lambda n, s, dt=F32: ctx.enter_context(nc.psum_tensor(n, s, dt))
        w_hi = sb("ex_w_hi", [P, RING, D], F32R)
        w_lo = sb("ex_w_lo", [P, RING, D], F32R)
        x = sb("ex_x", [P, XR, D])
        o = sb("ex_o", [P, 2, D])
        xT_hi = sb("ex_xT_hi", [P, 2, KT, P], F32R)
        xT_lo = sb("ex_xT_lo", [P, 2, KT, P], F32R)
        act_g = sb("ex_gate", [P, EG * FF])
        hid = sb("ex_hid", [P, EG * FF])
        hT_sb = sb("ex_hT_sb", [P, EG, P])
        g_row = sb("ex_g", [P, D])
        b_row = sb("ex_b", [P, D])
        stats = sb("ex_stats", [P, 12])
        mv = sb("ex_mv", [P, 4])
        half = sb("ex_half", [P, 1])
        gather_ids = sb("ex_gather_ids", [P, XR, 1], U32)
        store_ids = sb("ex_store_ids", [P, 2, 1], U32)
        gu = ps("ex_gu", [P, 2, NT])
        y = ps("ex_y", [P, 2, NT])
        xT = ps("ex_xT", [P, KT, P])
        hT = ps("ex_hT", [P, EG, P])
        rows_loaded = sem("ex_rows_loaded")
        consts = sem("ex_consts")
        passed = sem("ex_passed")
        passed_dve = sem("ex_passed_dve")
        gather_ids_done = sem("ex_gather_ids_done")
        store_ids_done = sem("ex_store_ids_done")
        x_loaded = [sem(f"ex_x_loaded{q}") for q in range(XR)]
        w_high = sem("ex_w_high")
        w_split = sem("ex_w_split")
        w_used = sem("ex_w_used")
        x_turned = sem("ex_x_turned")
        x_high = sem("ex_x_high")
        x_split = sem("ex_x_split")
        gate_done = sem("ex_gate_done")
        hid_done = sem("ex_hid_done")
        h_turned = sem("ex_h_turned")
        h_copied = sem("ex_h_copied")
        down_done = sem("ex_down_done")
        residual = sem("ex_residual")
        stat_chain = sem("ex_stat_chain")
        rstd_done = sem("ex_rstd_done")
        normed = sem("ex_normed")
        scaled = sem("ex_scaled")
        shifted = sem("ex_shifted")
        stored = sem("ex_stored")
        o_free = sem("ex_o_free")
        T = E_TILES

        def steps(eng, step):
            step(0, 0, True, False, False)
            step(1, 1, True, True, False)
            with eng.Fori(0, (T - 3) // XR) as j:
                for i in range(XR):
                    step(XR * j + 2 + i, (2 + i) % XR, True, True, True)
            step(T - 1, (T - 1) % XR, True, True, True)
            step(T, T % XR, False, True, True)
            step(T + 1, (T + 1) % XR, False, False, True)

        def chunk(s, i):
            return GUC * s + i

        def group_of(eng, t):
            return eng.value_load(table[0:1, bass.ds(t, 1)], min_val=0, max_val=EG - 1)

        meta_ids = meta[:, :, 0].bitcast(U32)

        with nc.Block() as block:

            @block.sync
            def _(sp):
                need = [sp.value_load(table[0:1, E_TILES + i:E_TILES + i + 1], min_val=1,
                                      max_val=GUC * T + 1) for i in range(4)]
                sp.dma_start(g_row[:], ln_g.partition_broadcast(P)).then_inc(rows_loaded, 16)
                sp.dma_start(b_row[:], ln_b.partition_broadcast(P)).then_inc(rows_loaded, 16)
                sp.wait_ge(x_loaded[1], 16)
                sp.wait_ge(gu_loaded, 16)
                sp.dma_start(gu_raw[:, 1], gu_w[1]).then_inc(gu_loaded, 16)
                sp.wait_ge(dn_loaded, 16)
                sp.dma_start(dn_raw[:, 1], dn_w[1]).then_inc(dn_loaded, 16)
                for g in (2, 3):
                    sp.wait_ge(gu_loaded, 16 * g)
                    sp.wait_ge(w_split, need[g - 2])
                    sp.dma_start(gu_raw[:, g % 2], gu_w[g]).then_inc(gu_loaded, 16)
                for g in (2, 3):
                    sp.wait_ge(dn_loaded, 16 * g)
                    sp.wait_ge(down_done, need[2 + g - 2])
                    sp.dma_start(dn_raw[:, g % 2], dn_w[g]).then_inc(dn_loaded, 16)
                sp.wait_ge(gu_loaded, 16 * EG)
                sp.wait_ge(dn_loaded, 16 * EG)

            @block.gpsimd
            def _(pool):
                def gather(t, q):
                    nc.gpsimd.tensor_copy(gather_ids[:, q], meta_ids[:, bass.ds(t, 1)]).then_inc(gather_ids_done, 1)
                    pool.wait_ge(gather_ids_done, t + 1)
                    pool.sem_inc(passed, 1)
                    nc.gpsimd.indirect_dma_start(out=x[:, q], out_offset=None, in_=h2_dram,
                                                 in_offset=bass.IndirectOffsetOnAxis(gather_ids[:, q], 0)
                                                 ).then_inc(x_loaded[q], 16)

                nc.gpsimd.memset(half[:], -0.5).then_inc(consts, 1)
                pool.wait_ge(consts, 1)
                pool.sem_inc(o_free, 2)
                gather(0, 0)

                def step(s, q, has_gu, has_dn, has_norm):
                    b = q % 2
                    if has_gu and not (isinstance(s, int) and s == T - 1):
                        if has_norm:
                            pool.wait_ge(residual, 2 * (s - 1))
                        gather(s + 1, (q + 1) % XR)
                    if has_norm:
                        t = s - 2
                        pool.wait_ge(stat_chain, 4 * t + 4)
                        nc.gpsimd.tensor_tensor(mv[:, 3:4], mv[:, 2:3], half[:], ALU.pow).then_inc(rstd_done, 1)
                        pool.wait_ge(rows_loaded, 32)
                        pool.wait_ge(normed, t + 1)
                        nc.gpsimd.tensor_tensor(o[:, b], o[:, b], g_row[:], ALU.mult).then_inc(scaled, 1)
                        nc.gpsimd.tensor_copy(store_ids[:, b], meta_ids[:, bass.ds(t, 1)]).then_inc(store_ids_done, 1)
                        pool.wait_ge(scaled, t + 1)
                        nc.gpsimd.tensor_tensor(o[:, b], o[:, b], b_row[:], ALU.add).then_inc(shifted, 1)
                        pool.wait_ge(store_ids_done, t + 1)
                        pool.wait_ge(shifted, t + 1)
                        pool.sem_inc(passed, 1)
                        nc.gpsimd.indirect_dma_start(out=out, out_offset=bass.IndirectOffsetOnAxis(store_ids[:, b], 0),
                                                     in_=o[:, b], in_offset=None, bounds_check=S - 1,
                                                     oob_is_err=False).then_inc(stored, 16)
                        pool.wait_ge(stored, 16 * t + 16)
                        pool.sem_inc(o_free, 1)

                steps(pool, step)

            @block.scalar
            def _(act):
                def high_part(s, i, group):
                    n = chunk(s, i)
                    act.wait_ge(gu_loaded, group * 16 + 16)
                    act.wait_ge(w_used, n + 1)
                    nc.scalar.copy(w_hi[:, i % RING], gu_raw[:, bass.ds(group % 2, 1), i
                                                             ].rearrange("p o n -> p (o n)")).then_inc(w_high, 1)

                def turned_x(t, b):
                    act.wait_ge(x_turned, t + 1)
                    nc.scalar.copy(xT_hi[:, b], xT[:]).then_inc(x_high, 1)

                def step(s, q, has_gu, has_dn, has_norm):
                    b = q % 2
                    if has_gu:
                        group = group_of(act, s)
                        for i in range(4):
                            high_part(s, i, group)
                    if has_dn:
                        act.wait_ge(h_turned, s)
                        act.wait_ge(down_done, s)
                        nc.scalar.copy(hT_sb[:], hT[:]).then_inc(h_copied, 1)
                    if has_gu:
                        for i in range(4, GUC):
                            high_part(s, i, group)
                        act.wait_ge(w_used, chunk(s, GUC - 1) + RING + 1)
                        if has_dn:
                            act.wait_ge(hid_done, s)
                        nc.scalar.activation(act_g[:], gu[:, 0], ACT.Silu).then_inc(gate_done, 1)
                        if not (isinstance(s, int) and s == T - 1):
                            turned_x(s + 1, 1 - b)

                turned_x(0, 0)
                steps(act, step)

            @block.tensor
            def _(pe):
                def turn_x(t, q):
                    pe.wait_ge(x_loaded[q], 16 * (t // XR + 1))
                    if not (isinstance(t, int) and t == 0):
                        pe.wait_ge(x_split, t)
                    for k in range(KT):
                        last = nc.tensor.transpose(xT[:, k], x[:, q, k * P:(k + 1) * P], ident[:])
                    last.then_inc(x_turned, 1)

                def gate_up(s, b, i):
                    pe.wait_ge(w_split, chunk(s, i) + 2)
                    r = i % RING
                    for c in range(2):
                        cols = slice(c * NT, (c + 1) * NT)
                        nc.tensor.matmul(gu[:, c], xT_hi[:, b, i], w_hi[:, r, cols], start=i == 0, stop=False)
                        nc.tensor.matmul(gu[:, c], xT_lo[:, b, i], w_hi[:, r, cols], start=False, stop=False)
                        last = nc.tensor.matmul(gu[:, c], xT_hi[:, b, i], w_lo[:, r, cols],
                                                start=False, stop=i == GUC - 1)
                    last.then_inc(w_used, 1)

                def step(s, q, has_gu, has_dn, has_norm):
                    b = q % 2
                    if has_gu:
                        pe.wait_ge(x_split, s + 1)
                        if has_dn:
                            pe.wait_ge(hid_done, s)
                        for i in range(2):
                            gate_up(s, b, i)
                    if has_dn:
                        pe.wait_ge(hid_done, s)
                        if has_norm:
                            pe.wait_ge(h_copied, s - 1)
                        for e in range(EG):
                            last = nc.tensor.transpose(hT[:, e], hid[:, e * FF:(e + 1) * FF], ident[:])
                        last.then_inc(h_turned, 1)
                    if has_gu:
                        for i in range(2, GUC):
                            gate_up(s, b, i)
                        if not (isinstance(s, int) and s == T - 1):
                            turn_x(s + 1, (q + 1) % XR)
                    if has_dn:
                        group = group_of(pe, s - 1)
                        pe.wait_ge(dn_loaded, group * 16 + 16)
                        pe.wait_ge(h_copied, s)
                        if has_norm:
                            pe.wait_ge(residual, 2 * s)
                        for e in range(EG):
                            for c in range(2):
                                w = dn_raw[:, bass.ds(group % 2, 1), e, c * NT:(c + 1) * NT]
                                last = nc.tensor.matmul(y[:, c], hT_sb[:, e], w.rearrange("p o n -> p (o n)"),
                                                        start=e == 0, stop=e == EG - 1)
                        last.then_inc(down_done, 1)

                pe.sem_inc(w_used, RING)
                pe.sem_inc(down_done, 1)
                turn_x(0, 0)
                steps(pe, step)

            @block.vector
            def _(dve):
                def low_part(s, i, group):
                    n = chunk(s, i)
                    dve.wait_ge(w_high, n + 1)
                    nc.vector.tensor_tensor(w_lo[:, i % RING], gu_raw[:, bass.ds(group % 2, 1), i
                                                                      ].rearrange("p o n -> p (o n)"),
                                            f32(w_hi[:, i % RING]), ALU.subtract).then_inc(w_split, 1)

                def x_low(t, b):
                    dve.wait_ge(x_high, t + 1)
                    nc.vector.tensor_tensor(xT_lo[:, b], xT[:], f32(xT_hi[:, b]), ALU.subtract).then_inc(x_split, 1)

                def step(s, q, has_gu, has_dn, has_norm):
                    b = q % 2

                    def low_parts(chunks):
                        if has_gu:
                            for i in chunks:
                                low_part(s, i, group)

                    if has_gu:
                        group = group_of(dve, s)
                    low_parts(range(4))
                    if has_norm:
                        t = s - 2
                        dve.wait_ge(down_done, t + 2)
                        dve.wait_ge(o_free, t + 1)
                        for c in range(2):
                            cols = slice(c * NT, (c + 1) * NT)
                            nc.vector.scalar_tensor_tensor(out=o[:, b, cols], in0=x[:, (q + 2) % XR, cols], scalar=ALPHA,
                                                           in1=y[:, c], op0=ALU.mult, op1=ALU.add
                                                           ).then_inc(residual, 1)
                        for c in range(2):
                            dve.wait_ge(residual, 2 * t + c + 3)
                            nc.vector.bn_stats(stats[:, 6 * c:6 * c + 6], o[:, b, c * NT:(c + 1) * NT]
                                               ).then_inc(stat_chain, 1)
                    low_parts(range(4, 5))
                    if has_norm:
                        dve.wait_ge(stat_chain, 4 * t + 2)
                        dve.sem_inc(passed_dve, 1)
                        nc.vector.bn_aggr(mv[:, 0:2], stats[:]).then_inc(stat_chain, 1)
                        dve.wait_ge(stat_chain, 4 * t + 3)
                        nc.vector.tensor_scalar(mv[:, 2:3], mv[:, 1:2], EPS, None, ALU.add).then_inc(stat_chain, 1)
                    low_parts(range(5, 6))
                    if has_norm:
                        dve.wait_ge(rstd_done, t + 1)
                        nc.vector.tensor_scalar(o[:, b], o[:, b], mv[:, 0:1], mv[:, 3:4],
                                                ALU.subtract, ALU.mult).then_inc(normed, 1)
                    low_parts(range(6, GUC))
                    if has_gu:
                        dve.wait_ge(gate_done, s + 1)
                        if has_dn:
                            dve.wait_ge(h_turned, s)
                        for e in range(EG):
                            cols = slice(e * FF, (e + 1) * FF)
                            op = nc.vector.scalar_tensor_tensor(
                                out=hid[:, cols], in0=gu[:, 1, cols],
                                scalar=meta[:, bass.ds(s, 1), 1 + e:2 + e].rearrange("p o w -> p (o w)"),
                                in1=act_g[:, cols], op0=ALU.mult, op1=ALU.mult)
                        op.then_inc(hid_done, 1)
                        if not (isinstance(s, int) and s == T - 1):
                            x_low(s + 1, 1 - b)

                dve.sem_inc(w_split, 1)
                dve.sem_inc(residual, 2)
                x_low(0, 0)
                steps(dve, step)


def hybrid_decoder_layer(nc, x, ln_in_g, ln_in_b, w_in, b_gate, conv_w, sg_w, sg_b, sg_ln_g, sg_ln_b,
                         w_br, w_o, ln_mix_g, ln_mix_b, w_router, router_bias, gu_w, dn_w,
                         ln_ffn_g, ln_ffn_b, out):
    scratch = lambda name, shape: nc.dram_tensor(name, shape, F32).ap()
    h_dram = scratch("h_scratch", [S, D])
    projT = scratch("projT_scratch", [COLS, P, S])
    v_nat = scratch("v_scratch", [S, W])
    yT = scratch("yT_scratch", [P, 3 * W // P, S])
    mergedT = scratch("mergedT_scratch", [KT, P, S])
    h2_dram = scratch("h2_scratch", [S + P, D])
    order = scratch("order_scratch", [E_TILES * P, META])
    with ExitStack() as ctx:
        sem = lambda name: ctx.enter_context(nc.semaphore(name))
        ident = ctx.enter_context(nc.sbuf_tensor("ident", [P, P], F32))
        logits = ctx.enter_context(nc.sbuf_tensor("logits", [P, TILES, E], F32))
        with ExitStack() as phase:
            hT_hi = phase.enter_context(nc.sbuf_tensor("hT_hi", [P, KT, S], F32R))
            hT_lo = phase.enter_context(nc.sbuf_tensor("hT_lo", [P, KT, S], F32R))
            input_norm(nc, sem, x, ln_in_g, ln_in_b, h_dram, hT_hi, hT_lo, ident)
            project(nc, sem, w_in, b_gate, projT, hT_hi, hT_lo)
        local_mixers(nc, sem, projT, conv_w, sg_w, sg_b, sg_ln_g, sg_ln_b, v_nat, yT, ident)
        attention(nc, sem, projT, v_nat, yT)
        merge_branches(nc, sem, projT, yT, w_br, mergedT)
        mix_out(nc, sem, mergedT, w_o, h_dram, ln_mix_g, ln_mix_b, w_router, h2_dram, logits, ident)
        meta = ctx.enter_context(nc.sbuf_tensor("meta", [P, E_TILES, META], F32))
        table = ctx.enter_context(nc.sbuf_tensor("table", [1, E_TILES + EG], U32))
        gu_raw = ctx.enter_context(nc.sbuf_tensor("gu_raw", [P, 2, GUC, 2 * EG * FF], F32))
        dn_raw = ctx.enter_context(nc.sbuf_tensor("dn_raw", [P, 2, DNC, D], F32))
        gu_loaded, dn_loaded = sem("gu_loaded"), sem("dn_loaded")
        dispatch(nc, sem, logits, router_bias, order, meta, table, gu_w, dn_w, gu_raw, dn_raw, gu_loaded, dn_loaded)
        experts(nc, sem, h2_dram, meta, table, gu_w, dn_w, gu_raw, dn_raw, gu_loaded, dn_loaded,
                ln_ffn_g, ln_ffn_b, out, ident)


def kernel(**inputs):
    import numpy as np
    import concourse.bacc as bacc
    from concourse.bass_utils import run_bass_kernel_spmd

    w = {name: np.asarray(a) for name, a in inputs.items()}
    by_rows = lambda a: a.reshape(-1, P, a.shape[-1]).transpose(1, 0, 2)
    ffn_in = lambda a: a.reshape(EG, EG, KT, P, FF).transpose(0, 3, 2, 1, 4).reshape(EG, P, KT, EG * FF)
    arrays = {
        "x": w["x"].reshape(S, D),
        "ln_in_g": w["ln_in_g"],
        "ln_in_b": w["ln_in_b"],
        "w_in": w["w_in"].reshape(KT, P, COLS, P).transpose(2, 1, 0, 3).reshape(COLS, P, D),
        "b_gate": w["b_gate"].reshape(COLS - GATES, P).T,
        "conv_w": w["conv_w"].reshape(3, W // P, P).transpose(2, 1, 0),
        "sg_w": w["sg_w"][0].transpose(2, 0, 1),
        "sg_b": w["sg_b"][0],
        "sg_ln_g": w["sg_ln_g"][0],
        "sg_ln_b": w["sg_ln_b"][0],
        "w_br": by_rows(w["w_br"].reshape(3 * W, D)),
        "w_o": by_rows(w["w_o"][0]),
        "ln_mix_g": w["ln_mix_g"][0],
        "ln_mix_b": w["ln_mix_b"][0],
        "w_router": by_rows(w["w_router"]),
        "router_bias": w["router_bias"],
        "gu_w": np.concatenate([ffn_in(w["w_gate"][0]), ffn_in(w["w_up"][0])], axis=-1),
        "dn_w": w["w_down"].reshape(EG, EG, FF, D).transpose(0, 2, 1, 3),
        "ln_ffn_g": w["ln_ffn_g"][0],
        "ln_ffn_b": w["ln_ffn_b"][0],
    }
    arrays = {f"{name}_in": np.ascontiguousarray(a) for name, a in arrays.items()}
    nc = bacc.Bacc("TRN2", target_bir_lowering=False, num_devices=1)
    args = [nc.dram_tensor(name, a.shape, mybir.dt.from_np(a.dtype), kind="ExternalInput").ap()
            for name, a in arrays.items()]
    out = nc.dram_tensor("layer_out", (1, S, D), F32, kind="ExternalOutput").ap()
    hybrid_decoder_layer(nc, *args, out.rearrange("o s d -> (o s) d"))
    r = run_bass_kernel_spmd(nc, [arrays], core_ids=[0])
    return r.results[0]["layer_out"]
```

```python
from contextlib import ExitStack

import concourse.bass as bass
from concourse import mybir

ALU = mybir.AluOpType
ACT = mybir.ActivationFunctionType
AX_X = mybir.AxisListType.X
F32 = mybir.dt.float32
F32R = mybir.dt.float32r
U32 = mybir.dt.uint32

P = 128
D = 1024
KT = D // P
S = 2048
TILES = S // P
NT = 512
TT = S // NT
H, DH = 4, 64
G_C, CHUNK = 4, 128
W = 256
EPS = 1e-5
ALPHA = 2.0 ** 0.25

HA, BG, CG, Q, K, V, U_C, V_C, GATES = 0, 2, 4, 6, 8, 10, 12, 14, 16
COLS = 40


def f32(ap):
    return ap.bitcast(F32)


def input_norm(nc, sem, x, ln_g, ln_b, h_dram, hT_hi, hT_lo, ident):
    with ExitStack() as ctx:
        sb = lambda n, s, dt=F32: ctx.enter_context(nc.sbuf_tensor(n, s, dt))
        ps = lambda n, s, dt=F32: ctx.enter_context(nc.psum_tensor(n, s, dt))
        xt = sb("in_x", [P, 2, D])
        xn = sb("in_xn", [P, 2, D])
        hn = sb("in_h", [P, 2, D])
        g_row = sb("in_g", [P, D])
        b_row = sb("in_b", [P, D])
        stats = sb("in_stats", [P, 2, 12])
        mv = sb("in_mv", [P, 2, 4])
        half = sb("in_half", [P, 1])
        tp = ps("in_tp", [P, 2, KT, P])
        rows_loaded = sem("in_rows_loaded")
        x_loaded = [sem(f"in_x_loaded{b}") for b in range(2)]
        aggr_done = sem("in_aggr_done")
        stat_chain = sem("in_stat_chain")
        rstd_done = sem("in_rstd_done")
        normed = sem("in_normed")
        scaled = sem("in_scaled")
        h_done = sem("in_h_done")
        consts = sem("in_consts")
        h_stored = [sem(f"in_h_stored{b}") for b in range(2)]
        transposed = sem("in_transposed")
        hi_done = sem("in_hi_done")
        lo_done = sem("in_lo_done")
        x_t = x.rearrange("(t p) d -> t p d", p=P)
        h_t = h_dram.rearrange("(t p) d -> t p d", p=P)

        with nc.Block() as block:

            @block.sync
            def _(sp):
                sp.dma_start(xt[:, 0], x_t[0]).then_inc(x_loaded[0], 16)
                sp.dma_start(xt[:, 1], x_t[1]).then_inc(x_loaded[1], 16)
                sp.dma_start(g_row[:], ln_g.partition_broadcast(P)).then_inc(rows_loaded, 16)
                sp.dma_start(b_row[:], ln_b.partition_broadcast(P)).then_inc(rows_loaded, 16)
                for t in range(TILES):
                    b = t % 2
                    if t + 2 < TILES:
                        sp.wait_ge(normed, t + 1)
                        sp.dma_start(xt[:, b], x_t[t + 2]).then_inc(x_loaded[b], 16)
                    sp.wait_ge(h_done, t + 1)
                    sp.dma_start(h_t[t], hn[:, b]).then_inc(h_stored[b], 16)
                for b in range(2):
                    sp.wait_ge(h_stored[b], 16 * (TILES // 2))

            @block.gpsimd
            def _(pool):
                nc.gpsimd.memset(ident[:], 0.0).then_inc(consts, 1)
                pool.wait_ge(consts, 1)
                nc.gpsimd.affine_select(out=ident[:], in_=ident[:], compare_op=ALU.not_equal, fill=1.0, base=0,
                                        pattern=[[-1, P]], channel_multiplier=1).then_inc(consts, 1)
                nc.gpsimd.memset(half[:], -0.5).then_inc(consts, 1)
                pool.wait_ge(consts, 3)
                pool.wait_ge(rows_loaded, 32)
                for t in range(TILES):
                    b = t % 2
                    pool.wait_ge(aggr_done, t + 1)
                    nc.gpsimd.tensor_tensor(mv[:, b, 3:4], mv[:, b, 2:3], half[:], ALU.pow).then_inc(rstd_done, 1)
                    pool.wait_ge(normed, t + 1)
                    if t >= 2:
                        pool.wait_ge(h_stored[b], 16 * (t // 2))
                        pool.wait_ge(transposed, t - 1)
                    nc.gpsimd.tensor_tensor(hn[:, b], xn[:, b], g_row[:], ALU.mult).then_inc(scaled, 1)
                    pool.wait_ge(scaled, t + 1)
                    nc.gpsimd.tensor_tensor(hn[:, b], hn[:, b], b_row[:], ALU.add).then_inc(h_done, 1)

            @block.vector
            def _(dve):
                def statistics(t):
                    b = t % 2
                    dve.wait_ge(x_loaded[b], 16 * (t // 2 + 1))
                    for c in range(2):
                        nc.vector.bn_stats(stats[:, b, 6 * c:6 * c + 6], xt[:, b, 512 * c:512 * c + 512]
                                           ).then_inc(stat_chain, 1)
                    dve.wait_ge(stat_chain, 3 * t + 2)
                    nc.vector.bn_aggr(mv[:, b, 0:2], stats[:, b]).then_inc(stat_chain, 1)
                    dve.wait_ge(stat_chain, 3 * t + 3)
                    nc.vector.tensor_scalar(mv[:, b, 2:3], mv[:, b, 1:2], EPS, None, ALU.add).then_inc(aggr_done, 1)

                def low_part(t):
                    dve.wait_ge(hi_done, t + 1)
                    cols = slice(t * P, (t + 1) * P)
                    nc.vector.tensor_tensor(hT_lo[:, :, cols], tp[:, t % 2], f32(hT_hi[:, :, cols]),
                                            ALU.subtract).then_inc(lo_done, 1)

                statistics(0)
                for t in range(TILES):
                    b = t % 2
                    if t + 1 < TILES:
                        statistics(t + 1)
                    dve.wait_ge(rstd_done, t + 1)
                    if t >= 2:
                        dve.wait_ge(scaled, t - 1)
                    nc.vector.tensor_scalar(xn[:, b], xt[:, b], mv[:, b, 0:1], mv[:, b, 3:4],
                                            ALU.subtract, ALU.mult).then_inc(normed, 1)
                    if t >= 2:
                        low_part(t - 2)
                low_part(TILES - 2)
                low_part(TILES - 1)

            @block.tensor
            def _(pe):
                for t in range(TILES):
                    pe.wait_ge(h_done, t + 1)
                    if t >= 2:
                        pe.wait_ge(lo_done, t - 1)
                    for k in range(KT):
                        last = nc.tensor.transpose(tp[:, t % 2, k], hn[:, t % 2, k * P:(k + 1) * P], ident[:])
                    last.then_inc(transposed, 1)

            @block.scalar
            def _(act):
                for t in range(TILES):
                    act.wait_ge(transposed, t + 1)
                    nc.scalar.copy(hT_hi[:, :, t * P:(t + 1) * P], tp[:, t % 2]).then_inc(hi_done, 1)


def project(nc, sem, w_tiles, projT, hT_hi, hT_lo):
    with ExitStack() as ctx:
        sb = lambda n, s, dt=F32: ctx.enter_context(nc.sbuf_tensor(n, s, dt))
        w_raw = sb("pj_w_raw", [P, 2, KT * P])
        w_hi = sb("pj_w_hi", [P, 2, KT * P], F32R)
        w_lo = sb("pj_w_lo", [P, 2, KT * P], F32R)
        ot = sb("pj_out", [P, 2, S])
        acc = ctx.enter_context(nc.psum_tensor("pj_acc", [P, 2 * TT, NT], F32))
        w_loaded = [sem(f"pj_w_loaded{b}") for b in range(2)]
        hi_done = sem("pj_hi_done")
        lo_done = sem("pj_lo_done")
        product_done = sem("pj_product_done")
        evacuated = sem("pj_evacuated")
        stored = [sem(f"pj_stored{b}") for b in range(2)]

        with nc.Block() as block:

            @block.sync
            def _(sp):
                sp.dma_start(w_raw[:, 0], w_tiles[0]).then_inc(w_loaded[0], 16)
                sp.dma_start(w_raw[:, 1], w_tiles[1]).then_inc(w_loaded[1], 16)

                def tile(m, b, load):
                    if load:
                        sp.wait_ge(lo_done, m + 1)
                        sp.dma_start(w_raw[:, b], w_tiles[bass.ds(m + 2, 1)].rearrange("o p n -> p (o n)")
                                     ).then_inc(w_loaded[b], 16)
                    sp.wait_ge(evacuated, TT * m + TT)
                    sp.dma_start(projT[bass.ds(m, 1)].rearrange("o p n -> p (o n)"), ot[:, b]
                                 ).then_inc(stored[b], 16)

                with sp.Fori(0, GATES // 2 - 1) as j:
                    tile(2 * j, 0, True)
                    tile(2 * j + 1, 1, True)
                tile(GATES - 2, 0, False)
                tile(GATES - 1, 1, False)
                for b in range(2):
                    sp.wait_ge(stored[b], 16 * (GATES // 2))

            @block.scalar
            def _(act):
                def high_part(n, b, m_half):
                    act.wait_ge(w_loaded[b], 16 * m_half)
                    nc.scalar.copy(w_hi[:, b], w_raw[:, b]).then_inc(hi_done, 1)

                def tile(m, b, half, first, last):
                    if not last:
                        high_part(m + 1, 1 - b, half + 1 + b)
                    if not first:
                        act.wait_ge(stored[b], 16 * half)
                    for t in range(TT):
                        act.wait_ge(product_done, TT * m + t + 1)
                        nc.scalar.copy(ot[:, b, t * NT:(t + 1) * NT], acc[:, b * TT + t]).then_inc(evacuated, 1)

                high_part(0, 0, 1)
                tile(0, 0, 0, True, False)
                tile(1, 1, 0, True, False)
                with act.Fori(1, GATES // 2 - 1) as j:
                    tile(2 * j, 0, j, False, False)
                    tile(2 * j + 1, 1, j, False, False)
                tile(GATES - 2, 0, GATES // 2 - 1, False, False)
                tile(GATES - 1, 1, GATES // 2 - 1, False, True)

            @block.vector
            def _(dve):
                with dve.Fori(0, GATES, 2) as i:
                    for b in range(2):
                        dve.wait_ge(hi_done, i + b + 1)
                        nc.vector.tensor_tensor(w_lo[:, b], w_raw[:, b], f32(w_hi[:, b]),
                                                ALU.subtract).then_inc(lo_done, 1)

            @block.tensor
            def _(pe):
                with pe.Fori(0, GATES, 2) as i:
                    for b in range(2):
                        pe.wait_ge(lo_done, i + b + 1)
                        for t in range(TT):
                            cols = slice(t * NT, (t + 1) * NT)
                            for k in range(KT):
                                w = slice(k * P, (k + 1) * P)
                                out = acc[:, b * TT + t]
                                nc.tensor.matmul(out, w_hi[:, b, w], hT_hi[:, k, cols], start=k == 0, stop=False)
                                nc.tensor.matmul(out, w_hi[:, b, w], hT_lo[:, k, cols], start=False, stop=False)
                                last = nc.tensor.matmul(out, w_lo[:, b, w], hT_hi[:, k, cols],
                                                        start=False, stop=k == KT - 1)
                            last.then_inc(product_done, 1)


def gates_and_local_mixers(nc, sem, w_tiles, b_gate, projT, hT_hi, hT_lo, conv_w, sg_w, sg_b, sg_g, sg_bb,
                           v_nat, yT, ident):
    N_GATES = COLS - GATES
    PER = N_GATES // TT
    CH = NT // CHUNK
    HALO = 2
    with ExitStack() as ctx:
        sb = lambda n, s, dt=F32: ctx.enter_context(nc.sbuf_tensor(n, s, dt))
        ps = lambda n, s, dt=F32: ctx.enter_context(nc.psum_tensor(n, s, dt))
        w_raw = sb("gm_w_raw", [P, 2, KT * P])
        w_hi = sb("gm_w_hi", [P, 2, KT * P], F32R)
        w_lo = sb("gm_w_lo", [P, 2, KT * P], F32R)
        ot = sb("gm_out", [P, TT, NT])
        bg = sb("gm_b_gate", [P, N_GATES])
        conv_u = sb("gm_conv_u", [P, 2, HALO + NT])
        conv_c = sb("gm_conv_c", [P, 2, NT])
        conv_b = sb("gm_conv_b", [P, 2, NT])
        vT = sb("gm_vT", [P, 2, NT])
        uT = sb("gm_uT", [P, 2, NT])
        vcT = sb("gm_vcT", [P, 2, NT])
        cw = sb("gm_cw", [P, 2, 3])
        wsT = sb("gm_wsT", [P, G_C, CHUNK])
        bias = sb("gm_bias", [P, 2, CHUNK])
        g_row = sb("gm_g", [P, W])
        b_row = sb("gm_b", [P, W])
        half = sb("gm_half", [P, 1])
        stats = sb("gm_stats", [P, 6])
        mv = sb("gm_mv", [P, 4])
        vn = sb("gm_vn", [P, W])
        vs = sb("gm_v", [P, W])
        fb = sb("gm_fb", [P, 2, CHUNK])
        acc = ps("gm_acc", [P, TT, NT])
        vc_ps = ps("gm_vc_ps", [P, 4, P])
        v_ps = ps("gm_v_ps", [P, 4, P])
        fT = ps("gm_fT", [P, 4, P])
        w_loaded = [sem(f"gm_w_loaded{b}") for b in range(2)]
        small_loaded = sem("gm_small_loaded")
        passed = sem("passed")
        hi_done = sem("gm_hi_done")
        lo_done = sem("gm_lo_done")
        product_done = sem("gm_product_done")
        evacuated = sem("gm_evacuated")
        stored = [sem(f"gm_stored{t}") for t in range(TT)]
        v_loaded = sem("gm_v_loaded")
        u_loaded = sem("gm_u_loaded")
        conv_loaded = sem("gm_conv_loaded")
        consts = sem("gm_consts")
        gelu_done = sem("gm_gelu_done")
        turned = sem("gm_turned")
        stat_chain = sem("gm_stat_chain")
        rstd_done = sem("gm_rstd_done")
        normed = sem("gm_normed")
        scaled = sem("gm_scaled")
        vn_done = sem("gm_vn_done")
        v_copied = sem("gm_v_copied")
        v_stored = sem("gm_v_stored")
        mixed = sem("gm_mixed")
        biased = sem("gm_biased")
        yc_done = sem("gm_yc_done")
        conv_chain = sem("gm_conv_chain")
        y_stored = sem("gm_y_stored")
        CONV_STEPS = 9
        rows = projT.rearrange("m p s -> p m s")
        v_t = v_nat.rearrange("(n p) c -> p n c", p=P)

        with nc.Block() as block:

            @block.sync
            def _(sp):
                def load_w(g, b):
                    sp.dma_start(w_raw[:, b], w_tiles[bass.ds(GATES + g % N_GATES, 1)].rearrange("o p n -> p (o n)")
                                 ).then_inc(w_loaded[b], 16)

                load_w(0, 0)
                load_w(1, 1)
                sp.dma_start(bg[:], b_gate).then_inc(small_loaded, 16)
                sp.dma_start(wsT[:], sg_w).then_inc(small_loaded, 16)
                for g in range(G_C):
                    sp.dma_start(bias[64 * (g % 2):64 * (g % 2) + 64, g // 2], sg_b[g].partition_broadcast(64)
                                 ).then_inc(small_loaded, 16)
                sp.dma_start(g_row[:], sg_g.partition_broadcast(P)).then_inc(small_loaded, 16)
                sp.dma_start(b_row[:], sg_bb.partition_broadcast(P)).then_inc(small_loaded, 16)
                sp.dma_start(cw[:], conv_w).then_inc(small_loaded, 16)
                for t in range(TT):
                    sp.sem_inc(stored[t], 16)
                sp.sem_inc(v_stored, 16)
                sp.sem_inc(y_stored, 16)
                with sp.Fori(0, TT) as q:
                    block_cols = bass.ds(q * NT, NT)
                    sp.wait_ge(turned, CH * q + 1)
                    sp.wait_ge(y_stored, 32 * q + 16)
                    for x, m, s in ((vcT[:], V_C, v_loaded), (vT[:], V, v_loaded),
                                    (conv_u[:, :, HALO:], HA, conv_loaded), (conv_c[:], CG, conv_loaded),
                                    (conv_b[:], BG, conv_loaded), (uT[:], U_C, u_loaded)):
                        sp.dma_start(x, rows[:, m:m + 2, block_cols]).then_inc(s, 16)
                    for i in range(PER):
                        g, b = PER * q + i, i % 2
                        sp.wait_ge(lo_done, g + 1)
                        load_w(g + 2, b)
                        for t in range(TT):
                            sp.wait_ge(evacuated, TT * g + t + 1 + TT)
                            sp.dma_start(rows[:, bass.ds(GATES + g, 1), t * NT:(t + 1) * NT
                                              ].rearrange("p o s -> p (o s)"), ot[:, t]).then_inc(stored[t], 16)
                        if 1 <= i <= CH:
                            chunk = CH * q + i - 1
                            sp.wait_ge(v_copied, chunk + 2)
                            sp.dma_start(v_t[:, bass.ds(chunk, 1)].rearrange("p o c -> p (o c)"), vs[:]
                                         ).then_inc(v_stored, 16)
                        if i == 1:
                            sp.wait_ge(conv_chain, CONV_STEPS * (q + 1))
                            sp.dma_start(yT[:, 0:2, block_cols], conv_c[:]).then_inc(y_stored, 16)
                        if i == PER - 1:
                            sp.wait_ge(yc_done, CH * (q + 1))
                            sp.dma_start(yT[:, 4:6, block_cols], uT[:]).then_inc(y_stored, 16)
                for b in range(2):
                    sp.wait_ge(w_loaded[b], 16 * (N_GATES // 2 + 1))
                for t in range(TT):
                    sp.wait_ge(stored[t], 16 * (N_GATES + 1))
                sp.wait_ge(v_stored, 16 * (CH * TT + 1))
                sp.wait_ge(y_stored, 16 * (2 * TT + 1))

            @block.gpsimd
            def _(pool):
                nc.gpsimd.memset(half[:], -0.5).then_inc(consts, 1)
                nc.gpsimd.memset(conv_u[:, :, 0:HALO], 0.0).then_inc(consts, 1)
                pool.wait_ge(small_loaded, 9 * 16)
                nc.gpsimd.affine_select(out=wsT[:], in_=wsT[:], compare_op=ALU.is_ge, fill=0.0, base=0,
                                        pattern=[[0, G_C], [1, CHUNK]], channel_multiplier=-1
                                        ).then_inc(consts, 1)
                pool.wait_ge(consts, 2)
                with pool.Fori(0, TT) as q:
                    for k in range(CH):
                        chunk = CH * q + k
                        pool.wait_ge(stat_chain, 3 * chunk + 3)
                        nc.gpsimd.tensor_tensor(mv[:, 3:4], mv[:, 2:3], half[:], ALU.pow).then_inc(rstd_done, 1)
                        pool.wait_ge(normed, chunk + 2)
                        nc.gpsimd.tensor_tensor(vn[:], vn[:], g_row[:], ALU.mult).then_inc(scaled, 1)
                        pool.wait_ge(scaled, chunk + 1)
                        nc.gpsimd.tensor_tensor(vn[:], vn[:], b_row[:], ALU.add).then_inc(vn_done, 1)

            @block.scalar
            def _(act):
                def high_part(b, count):
                    act.wait_ge(w_loaded[b], 16 * count)
                    nc.scalar.copy(w_hi[:, b], w_raw[:, b]).then_inc(hi_done, 1)

                act.sem_inc(evacuated, TT)
                act.sem_inc(v_copied, 1)
                high_part(0, 1)
                act.wait_ge(small_loaded, 9 * 16)
                with act.Fori(0, TT) as q:
                    for i in range(PER):
                        g = PER * q + i
                        high_part((i + 1) % 2, PER // 2 * q + (i + 1) // 2 + 1)
                        for t in range(TT):
                            act.wait_ge(stored[t], 16 * g + 16)
                            act.wait_ge(product_done, TT * g + t + 1)
                            act.sem_inc(passed, 1)
                            nc.scalar.activation(ot[:, t], acc[:, t], ACT.Sigmoid, bias=bg[:, bass.ds(g, 1)]
                                                 ).then_inc(evacuated, 1)
                        if i == 0:
                            act.wait_ge(v_loaded, 32 * q + 32)
                            nc.scalar.activation(vcT[:], vcT[:], ACT.Gelu_apprx_tanh).then_inc(gelu_done, 1)
                            act.wait_ge(u_loaded, 16 * q + 16)
                            nc.scalar.activation(uT[:], uT[:], ACT.Gelu_apprx_tanh).then_inc(gelu_done, 1)
                        if 1 <= i <= CH:
                            chunk = CH * q + i - 1
                            act.wait_ge(v_stored, 16 * chunk + 16)
                            act.wait_ge(turned, chunk + 2)
                            nc.scalar.copy(vs[:], v_ps[:, 0:2].rearrange("p c t -> p (c t)")).then_inc(v_copied, 1)

            @block.tensor
            def _(pe):
                pe.sem_inc(turned, 1)
                pe.sem_inc(mixed, 1)
                with pe.Fori(0, TT) as q:
                    for i in range(PER):
                        g, b = PER * q + i, i % 2
                        if i >= 2:
                            chunk = CH * q + i - 2
                            pe.wait_ge(biased, chunk + 1)
                            pe.wait_ge(consts, 3)
                            pe.wait_ge(vn_done, chunk + 1)
                            for gr in range(G_C):
                                r = 64 * (gr % 2)
                                last = nc.tensor.matmul(fT[r:r + 64, gr // 2], vn[:, gr * 64:(gr + 1) * 64],
                                                        wsT[:, gr], start=True, stop=True)
                            last.then_inc(mixed, 1)
                        if 1 <= i <= CH:
                            k = i - 1
                            chunk = CH * q + k
                            pe.wait_ge(gelu_done, 2 * q + 1)
                            pe.wait_ge(v_copied, chunk + 1)
                            pe.wait_ge(normed, chunk + 1)
                            cols = slice(k * CHUNK, (k + 1) * CHUNK)
                            for c in range(2):
                                nc.tensor.transpose(vc_ps[:, c], vcT[:, c, cols], ident[:])
                                last = nc.tensor.transpose(v_ps[:, c], vT[:, c, cols], ident[:])
                            last.then_inc(turned, 1)
                        pe.wait_ge(lo_done, g + 1)
                        for t in range(TT):
                            pe.wait_ge(evacuated, TT * g + t + 1)
                            for k in range(KT):
                                w, x = slice(k * P, (k + 1) * P), slice(t * NT, (t + 1) * NT)
                                out = acc[:, t]
                                nc.tensor.matmul(out, w_hi[:, b, w], hT_hi[:, k, x], start=k == 0, stop=False)
                                nc.tensor.matmul(out, w_hi[:, b, w], hT_lo[:, k, x], start=False, stop=False)
                                last = nc.tensor.matmul(out, w_lo[:, b, w], hT_hi[:, k, x],
                                                        start=False, stop=k == KT - 1)
                            last.then_inc(product_done, 1)

            @block.vector
            def _(dve):
                def low_part(b, g):
                    dve.wait_ge(hi_done, g + 1)
                    nc.vector.tensor_tensor(w_lo[:, b], w_raw[:, b], f32(w_hi[:, b]), ALU.subtract
                                            ).then_inc(lo_done, 1)

                def convolve(q):
                    step = [0]

                    def chained(op):
                        step[0] += 1
                        op.then_inc(conv_chain, 1)
                        dve.wait_ge(conv_chain, CONV_STEPS * q + step[0])

                    u = conv_u[:, :, HALO:]
                    dve.wait_ge(conv_loaded, 48 * q + 48)
                    chained(nc.vector.tensor_tensor(u, conv_c[:], u, ALU.mult))
                    for tap in range(3):
                        for c in range(2):
                            y, x = conv_c[:, c], conv_u[:, c, tap:tap + NT]
                            if tap == 0:
                                op = nc.vector.tensor_scalar(y, x, cw[:, c, 0:1], None, ALU.mult)
                            else:
                                op = nc.vector.scalar_tensor_tensor(out=y, in0=x, scalar=cw[:, c, tap:tap + 1],
                                                                    in1=y, op0=ALU.mult, op1=ALU.add)
                            chained(op)
                    chained(nc.vector.tensor_tensor(conv_c[:], conv_c[:], conv_b[:], ALU.mult))
                    chained(nc.vector.tensor_copy(conv_u[:, :, 0:HALO], conv_u[:, :, NT:NT + HALO]))

                def gate(q, k):
                    chunk = CH * q + k
                    dve.wait_ge(mixed, chunk + 2)
                    nc.vector.tensor_tensor(fb[:], fT[:, 0:2], bias[:], ALU.add).then_inc(biased, 1)
                    dve.wait_ge(biased, chunk + 2)
                    dve.wait_ge(gelu_done, 2 * q + 2)
                    u = uT[:, :, k * CHUNK:(k + 1) * CHUNK]
                    nc.vector.tensor_tensor(u, u, fb[:], ALU.mult).then_inc(yc_done, 1)

                def normalise(q, k):
                    chunk = CH * q + k
                    vc = vc_ps[:, 0:2].rearrange("p c t -> p (c t)")
                    dve.wait_ge(turned, chunk + 2)
                    nc.vector.bn_stats(stats[:], vc).then_inc(stat_chain, 1)
                    dve.wait_ge(stat_chain, 3 * chunk + 1)
                    dve.sem_inc(passed, 1)
                    nc.vector.bn_aggr(mv[:, 0:2], stats[:]).then_inc(stat_chain, 1)
                    dve.wait_ge(stat_chain, 3 * chunk + 2)
                    nc.vector.tensor_scalar(mv[:, 2:3], mv[:, 1:2], EPS, None, ALU.add).then_inc(stat_chain, 1)
                    dve.wait_ge(rstd_done, chunk + 1)
                    dve.wait_ge(mixed, chunk + 1)
                    nc.vector.tensor_scalar(vn[:], vc, mv[:, 0:1], mv[:, 3:4], ALU.subtract, ALU.mult
                                            ).then_inc(normed, 1)

                dve.sem_inc(normed, 1)
                dve.sem_inc(biased, 1)
                low_part(0, 0)
                dve.wait_ge(small_loaded, 9 * 16)
                dve.wait_ge(consts, 2)
                with dve.Fori(0, TT) as q:
                    for i in range(PER):
                        low_part((i + 1) % 2, PER * q + i + 1)
                        if i == 0:
                            convolve(q)
                        if i >= 2:
                            gate(q, i - 2)
                        if 1 <= i <= CH:
                            normalise(q, i - 1)



def attention(nc, sem, projT, v_nat, yT):
    SCALE = DH ** -0.5
    R = 8
    RZ = 4
    HEADS = 2
    SP_CAP = 44.0

    LN, SP, HI, LO, OWN, SUM, REST, EXP, MASK, AV, OUT = 1, 2, 3, 3, 4, 5, 6, 6, 7, 8, 9

    chain = [[], []]
    for c, tiles in enumerate(((3, 0), (2, 1))):
        for qt in tiles:
            blocks = list(range(4 * qt + 3, -1, -1))
            for kb in blocks:
                d = kb - 4 * qt
                chain[c].append((c, qt, kb, d, min(P * max(d, 0), NT // 2), kb == blocks[0], kb == 0))
    head_items = [x for pair in zip(*chain) for x in pair]
    PER_HEAD = len(head_items)
    items = [(s,) + x for s in range(HEADS) for x in head_items]
    N = len(items)

    with ExitStack() as ctx:
        sb = lambda n, s, dt=F32: ctx.enter_context(nc.sbuf_tensor(n, s, dt))
        ps = lambda n, s, dt=F32: ctx.enter_context(nc.psum_tensor(n, s, dt))
        q_raw = sb("at_q_raw", [P, S])
        k_raw = sb("at_k_raw", [P, S])
        q_hi = sb("at_q_hi", [P, HEADS, S], F32R)
        q_lo = sb("at_q_lo", [P, HEADS, S], F32R)
        k_st = sb("at_k", [P, HEADS, S], F32R)
        v_sb = sb("at_v", [P, HEADS, TILES, DH])
        neg_own = sb("at_neg_own", [P, P], F32R)
        neg_rest = sb("at_neg_rest", [P, P], F32R)
        z_sb = sb("at_z", [P, R, NT])
        e_sb = sb("at_e", [P, R, NT])
        sp_sb = sb("at_sp", [P, R, NT])
        sp_hi = sb("at_sp_hi", [P, R, NT], F32R)
        sp_lo = sb("at_sp_lo", [P, R, NT], F32R)
        t_sb = sb("at_t", [P, R, NT])
        a_sb = sb("at_a", [P, R, NT])
        y_sb = sb("at_y", [DH, 2, NT])
        z_ps = ps("at_z_ps", [P, RZ, NT])
        sum_ps = ps("at_sum_ps", [P, 2, NT])
        y_ps = ps("at_y_ps", [P, 2, NT])

        consts = sem("at_consts")
        passed = sem("passed")
        q_loaded = sem("at_q_loaded")
        k_loaded = sem("at_k_loaded")
        v_loaded = sem("at_v_loaded")
        prep = sem("at_prep")
        z_done = sem("at_z_done")
        z_copied = sem("at_z_copied")
        e_done = sem("at_e_done")
        l_done = sem("at_l_done")
        sp_done = sem("at_sp_done")
        masked = sem("at_masked")
        hi_done = sem("at_hi_done")
        lo_done = sem("at_lo_done")
        own_done = sem("at_own_done")
        t_done = sem("at_t_done")
        rest_done = sem("at_rest_done")
        a_done = sem("at_a_done")
        a_masked = sem("at_a_masked")
        av_done = sem("at_av_done")
        y_done = sem("at_y_done")
        y_stored = [sem(f"at_y_stored{c}") for c in range(2)]

        proj_rows = projT.rearrange("m p s -> (m p) s")
        v_heads = v_nat.rearrange("(n p) (h d) -> p n h d", p=P, d=DH)
        y_heads = yT[:, 2:4].rearrange("(r p) m s -> m r p s", p=DH)
        diag_before = [sum(1 for x in items[:n] if x[4] >= 0) for n in range(N + 1)]
        last_before = [sum(1 for x in items[:n] if x[7]) for n in range(N + 1)]
        DIAG, LASTS = diag_before[N], last_before[N]
        lasts = [n for n in range(N) if items[n][7]]
        chain_tile = lambda n: sum(1 for m in lasts if m < n and items[m][1] == items[n][1])

        def tile_before(n):
            own = [x for x, m in enumerate(lasts) if items[m][1] == items[n][1]]
            k = chain_tile(n)
            return own[k - 1] if k else own[-1] - LASTS

        PARTS = S // NT
        PREP = 4 * PARTS

        ringed = dict(act=(z_copied, e_done, l_done, a_done, y_done), dve=(sp_done, hi_done, t_done), pe=(z_done, own_done, av_done))
        done = lambda n: R + n + 1
        freed = lambda n: n + 1

        with nc.Block() as block:

            @block.sync
            def _(sp):
                def load(h, slot, first):
                    for half in range(2):
                        r = slice(half * DH, half * DH + DH)
                        sp.dma_start(q_raw[r], proj_rows[bass.ds(Q * P + h * DH, DH)]).then_inc(q_loaded, 16)
                        sp.dma_start(k_raw[r], proj_rows[bass.ds(K * P + h * DH, DH)]).then_inc(k_loaded, 16)
                    sp.dma_start(v_sb[:, slot], v_heads[:, :, bass.ds(h, 1)].rearrange("p n o d -> p n (o d)")
                                 ).then_inc(v_loaded, 16)

                def store(n, count, pair):
                    slot, c, qt = items[n][0:3]
                    sp.wait_ge(y_done, count)
                    sp.dma_start(y_heads[bass.ds(pair, 1), slot, :, qt * NT:(qt + 1) * NT
                                         ].rearrange("o p s -> p (o s)"), y_sb[:, c]).then_inc(y_stored[c], 16)

                for c in range(2):
                    sp.sem_inc(y_stored[c], 16)
                load(0, 0, True)
                with sp.Fori(0, H // HEADS) as j:
                    sp.wait_ge(prep, PREP * (HEADS * j + 1))
                    load(HEADS * j + 1, 1, False)
                    for x, n in enumerate(lasts):
                        if x == LASTS // 2:
                            sp.wait_ge(prep, PREP * (HEADS * j + 2))
                            load((HEADS * j + 2) % H, 0, False)
                        store(n, j * LASTS + done(x), j)
                for c in range(2):
                    sp.wait_ge(y_stored[c], 16 * (H // HEADS) * (LASTS // 2) + 16)

            @block.gpsimd
            def _(pool):
                nc.gpsimd.memset(e_sb[:, 0, 0:P], -1.0).then_inc(consts, 1)
                pool.wait_ge(consts, 1)
                nc.gpsimd.affine_select(out=z_sb[:, 0, 0:P], in_=e_sb[:, 0, 0:P], compare_op=ALU.is_ge, fill=0.0,
                                        base=0, pattern=[[-1, P]], channel_multiplier=1).then_inc(consts, 1)
                nc.gpsimd.affine_select(out=z_sb[:, 0, P:2 * P], in_=e_sb[:, 0, 0:P], compare_op=ALU.is_gt, fill=0.0,
                                        base=0, pattern=[[1, P]], channel_multiplier=-1).then_inc(consts, 1)

                def causal(tile, d, c0):
                    return nc.gpsimd.affine_select(out=tile, in_=tile, compare_op=ALU.is_gt, fill=0.0,
                                                   base=c0 - d * P, pattern=[[1, NT - c0]], channel_multiplier=-1)

                pool.sem_inc(lo_done, R)
                with pool.Fori(0, H // HEADS) as j:
                    for s in range(N + MASK):
                        if LO <= s < N + LO:
                            n = s - LO
                            c0 = items[n][5]
                            pool.wait_ge(hi_done, j * N + done(n))
                            nc.gpsimd.tensor_tensor(sp_lo[:, n % R, c0:NT], sp_sb[:, n % R, c0:NT],
                                                    f32(sp_hi[:, n % R, c0:NT]), ALU.subtract).then_inc(lo_done, 1)
                        if SP <= s < N + SP:
                            n = s - SP
                            slot, c, qt, kb, d, c0, first, last = items[n]
                            tile = sp_sb[:, n % R, c0:NT]
                            if d >= 0:
                                pool.wait_ge(sp_done, j * N + done(n))
                                pool.sem_inc(passed, 1)
                                causal(tile, d, c0).then_inc(masked, 1)
                        if MASK <= s + 1 < N + MASK and items[s + 1 - MASK][4] >= 0:
                            n = s + 1 - MASK
                            slot, c, qt, kb, d, c0, first, last = items[n]
                            pool.wait_ge(a_done, j * N + done(n))
                            pool.sem_inc(passed, 1)
                            causal(a_sb[:, n % R, c0:NT], d, c0).then_inc(a_masked, 1)

            @block.scalar
            def _(act):
                for s in ringed["act"]:
                    act.sem_inc(s, R)
                nc.scalar.preload_act_table_set("natural_log_exp_and_others")
                act.wait_ge(consts, 5)
                with act.Fori(0, H // HEADS) as j:
                    for s in range(N + OUT):
                        if s < N:
                            n = s
                            c0 = items[n][5]
                            z = z_ps[:, n % RZ, c0:NT]
                            act.wait_ge(z_done, j * N + done(n))
                            act.wait_ge(t_done, j * N + freed(n))
                            nc.scalar.copy(z_sb[:, n % R, c0:NT], z).then_inc(z_copied, 1)
                        if LN <= s < N + LN:
                            n = s - LN
                            e = e_sb[:, n % R, items[n][5]:NT]
                            act.wait_ge(e_done, j * N + done(n))
                            nc.scalar.activation(e, e, ACT.Ln, bias=1.0).then_inc(l_done, 1)
                        if s < N:
                            n = s
                            c0 = items[n][5]
                            act.wait_ge(sp_done, j * N + freed(n))
                            nc.scalar.activation(e_sb[:, n % R, c0:NT], z_ps[:, n % RZ, c0:NT], ACT.Exp
                                                 ).then_inc(e_done, 1)
                        if EXP <= s < N + EXP:
                            n = s - EXP
                            c0 = items[n][5]
                            act.wait_ge(t_done, j * N + done(n))
                            act.wait_ge(av_done, j * N + freed(n))
                            nc.scalar.activation(a_sb[:, n % R, c0:NT], t_sb[:, n % R, c0:NT], ACT.Exp
                                                 ).then_inc(a_done, 1)
                        if s >= OUT and items[s - OUT][7]:
                            n = s - OUT
                            c = items[n][1]
                            act.wait_ge(av_done, j * N + done(n))
                            act.wait_ge(y_stored[c], 16 * (j * (LASTS // 2) + chain_tile(n) + 1))
                            nc.scalar.copy(y_sb[:, c], y_ps[0:DH, c]).then_inc(y_done, 1)

            @block.tensor
            def _(pe):
                for s in ringed["pe"]:
                    pe.sem_inc(s, R)
                pe.sem_inc(rest_done, R)
                pe.wait_ge(consts, 5)
                with pe.Fori(0, H // HEADS) as j:
                    for s in range(-1, N + AV):
                        if s + 1 < N:
                            n = s + 1
                            slot, c, qt, kb, d, c0, first, last = items[n]
                            if n % PER_HEAD == 0:
                                pe.wait_ge(prep, PREP * (HEADS * j + slot + 1))
                            pe.wait_ge(e_done, j * N + done(n - RZ))
                            qs = slice(qt * NT + c0, (qt + 1) * NT)
                            out = z_ps[:, n % RZ, c0:NT]
                            kw = k_st[:, slot, kb * P:(kb + 1) * P]
                            nc.tensor.matmul(out, kw, q_hi[:, slot, qs], start=True, stop=False)
                            nc.tensor.matmul(out, kw, q_lo[:, slot, qs], start=False, stop=True).then_inc(z_done, 1)
                        if REST <= s < N + REST:
                            n = s - REST
                            slot, c, qt, kb, d, c0, first, last = items[n]
                            out = sum_ps[:, c, c0:NT]
                            pe.wait_ge(t_done, j * N + done(n))
                            for part in (sp_hi, sp_lo):
                                mm = nc.tensor.matmul(out, neg_rest[:], part[:, n % R, c0:NT], start=False,
                                                      stop=last and part is sp_lo, skip_group_check=True)
                            mm.then_inc(rest_done, 1)
                        if OWN <= s < N + OWN:
                            n = s - OWN
                            slot, c, qt, kb, d, c0, first, last = items[n]
                            out = sum_ps[:, c, c0:NT]
                            pe.wait_ge(lo_done, j * N + done(n))
                            for part in (sp_hi, sp_lo):
                                mm = nc.tensor.matmul(out, neg_own[:], part[:, n % R, c0:NT],
                                                      start=first and part is sp_hi, stop=False,
                                                      skip_group_check=True)
                            mm.then_inc(own_done, 1)
                        if AV <= s < N + AV:
                            n = s - AV
                            slot, c, qt, kb, d, c0, first, last = items[n]
                            pe.wait_ge(a_done, j * N + done(n))
                            if d >= 0:
                                pe.wait_ge(a_masked, j * DIAG + diag_before[n] + 1)
                            if first:
                                pe.wait_ge(y_done, j * LASTS + done(tile_before(n)))
                            nc.tensor.matmul(y_ps[0:DH, c, c0:NT], v_sb[:, slot, kb], a_sb[:, n % R, c0:NT],
                                             start=first, stop=last, skip_group_check=True).then_inc(av_done, 1)

            @block.vector
            def _(dve):
                for s in ringed["dve"]:
                    dve.sem_inc(s, R)
                dve.wait_ge(consts, 3)
                nc.vector.tensor_copy(neg_own[:], z_sb[:, 0, 0:P]).then_inc(consts, 1)
                nc.vector.tensor_copy(neg_rest[:], z_sb[:, 0, P:2 * P]).then_inc(consts, 1)

                def split(i, head, slot):
                    part, step = divmod(i, 4)
                    x = slice(part * NT, (part + 1) * NT)
                    lower = slice(DH, P)
                    if i == 0:
                        dve.wait_ge(q_loaded, 32 * (head + 1))
                        dve.wait_ge(k_loaded, 32 * (head + 1))
                        dve.wait_ge(v_loaded, 16 * (head + 1))
                    if step == 0:
                        op = nc.vector.tensor_scalar(q_hi[:, slot, x], q_raw[:, x], SCALE, None, ALU.mult)
                    elif step == 1:
                        op = nc.vector.tensor_copy(k_st[:, slot, x], k_raw[:, x])
                    elif step == 2:
                        dve.wait_ge(prep, PREP * head + 4 * part + 1)
                        op = nc.vector.scalar_tensor_tensor(out=q_lo[:, slot, x], in0=q_raw[:, x], scalar=SCALE,
                                                            in1=f32(q_hi[:, slot, x]), op0=ALU.mult,
                                                            op1=ALU.subtract)
                    else:
                        dve.wait_ge(prep, PREP * head + 4 * part + 2)
                        op = nc.vector.tensor_tensor(k_st[lower, slot, x], k_raw[lower, x],
                                                     f32(k_st[lower, slot, x]), ALU.subtract)
                    op.then_inc(prep, 1)

                for i in range(PREP):
                    split(i, 0, 0)
                with dve.Fori(0, H // HEADS) as j:
                    for s in range(N + SUM):
                        if HI <= s < N + HI:
                            n = s - HI
                            d, c0 = items[n][4:6]
                            if d >= 0:
                                dve.wait_ge(masked, j * DIAG + diag_before[n] + 1)
                            dve.wait_ge(sp_done, j * N + done(n))
                            dve.wait_ge(rest_done, j * N + freed(n))
                            nc.vector.tensor_copy(sp_hi[:, n % R, c0:NT], sp_sb[:, n % R, c0:NT]
                                                  ).then_inc(hi_done, 1)
                        if SP <= s < N + SP:
                            n = s - SP
                            c0 = items[n][5]
                            dve.wait_ge(l_done, j * N + done(n))
                            dve.wait_ge(z_copied, j * N + done(n))
                            dve.wait_ge(lo_done, j * N + freed(n))
                            nc.vector.scalar_tensor_tensor(out=sp_sb[:, n % R, c0:NT], in0=e_sb[:, n % R, c0:NT],
                                                           scalar=SP_CAP, in1=z_sb[:, n % R, c0:NT], op0=ALU.min,
                                                           op1=ALU.max).then_inc(sp_done, 1)
                        if SUM <= s < N + SUM:
                            n = s - SUM
                            slot, c, qt, kb, d, c0, first, last = items[n]
                            dve.wait_ge(own_done, j * N + done(n))
                            dve.wait_ge(a_done, j * N + freed(n))
                            nc.vector.tensor_tensor(t_sb[:, n % R, c0:NT], sum_ps[:, c, c0:NT],
                                                    z_sb[:, n % R, c0:NT], ALU.add).then_inc(t_done, 1)
                        for slot in range(HEADS):
                            i = s - slot * PER_HEAD - 16
                            if 0 <= i < PREP:
                                split(i, HEADS * j + slot + 1, 1 - slot)


E = 16


def merge_branches(nc, sem, projT, yT, w_br, mergedT, w_o, w_o_raw, w_o_loaded):
    B = 3
    KB = W // P
    with ExitStack() as ctx:
        sb = lambda n, s, dt=F32: ctx.enter_context(nc.sbuf_tensor(n, s, dt))
        w_raw = sb("mb_w_raw", [P, B * KB, D])
        w_hi = sb("mb_w_hi", [P, B * KB, D], F32R)
        w_lo = sb("mb_w_lo", [P, B * KB, D], F32R)
        y_raw = sb("mb_y_raw", [P, B * KB, NT])
        y_hi = sb("mb_y_hi", [P, 2, B * KB, NT], F32R)
        y_lo = sb("mb_y_lo", [P, 2, B * KB, NT], F32R)
        gate = sb("mb_gate", [P, 4, B, NT])
        part = sb("mb_part", [P, 2, B, NT])
        acc = ctx.enter_context(nc.psum_tensor("mb_acc", [P, 2, B, NT], F32))
        w_loaded = [sem(f"mb_w_loaded{i}") for i in range(B)]
        y_loaded = sem("mb_y_loaded")
        gate_loaded = [sem(f"mb_gate_loaded{b}") for b in range(4)]
        w_hi_done = sem("mb_w_hi_done")
        w_lo_done = sem("mb_w_lo_done")
        y_hi_done = sem("mb_y_hi_done")
        y_lo_done = sem("mb_y_lo_done")
        product_done = sem("mb_product_done")
        gated = sem("mb_gated")
        summed = sem("mb_summed")
        stored = [sem(f"mb_stored{b}") for b in range(2)]
        gates_dram = projT[GATES:COLS].rearrange("(i m) p s -> m p i s", i=B)
        n_items = TT * KT

        with nc.Block() as block:

            @block.sync
            def _(sp):
                def load_y(t):
                    sp.dma_start(y_raw[:], yT[:, :, bass.ds(t * NT, NT)]).then_inc(y_loaded, 16)

                def load_gates(t, m):
                    sp.dma_start(gate[:, m % 4], gates_dram[m, :, :, bass.ds(t * NT, NT)]
                                 ).then_inc(gate_loaded[m % 4], 16)

                load_y(0)
                for i in range(B):
                    r = slice(i * KB, (i + 1) * KB)
                    sp.dma_start(w_raw[:, r], w_br[:, r]).then_inc(w_loaded[i], 16)
                for m in range(4):
                    load_gates(0, m)
                for k in range(KT):
                    sp.dma_start(w_o_raw[:, k], w_o[:, k]).then_inc(w_o_loaded, 16)
                for b in range(2):
                    sp.sem_inc(stored[b], 16)
                with sp.Fori(0, TT // 2) as j:
                    for b in range(2):
                        t = 2 * j + b
                        for m in range(KT):
                            n = t * KT + m
                            if m == 0:
                                sp.wait_ge(y_lo_done, t + 1)
                                load_y((t + 1) % TT)
                            sp.wait_ge(summed, 2 * n + 2)
                            sp.dma_start(mergedT[m, :, bass.ds(t * NT, NT)], part[:, m % 2, 0]
                                         ).then_inc(stored[m % 2], 16)
                            ahead = t if m < KT - 4 else (t + 1) % TT
                            load_gates(ahead, (m + 4) % KT)
                for b in range(2):
                    sp.wait_ge(stored[b], 16 * (n_items // 2) + 16)
                for b in range(4):
                    sp.wait_ge(gate_loaded[b], 16 * (n_items // 4 + 1))
                sp.wait_ge(y_loaded, 16 * (TT + 1))
                sp.wait_ge(w_o_loaded, 16 * KT)

            @block.scalar
            def _(act):
                def y_high(t, b):
                    act.wait_ge(y_loaded, 16 * (t + 1))
                    nc.scalar.copy(y_hi[:, b], y_raw[:]).then_inc(y_hi_done, 1)

                y_high(0, 0)
                for i in range(B):
                    r = slice(i * KB, (i + 1) * KB)
                    act.wait_ge(w_loaded[i], 16)
                    nc.scalar.copy(w_hi[:, r], w_raw[:, r]).then_inc(w_hi_done, 1)
                with act.Fori(0, TT // 2) as j:
                    for b in range(2):
                        t = 2 * j + b
                        act.wait_ge(product_done, t * KT + 1)
                        y_high(t + 1, 1 - b)

            @block.vector
            def _(dve):
                def y_low(t, b):
                    dve.wait_ge(y_hi_done, t + 1)
                    nc.vector.tensor_tensor(y_lo[:, b], y_raw[:], f32(y_hi[:, b]), ALU.subtract
                                            ).then_inc(y_lo_done, 1)

                dve.sem_inc(gated, 2 * B)
                y_low(0, 0)
                for i in range(B):
                    r = slice(i * KB, (i + 1) * KB)
                    dve.wait_ge(w_hi_done, i + 1)
                    nc.vector.tensor_tensor(w_lo[:, r], w_raw[:, r], f32(w_hi[:, r]), ALU.subtract
                                            ).then_inc(w_lo_done, 1)
                with dve.Fori(0, TT // 2) as j:
                    for b in range(2):
                        t = 2 * j + b
                        for m in range(KT):
                            n = t * KT + m
                            if m == 3:
                                y_low(t + 1, 1 - b)
                            dve.wait_ge(gate_loaded[m % 4], 16 * (t * (KT // 4) + m // 4 + 1))
                            dve.wait_ge(product_done, n + 2)
                            dve.wait_ge(stored[m % 2], 16 * (t * (KT // 2) + m // 2 + 1))
                            for i in range(B):
                                nc.vector.tensor_tensor(part[:, m % 2, i], acc[:, m % 2, i], gate[:, m % 4, i],
                                                        ALU.mult).then_inc(gated, 1)
                            for i in range(1, B):
                                dve.wait_ge(gated, B * (n + 2) + i + 1)
                                if i > 1:
                                    dve.wait_ge(summed, 2 * n + 1)
                                nc.vector.tensor_tensor(part[:, m % 2, 0], part[:, m % 2, 0], part[:, m % 2, i],
                                                        ALU.add).then_inc(summed, 1)

            @block.tensor
            def _(pe):
                pe.sem_inc(product_done, 1)
                pe.wait_ge(w_lo_done, B)
                with pe.Fori(0, TT // 2) as j:
                    for b in range(2):
                        t = 2 * j + b
                        pe.wait_ge(y_lo_done, t + 1)
                        for m in range(KT):
                            n = t * KT + m
                            pe.wait_ge(gated, B * n + B)
                            for i in range(B):
                                for k in range(KB):
                                    ik = i * KB + k
                                    out, c = acc[:, m % 2, i], slice(m * P, (m + 1) * P)
                                    nc.tensor.matmul(out, w_hi[:, ik, c], y_hi[:, b, ik], start=k == 0, stop=False)
                                    nc.tensor.matmul(out, w_hi[:, ik, c], y_lo[:, b, ik], start=False, stop=False)
                                    last = nc.tensor.matmul(out, w_lo[:, ik, c], y_hi[:, b, ik],
                                                            start=False, stop=k == KB - 1)
                            last.then_inc(product_done, 1)


def mix_out(nc, sem, mergedT, w_raw, w_loaded, h_dram, ln_g, ln_b, w_router, h2_dram, logits, ident):
    HR = 4
    with ExitStack() as ctx:
        sb = lambda n, s, dt=F32: ctx.enter_context(nc.sbuf_tensor(n, s, dt))
        ps = lambda n, s, dt=F32: ctx.enter_context(nc.psum_tensor(n, s, dt))
        w_hi = sb("mo_w_hi", [P, KT, D], F32R)
        w_lo = sb("mo_w_lo", [P, KT, D], F32R)
        wr = sb("mo_w_router", [P, KT, E])
        m_raw = sb("mo_m_raw", [P, 2, KT, P])
        m_hi = sb("mo_m_hi", [P, 2, KT, P], F32R)
        m_lo = sb("mo_m_lo", [P, 2, KT, P], F32R)
        h = sb("mo_h", [P, 2, D])
        g_row = sb("mo_g", [P, D])
        b_row = sb("mo_b", [P, D])
        x2 = sb("mo_x2", [P, 2, D])
        h2 = sb("mo_h2", [P, HR, D])
        h2T = sb("mo_h2T", [P, KT, P])
        zeros = sb("mo_zeros", [P, D])
        stats = sb("mo_stats", [P, 2, 12])
        mv = sb("mo_mv", [P, 2, 4])
        half = sb("mo_half", [P, 1])
        out = ps("mo_out", [P, 2, 2, NT])
        tp = ps("mo_tp", [P, KT, P])
        lg = ps("mo_lg", [P, 2, NT])
        rows_loaded = sem("mo_rows_loaded")
        m_loaded = [sem(f"mo_m_loaded{b}") for b in range(2)]
        h_loaded = [sem(f"mo_h_loaded{b}") for b in range(2)]
        w_hi_done = sem("mo_w_hi_done")
        w_lo_done = sem("mo_w_lo_done")
        m_hi_done = sem("mo_m_hi_done")
        m_lo_done = sem("mo_m_lo_done")
        product_done = sem("mo_product_done")
        residual = sem("mo_residual")
        stat_chain = sem("mo_stat_chain")
        passed = sem("passed")
        consts = sem("mo_consts")
        rstd_done = sem("mo_rstd_done")
        normed = sem("mo_normed")
        scaled = sem("mo_scaled")
        h2_done = sem("mo_h2_done")
        h2_stored = [sem(f"mo_h2_stored{q}") for q in range(HR)]
        pad_stored = sem("mo_pad_stored")
        turned = sem("mo_turned")
        h2T_done = sem("mo_h2T_done")
        logit_done = sem("mo_logit_done")
        logits_copied = sem("mo_logits_copied")
        m_t = mergedT.rearrange("m p (t c) -> p t m c", c=P)
        h_t = h_dram.rearrange("(t p) d -> p t d", p=P)
        h2_t = h2_dram.rearrange("(t p) d -> p t d", p=P)
        flat = lambda a: a.rearrange("p o d -> p (o d)")

        def steps(eng, step):
            for s in range(HR):
                step(s, s, True)
            with eng.Fori(1, TILES // HR) as j:
                for q in range(HR):
                    step(HR * j + q, q, True)
            for s in range(TILES, TILES + 3):
                step(s, s % HR, False)

        def first(s, lag):
            return isinstance(s, int) and s < lag

        def past(s, lag):
            return isinstance(s, int) and s - lag >= TILES

        with nc.Block() as block:

            @block.sync
            def _(sp):
                def step(s, q, product):
                    if product:
                        b = q % 2
                        if not first(s, 2):
                            sp.wait_ge(residual, 2 * s - 2)
                        sp.dma_start(m_raw[:, b], m_t[:, bass.ds(s, 1)].rearrange("p o m c -> p (o m) c")
                                     ).then_inc(m_loaded[b], 16)
                        sp.dma_start(h[:, b], flat(h_t[:, bass.ds(s, 1)])).then_inc(h_loaded[b], 16)
                    if isinstance(s, int) and s == 0:
                        sp.dma_start(g_row[:], ln_g.partition_broadcast(P)).then_inc(rows_loaded, 16)
                        sp.dma_start(b_row[:], ln_b.partition_broadcast(P)).then_inc(rows_loaded, 16)
                        sp.dma_start(wr[:], w_router).then_inc(rows_loaded, 16)
                    if not first(s, 3):
                        sp.wait_ge(h2_done, s - 2)
                        sp.dma_start(flat(h2_t[:, bass.ds(s - 3, 1)]), h2[:, (q + 1) % HR]
                                     ).then_inc(h2_stored[(q + 1) % HR], 16)

                steps(sp, step)
                sp.wait_ge(consts, 2)
                sp.dma_start(flat(h2_t[:, TILES:TILES + 1]), zeros[:]).then_inc(pad_stored, 16)
                for q in range(HR):
                    sp.wait_ge(h2_stored[q], 16 * (TILES // HR))
                sp.wait_ge(pad_stored, 16)

            @block.gpsimd
            def _(pool):
                nc.gpsimd.memset(half[:], -0.5).then_inc(consts, 1)
                nc.gpsimd.memset(zeros[:], 0.0).then_inc(consts, 1)
                pool.wait_ge(consts, 2)
                pool.wait_ge(rows_loaded, 48)

                def step(s, q, product):
                    if first(s, 1) or past(s, 1):
                        return
                    q, b = (q - 1) % HR, (q - 1) % 2
                    pool.wait_ge(stat_chain, 4 * s)
                    nc.gpsimd.tensor_tensor(mv[:, b, 3:4], mv[:, b, 2:3], half[:], ALU.pow).then_inc(rstd_done, 1)
                    if not first(s, HR + 1):
                        pool.wait_ge(h2_stored[q], 16 * ((s - 1) // HR))
                        pool.wait_ge(turned, s - HR)
                    pool.wait_ge(normed, s)
                    nc.gpsimd.tensor_tensor(h2[:, q], x2[:, b], g_row[:], ALU.mult).then_inc(scaled, 1)
                    pool.wait_ge(scaled, s)
                    nc.gpsimd.tensor_tensor(h2[:, q], h2[:, q], b_row[:], ALU.add).then_inc(h2_done, 1)

                steps(pool, step)

            @block.scalar
            def _(act):
                def step(s, q, product):
                    if product:
                        b = q % 2
                        act.wait_ge(m_loaded[b], 16 * (s // 2 + 1))
                        if not first(s, 2):
                            act.wait_ge(product_done, 2 * s - 2)
                        nc.scalar.copy(m_hi[:, b], m_raw[:, b]).then_inc(m_hi_done, 1)
                    if isinstance(s, int) and s == 0:
                        act.wait_ge(w_loaded, 16 * KT)
                        for k in range(KT):
                            nc.scalar.copy(w_hi[:, k], w_raw[:, k]).then_inc(w_hi_done, 1)
                    if not first(s, 3):
                        if not first(s, 4):
                            act.wait_ge(logit_done, s - 3)
                        act.wait_ge(turned, s - 2)
                        nc.scalar.copy(h2T[:], tp[:]).then_inc(h2T_done, 1)

                steps(act, step)
                act.wait_ge(logit_done, TILES)
                for b in range(2):
                    nc.scalar.copy(logits[:, b::2], lg[:, b, 0:TILES // 2 * E].rearrange("p (t e) -> p t e", e=E)
                                   ).then_inc(logits_copied, 1)

            @block.vector
            def _(dve):
                def step(s, q, product):
                    if product:
                        b = q % 2
                        if not first(s, 2):
                            dve.wait_ge(product_done, 2 * s - 2)
                        dve.wait_ge(m_hi_done, s + 1)
                        nc.vector.tensor_tensor(m_lo[:, b], m_raw[:, b], f32(m_hi[:, b]), ALU.subtract
                                                ).then_inc(m_lo_done, 1)
                    if isinstance(s, int) and s == 0:
                        for k in range(KT):
                            dve.wait_ge(w_hi_done, k + 1)
                            nc.vector.tensor_tensor(w_lo[:, k], w_raw[:, k], f32(w_hi[:, k]), ALU.subtract
                                                    ).then_inc(w_lo_done, 1)
                    if first(s, 1) or past(s, 1):
                        return
                    b = (q - 1) % 2
                    dve.wait_ge(h_loaded[b], 16 * ((s - 1) // 2 + 1))
                    if not first(s, 3):
                        dve.wait_ge(scaled, s - 2)
                    for c in range(2):
                        x = slice(c * NT, (c + 1) * NT)
                        dve.wait_ge(product_done, 2 * s - 1 + c)
                        nc.vector.scalar_tensor_tensor(out=x2[:, b, x], in0=h[:, b, x], scalar=ALPHA,
                                                       in1=out[:, b, c], op0=ALU.mult, op1=ALU.add
                                                       ).then_inc(residual, 1)
                    for c in range(2):
                        dve.wait_ge(residual, 2 * s - 1 + c)
                        nc.vector.bn_stats(stats[:, b, 6 * c:6 * c + 6], x2[:, b, c * NT:(c + 1) * NT]
                                           ).then_inc(stat_chain, 1)
                    dve.wait_ge(stat_chain, 4 * s - 2)
                    dve.sem_inc(passed, 1)
                    nc.vector.bn_aggr(mv[:, b, 0:2], stats[:, b]).then_inc(stat_chain, 1)
                    dve.wait_ge(stat_chain, 4 * s - 1)
                    nc.vector.tensor_scalar(mv[:, b, 2:3], mv[:, b, 1:2], EPS, None, ALU.add).then_inc(stat_chain, 1)
                    dve.wait_ge(rstd_done, s)
                    nc.vector.tensor_scalar(x2[:, b], x2[:, b], mv[:, b, 0:1], mv[:, b, 3:4],
                                            ALU.subtract, ALU.mult).then_inc(normed, 1)

                steps(dve, step)

            @block.tensor
            def _(pe):
                def product_half(s, b, c):
                    if not first(s, 2):
                        pe.wait_ge(residual, 2 * s - 3 + c)
                    for k in range(KT):
                        if isinstance(s, int) and s == 0 and c == 0:
                            pe.wait_ge(w_lo_done, k + 1)
                        o, x = out[:, b, c], slice(c * NT, (c + 1) * NT)
                        nc.tensor.matmul(o, m_hi[:, b, k], w_hi[:, k, x], start=k == 0, stop=False)
                        nc.tensor.matmul(o, m_lo[:, b, k], w_hi[:, k, x], start=False, stop=False)
                        last = nc.tensor.matmul(o, m_hi[:, b, k], w_lo[:, k, x], start=False, stop=k == KT - 1)
                    last.then_inc(product_done, 1)

                def step(s, q, product):
                    if product:
                        pe.wait_ge(m_lo_done, s + 1)
                        product_half(s, q % 2, 0)
                    if not first(s, 3):
                        pe.wait_ge(h2T_done, s - 2)
                        cols = bass.ds((s - 3) // 2 * E, E)
                        for k in range(KT):
                            last = nc.tensor.matmul(lg[:, (q + 1) % 2, cols], h2T[:, k], wr[:, k], start=k == 0,
                                                    stop=k == KT - 1, skip_group_check=True)
                        last.then_inc(logit_done, 1)
                    if product:
                        product_half(s, q % 2, 1)
                    if not first(s, 2) and not past(s, 2):
                        pe.wait_ge(h2_done, s - 1)
                        if not first(s, 3):
                            pe.wait_ge(h2T_done, s - 2)
                        for k in range(KT):
                            last = nc.tensor.transpose(tp[:, k], h2[:, (q + 2) % HR, k * P:(k + 1) * P], ident[:])
                        last.then_inc(turned, 1)

                steps(pe, step)


EG = 4
FF = 128
GUC, DNC = KT, EG
E_TILES = TILES + EG - 1
META = 8


def dispatch(nc, sem, logits, router_bias, order, meta, table, gu_w, dn_w, gu_raw, dn_raw, gu_loaded, dn_loaded):
    with ExitStack() as ctx:
        sb = lambda n, s, dt=F32: ctx.enter_context(nc.sbuf_tensor(n, s, dt))
        TG = TILES * EG
        bias = sb("dp_bias", [P, E])
        score = sb("dp_score", [P, TG, EG])
        sel = sb("dp_sel", [P, TG, EG])
        rank = sb("dp_rank", [P, TG, EG])
        cmp = sb("dp_cmp", [P, TG])
        taken = sb("dp_taken", [P, TG, EG])
        g_score = sb("dp_g_score", [P, TG])
        g_rank = sb("dp_g_rank", [P, TG])
        best = sb("dp_best", [P, TG])
        before = sb("dp_before", [P, P])
        ones = sb("dp_ones", [P, P])
        tile_sum = sb("dp_tile_sum", [P, TG])
        upto = sb("dp_upto", [P, TG])
        place = sb("dp_place", [P, TG])
        slot = sb("dp_slot", [P, TILES])
        slot_u = sb("dp_slot_u", [P, TILES], U32)
        denom = sb("dp_denom", [P, TILES])
        rdenom = sb("dp_rdenom", [P, TILES])
        weight = sb("dp_weight", [P, TILES, EG])
        steps = sb("dp_steps", [P, TILES])
        over = sb("dp_over", [P, EG, TILES])
        g_tiles = sb("dp_g_tiles", [P, EG])
        start = sb("dp_start", [P, EG])
        tile_no = sb("dp_tile_no", [P, E_TILES])
        past = sb("dp_past", [P, 3, E_TILES])
        group = sb("dp_group", [P, E_TILES])
        need = sb("dp_need", [P, 4])
        pad = sb("dp_pad", [P, E_TILES, META])
        row = sb("dp_row", [P, TILES, META])
        ps = ctx.enter_context(nc.psum_tensor("dp_ps", [P, 2, NT], F32))
        loaded = sem("dp_loaded")
        consts = sem("dp_consts")
        scored = sem("dp_scored")
        chain = sem("dp_chain")
        counted = sem("dp_counted")
        padded = sem("dp_padded")
        row_done = sem("dp_row_done")
        scattered = sem("dp_scattered")
        meta_loaded = sem("dp_meta_loaded")
        order_t = order.rearrange("(t p) w -> p t w", p=P)

        with nc.Block() as block:

            @block.sync
            def _(sp):
                sp.dma_start(bias[:], router_bias.partition_broadcast(P)).then_inc(loaded, 16)
                sp.dma_start(gu_raw[:, 0], gu_w[0]).then_inc(gu_loaded, 16)
                sp.dma_start(dn_raw[:, 0], dn_w[0]).then_inc(dn_loaded, 16)
                sp.wait_ge(consts, 6)
                sp.dma_start(order_t, pad[:]).then_inc(padded, 16)
                sp.wait_ge(scattered, 16 * TILES)
                sp.dma_start(meta[:], order_t).then_inc(meta_loaded, 16)
                sp.wait_ge(meta_loaded, 16)

            @block.gpsimd
            def _(pool):
                nc.gpsimd.memset(pad[:], 0.0).then_inc(consts, 1)
                nc.gpsimd.memset(row[:], 0.0).then_inc(consts, 1)
                nc.gpsimd.memset(ones[:], 1.0).then_inc(consts, 1)
                pool.wait_ge(consts, 3)
                nc.gpsimd.affine_select(out=before[:], in_=ones[:], compare_op=ALU.is_gt, fill=0.0, base=0,
                                        pattern=[[1, P]], channel_multiplier=-1).then_inc(consts, 1)
                nc.gpsimd.iota(pad[:, :, 0].bitcast(U32), [[0, E_TILES]], base=S, channel_multiplier=1
                               ).then_inc(consts, 1)
                nc.gpsimd.iota(row[:, :, 0].bitcast(U32), [[P, TILES]], base=0, channel_multiplier=1
                               ).then_inc(consts, 1)
                nc.gpsimd.iota(steps[:], [[P, TILES]], base=0, channel_multiplier=0,
                               allow_small_or_imprecise_dtypes=True).then_inc(consts, 1)
                nc.gpsimd.iota(tile_no[:], [[1, E_TILES]], base=0, channel_multiplier=0,
                               allow_small_or_imprecise_dtypes=True).then_inc(consts, 1)
                pool.wait_ge(padded, 16)
                pool.wait_ge(row_done, 2)
                for t in range(TILES):
                    nc.gpsimd.indirect_dma_start(out=order, out_offset=bass.IndirectOffsetOnAxis(slot_u[:, t:t + 1], 0),
                                                 in_=row[:, t], in_offset=None).then_inc(scattered, 16)

            @block.scalar
            def _(act):
                nc.scalar.activation(score[:].rearrange("p (t g) e -> p t (g e)", g=EG), logits[:], ACT.Sigmoid
                                     ).then_inc(scored, 1)

            @block.tensor
            def _(pe):
                pe.wait_ge(consts, 4)
                pe.wait_ge(counted, 1)
                nc.tensor.matmul(ps[:, 0, 0:TG], before[:], best[:], start=True, stop=True)
                nc.tensor.matmul(ps[:, 1, 0:TG], ones[:], best[:], start=True, stop=True).then_inc(counted, 1)

            @block.vector
            def _(dve):
                count = [0]

                def link(op):
                    count[0] += 1
                    op.then_inc(chain, 1)
                    dve.wait_ge(chain, count[0])

                def ranks(out, x, n):
                    for i in range(n):
                        for j in [j for j in range(n) if j != i]:
                            first = j == (0 if i else 1)
                            op = ALU.is_gt if j > i else ALU.is_ge
                            if first:
                                link(nc.vector.tensor_tensor(out[:, :, i], x[:, :, j], x[:, :, i], op))
                            else:
                                tmp = cmp[:, 0:x.shape[1]]
                                link(nc.vector.tensor_tensor(tmp, x[:, :, j], x[:, :, i], op))
                                link(nc.vector.tensor_tensor(out[:, :, i], out[:, :, i], tmp, ALU.add))

                by_token = lambda a: a.rearrange("p (t g) e -> p t (g e)", g=EG)
                by_group = lambda a: a.rearrange("p (t g) -> p t g", g=EG)
                dve.wait_ge(loaded, 16)
                dve.wait_ge(scored, 1)
                link(nc.vector.tensor_tensor(by_token(sel[:]), by_token(score[:]),
                                             bias[:].unsqueeze(1).to_broadcast([P, TILES, E]), ALU.add))
                ranks(rank[:], sel[:], EG)
                link(nc.vector.tensor_scalar(taken[:], rank[:], 2.0, None, ALU.is_lt))
                link(nc.vector.tensor_tensor(rank[:], sel[:], taken[:], ALU.mult))
                link(nc.vector.tensor_reduce(g_score[:], rank[:], AX_X, ALU.add))
                ranks(by_group(g_rank[:]), by_group(g_score[:]), EG)
                nc.vector.tensor_scalar(best[:], g_rank[:], 1.0, None, ALU.is_lt).then_inc(counted, 1)
                dve.wait_ge(counted, 1)
                link(nc.vector.tensor_tensor(taken[:], taken[:], score[:], ALU.mult))
                link(nc.vector.tensor_tensor(taken[:], taken[:], best[:].unsqueeze(2).to_broadcast([P, TG, EG]),
                                             ALU.mult))
                link(nc.vector.tensor_reduce(denom[:], by_token(taken[:]), AX_X, ALU.add))
                link(nc.vector.reciprocal(rdenom[:], denom[:]))
                link(nc.vector.tensor_reduce(weight[:], taken[:].rearrange("p (t g) e -> p t e g", g=EG),
                                             AX_X, ALU.add))
                dve.wait_ge(consts, 8)
                nc.vector.tensor_tensor(row[:, :, 1:1 + EG], weight[:],
                                        rdenom[:].unsqueeze(2).to_broadcast([P, TILES, EG]), ALU.mult
                                        ).then_inc(row_done, 1)
                dve.wait_ge(counted, 2)
                link(nc.vector.tensor_copy(tile_sum[:], ps[:, 1, 0:TG]))
                for g in range(EG):
                    x = by_group(tile_sum[:])[:, :, g]
                    link(nc.vector.tensor_tensor_scan(by_group(upto[:])[:, :, g], ones[:, 0:TILES], x, 0.0,
                                                      ALU.mult, ALU.add))
                link(nc.vector.tensor_tensor(place[:], upto[:], tile_sum[:], ALU.subtract))
                link(nc.vector.tensor_tensor(place[:], place[:], ps[:, 0, 0:TG], ALU.add))
                total = by_group(upto[:])[:, TILES - 1]
                link(nc.vector.tensor_tensor(over[:], total.unsqueeze(2).to_broadcast([P, EG, TILES]),
                                             steps[:].unsqueeze(1).to_broadcast([P, EG, TILES]), ALU.is_gt))
                link(nc.vector.tensor_reduce(g_tiles[:], over[:], AX_X, ALU.add))
                link(nc.vector.memset(start[:, 0:1], 0.0))
                for g in range(1, EG):
                    link(nc.vector.tensor_tensor(start[:, g:g + 1], start[:, g - 1:g], g_tiles[:, g - 1:g], ALU.add))
                link(nc.vector.scalar_tensor_tensor(out=by_group(place[:]),
                                                    in0=start[:].unsqueeze(1).to_broadcast([P, TILES, EG]),
                                                    scalar=float(P), in1=by_group(place[:]), op0=ALU.mult, op1=ALU.add))
                link(nc.vector.tensor_tensor(place[:], place[:], best[:], ALU.mult))
                link(nc.vector.tensor_reduce(slot[:], by_group(place[:]), AX_X, ALU.add))
                nc.vector.tensor_copy(slot_u[:], slot[:]).then_inc(row_done, 1)
                link(nc.vector.tensor_tensor(past[:], tile_no[:].unsqueeze(1).to_broadcast([P, 3, E_TILES]),
                                             start[:, 1:EG].unsqueeze(2).to_broadcast([P, 3, E_TILES]), ALU.is_ge))
                link(nc.vector.tensor_reduce(group[:], past[:].rearrange("p g t -> p t g"), AX_X, ALU.add))
                link(nc.vector.tensor_copy(table[:, 0:E_TILES], group[0:1, :]))
                for c, a_tile in enumerate((GUC, 1)):
                    link(nc.vector.tensor_scalar(need[:, 2 * c:2 * c + 2], start[:, 1:3], float(a_tile), 1.0,
                                                 ALU.mult, ALU.add))
                link(nc.vector.tensor_copy(table[:, E_TILES:E_TILES + 4], need[0:1, :]))


def experts(nc, sem, h2_dram, meta, table, gu_w, dn_w, gu_raw, dn_raw, gu_loaded, dn_loaded, ln_g, ln_b, out, ident):
    RING = 4
    XR = 4
    with ExitStack() as ctx:
        sb = lambda n, s, dt=F32: ctx.enter_context(nc.sbuf_tensor(n, s, dt))
        ps = lambda n, s, dt=F32: ctx.enter_context(nc.psum_tensor(n, s, dt))
        w_hi = sb("ex_w_hi", [P, RING, D], F32R)
        w_lo = sb("ex_w_lo", [P, RING, D], F32R)
        x = sb("ex_x", [P, XR, D])
        o = sb("ex_o", [P, 2, D])
        xT_hi = sb("ex_xT_hi", [P, 2, KT, P], F32R)
        xT_lo = sb("ex_xT_lo", [P, 2, KT, P], F32R)
        act_g = sb("ex_gate", [P, EG * FF])
        hid = sb("ex_hid", [P, EG * FF])
        hT_sb = sb("ex_hT_sb", [P, EG, P])
        g_row = sb("ex_g", [P, D])
        b_row = sb("ex_b", [P, D])
        stats = sb("ex_stats", [P, 12])
        mv = sb("ex_mv", [P, 4])
        half = sb("ex_half", [P, 1])
        gather_ids = sb("ex_gather_ids", [P, XR, 1], U32)
        store_ids = sb("ex_store_ids", [P, 2, 1], U32)
        gu = ps("ex_gu", [P, 2, NT])
        y = ps("ex_y", [P, 2, NT])
        xT = ps("ex_xT", [P, KT, P])
        hT = ps("ex_hT", [P, EG, P])
        rows_loaded = sem("ex_rows_loaded")
        consts = sem("ex_consts")
        passed = sem("passed")
        gather_ids_done = sem("ex_gather_ids_done")
        store_ids_done = sem("ex_store_ids_done")
        x_loaded = [sem(f"ex_x_loaded{q}") for q in range(XR)]
        w_high = sem("ex_w_high")
        w_split = sem("ex_w_split")
        w_used = sem("ex_w_used")
        x_turned = sem("ex_x_turned")
        x_high = sem("ex_x_high")
        x_split = sem("ex_x_split")
        gate_done = sem("ex_gate_done")
        hid_done = sem("ex_hid_done")
        h_turned = sem("ex_h_turned")
        h_copied = sem("ex_h_copied")
        down_done = sem("ex_down_done")
        residual = sem("ex_residual")
        stat_chain = sem("ex_stat_chain")
        rstd_done = sem("ex_rstd_done")
        normed = sem("ex_normed")
        scaled = sem("ex_scaled")
        shifted = sem("ex_shifted")
        stored = sem("ex_stored")
        o_free = sem("ex_o_free")
        T = E_TILES

        def steps(eng, step):
            step(0, 0, True, False, False)
            step(1, 1, True, True, False)
            with eng.Fori(0, (T - 3) // XR) as j:
                for i in range(XR):
                    step(XR * j + 2 + i, (2 + i) % XR, True, True, True)
            step(T - 1, (T - 1) % XR, True, True, True)
            step(T, T % XR, False, True, True)
            step(T + 1, (T + 1) % XR, False, False, True)

        def chunk(s, i):
            return GUC * s + i

        def group_of(eng, t):
            return eng.value_load(table[0:1, bass.ds(t, 1)], min_val=0, max_val=EG - 1)

        meta_ids = meta[:, :, 0].bitcast(U32)

        with nc.Block() as block:

            @block.sync
            def _(sp):
                need = [sp.value_load(table[0:1, E_TILES + i:E_TILES + i + 1], min_val=1,
                                      max_val=GUC * T + 1) for i in range(4)]
                sp.dma_start(g_row[:], ln_g.partition_broadcast(P)).then_inc(rows_loaded, 16)
                sp.dma_start(b_row[:], ln_b.partition_broadcast(P)).then_inc(rows_loaded, 16)
                sp.wait_ge(x_loaded[1], 16)
                sp.wait_ge(gu_loaded, 16)
                sp.dma_start(gu_raw[:, 1], gu_w[1]).then_inc(gu_loaded, 16)
                sp.wait_ge(dn_loaded, 16)
                sp.dma_start(dn_raw[:, 1], dn_w[1]).then_inc(dn_loaded, 16)
                for g in (2, 3):
                    sp.wait_ge(gu_loaded, 16 * g)
                    sp.wait_ge(w_split, need[g - 2])
                    sp.dma_start(gu_raw[:, g % 2], gu_w[g]).then_inc(gu_loaded, 16)
                for g in (2, 3):
                    sp.wait_ge(dn_loaded, 16 * g)
                    sp.wait_ge(down_done, need[2 + g - 2])
                    sp.dma_start(dn_raw[:, g % 2], dn_w[g]).then_inc(dn_loaded, 16)
                sp.wait_ge(gu_loaded, 16 * EG)
                sp.wait_ge(dn_loaded, 16 * EG)

            @block.gpsimd
            def _(pool):
                def gather(t, q):
                    nc.gpsimd.tensor_copy(gather_ids[:, q], meta_ids[:, bass.ds(t, 1)]).then_inc(gather_ids_done, 1)
                    pool.wait_ge(gather_ids_done, t + 1)
                    pool.sem_inc(passed, 1)
                    nc.gpsimd.indirect_dma_start(out=x[:, q], out_offset=None, in_=h2_dram,
                                                 in_offset=bass.IndirectOffsetOnAxis(gather_ids[:, q], 0)
                                                 ).then_inc(x_loaded[q], 16)

                nc.gpsimd.memset(half[:], -0.5).then_inc(consts, 1)
                pool.wait_ge(consts, 1)
                pool.sem_inc(o_free, 2)
                gather(0, 0)

                def step(s, q, has_gu, has_dn, has_norm):
                    b = q % 2
                    if has_gu and not (isinstance(s, int) and s == T - 1):
                        if has_norm:
                            pool.wait_ge(residual, 2 * (s - 1))
                        gather(s + 1, (q + 1) % XR)
                    if has_norm:
                        t = s - 2
                        pool.wait_ge(stat_chain, 4 * t + 4)
                        nc.gpsimd.tensor_tensor(mv[:, 3:4], mv[:, 2:3], half[:], ALU.pow).then_inc(rstd_done, 1)
                        pool.wait_ge(rows_loaded, 32)
                        pool.wait_ge(normed, t + 1)
                        nc.gpsimd.tensor_tensor(o[:, b], o[:, b], g_row[:], ALU.mult).then_inc(scaled, 1)
                        nc.gpsimd.tensor_copy(store_ids[:, b], meta_ids[:, bass.ds(t, 1)]).then_inc(store_ids_done, 1)
                        pool.wait_ge(scaled, t + 1)
                        nc.gpsimd.tensor_tensor(o[:, b], o[:, b], b_row[:], ALU.add).then_inc(shifted, 1)
                        pool.wait_ge(store_ids_done, t + 1)
                        pool.wait_ge(shifted, t + 1)
                        pool.sem_inc(passed, 1)
                        nc.gpsimd.indirect_dma_start(out=out, out_offset=bass.IndirectOffsetOnAxis(store_ids[:, b], 0),
                                                     in_=o[:, b], in_offset=None, bounds_check=S - 1,
                                                     oob_is_err=False).then_inc(stored, 16)
                        pool.wait_ge(stored, 16 * t + 16)
                        pool.sem_inc(o_free, 1)

                steps(pool, step)

            @block.scalar
            def _(act):
                def high_part(s, i, group):
                    n = chunk(s, i)
                    act.wait_ge(gu_loaded, group * 16 + 16)
                    act.wait_ge(w_used, n + 1)
                    nc.scalar.copy(w_hi[:, i % RING], gu_raw[:, bass.ds(group % 2, 1), i
                                                             ].rearrange("p o n -> p (o n)")).then_inc(w_high, 1)

                def turned_x(t, b):
                    act.wait_ge(x_turned, t + 1)
                    nc.scalar.copy(xT_hi[:, b], xT[:]).then_inc(x_high, 1)

                def step(s, q, has_gu, has_dn, has_norm):
                    b = q % 2
                    if has_gu:
                        group = group_of(act, s)
                        for i in range(4):
                            high_part(s, i, group)
                    if has_dn:
                        act.wait_ge(h_turned, s)
                        act.wait_ge(down_done, s)
                        nc.scalar.copy(hT_sb[:], hT[:]).then_inc(h_copied, 1)
                    if has_gu:
                        for i in range(4, GUC):
                            high_part(s, i, group)
                        act.wait_ge(w_used, chunk(s, GUC - 1) + RING + 1)
                        if has_dn:
                            act.wait_ge(hid_done, s)
                        nc.scalar.activation(act_g[:], gu[:, 0], ACT.Silu).then_inc(gate_done, 1)
                        if not (isinstance(s, int) and s == T - 1):
                            turned_x(s + 1, 1 - b)

                turned_x(0, 0)
                steps(act, step)

            @block.tensor
            def _(pe):
                def turn_x(t, q):
                    pe.wait_ge(x_loaded[q], 16 * (t // XR + 1))
                    if not (isinstance(t, int) and t == 0):
                        pe.wait_ge(x_split, t)
                    for k in range(KT):
                        last = nc.tensor.transpose(xT[:, k], x[:, q, k * P:(k + 1) * P], ident[:])
                    last.then_inc(x_turned, 1)

                def gate_up(s, b, i):
                    pe.wait_ge(w_split, chunk(s, i) + 2)
                    r = i % RING
                    for c in range(2):
                        cols = slice(c * NT, (c + 1) * NT)
                        nc.tensor.matmul(gu[:, c], xT_hi[:, b, i], w_hi[:, r, cols], start=i == 0, stop=False)
                        nc.tensor.matmul(gu[:, c], xT_lo[:, b, i], w_hi[:, r, cols], start=False, stop=False)
                        last = nc.tensor.matmul(gu[:, c], xT_hi[:, b, i], w_lo[:, r, cols],
                                                start=False, stop=i == GUC - 1)
                    last.then_inc(w_used, 1)

                def step(s, q, has_gu, has_dn, has_norm):
                    b = q % 2
                    if has_gu:
                        pe.wait_ge(x_split, s + 1)
                        if has_dn:
                            pe.wait_ge(hid_done, s)
                        for i in range(2):
                            gate_up(s, b, i)
                    if has_dn:
                        pe.wait_ge(hid_done, s)
                        if has_norm:
                            pe.wait_ge(h_copied, s - 1)
                        for e in range(EG):
                            last = nc.tensor.transpose(hT[:, e], hid[:, e * FF:(e + 1) * FF], ident[:])
                        last.then_inc(h_turned, 1)
                    if has_gu:
                        for i in range(2, GUC):
                            gate_up(s, b, i)
                        if not (isinstance(s, int) and s == T - 1):
                            turn_x(s + 1, (q + 1) % XR)
                    if has_dn:
                        group = group_of(pe, s - 1)
                        pe.wait_ge(dn_loaded, group * 16 + 16)
                        pe.wait_ge(h_copied, s)
                        if has_norm:
                            pe.wait_ge(residual, 2 * s)
                        for e in range(EG):
                            for c in range(2):
                                w = dn_raw[:, bass.ds(group % 2, 1), e, c * NT:(c + 1) * NT]
                                last = nc.tensor.matmul(y[:, c], hT_sb[:, e], w.rearrange("p o n -> p (o n)"),
                                                        start=e == 0, stop=e == EG - 1)
                        last.then_inc(down_done, 1)

                pe.sem_inc(w_used, RING)
                pe.sem_inc(down_done, 1)
                turn_x(0, 0)
                steps(pe, step)

            @block.vector
            def _(dve):
                def low_part(s, i, group):
                    n = chunk(s, i)
                    dve.wait_ge(w_high, n + 1)
                    nc.vector.tensor_tensor(w_lo[:, i % RING], gu_raw[:, bass.ds(group % 2, 1), i
                                                                      ].rearrange("p o n -> p (o n)"),
                                            f32(w_hi[:, i % RING]), ALU.subtract).then_inc(w_split, 1)

                def x_low(t, b):
                    dve.wait_ge(x_high, t + 1)
                    nc.vector.tensor_tensor(xT_lo[:, b], xT[:], f32(xT_hi[:, b]), ALU.subtract).then_inc(x_split, 1)

                def step(s, q, has_gu, has_dn, has_norm):
                    b = q % 2

                    def low_parts(chunks):
                        if has_gu:
                            for i in chunks:
                                low_part(s, i, group)

                    if has_gu:
                        group = group_of(dve, s)
                    low_parts(range(4))
                    if has_norm:
                        t = s - 2
                        dve.wait_ge(down_done, t + 2)
                        dve.wait_ge(o_free, t + 1)
                        for c in range(2):
                            cols = slice(c * NT, (c + 1) * NT)
                            nc.vector.scalar_tensor_tensor(out=o[:, b, cols], in0=x[:, (q + 2) % XR, cols], scalar=ALPHA,
                                                           in1=y[:, c], op0=ALU.mult, op1=ALU.add
                                                           ).then_inc(residual, 1)
                        for c in range(2):
                            dve.wait_ge(residual, 2 * t + c + 3)
                            nc.vector.bn_stats(stats[:, 6 * c:6 * c + 6], o[:, b, c * NT:(c + 1) * NT]
                                               ).then_inc(stat_chain, 1)
                    low_parts(range(4, 5))
                    if has_norm:
                        dve.wait_ge(stat_chain, 4 * t + 2)
                        dve.sem_inc(passed, 1)
                        nc.vector.bn_aggr(mv[:, 0:2], stats[:]).then_inc(stat_chain, 1)
                        dve.wait_ge(stat_chain, 4 * t + 3)
                        nc.vector.tensor_scalar(mv[:, 2:3], mv[:, 1:2], EPS, None, ALU.add).then_inc(stat_chain, 1)
                    low_parts(range(5, 6))
                    if has_norm:
                        dve.wait_ge(rstd_done, t + 1)
                        nc.vector.tensor_scalar(o[:, b], o[:, b], mv[:, 0:1], mv[:, 3:4],
                                                ALU.subtract, ALU.mult).then_inc(normed, 1)
                    low_parts(range(6, GUC))
                    if has_gu:
                        dve.wait_ge(gate_done, s + 1)
                        if has_dn:
                            dve.wait_ge(h_turned, s)
                        for e in range(EG):
                            cols = slice(e * FF, (e + 1) * FF)
                            op = nc.vector.scalar_tensor_tensor(
                                out=hid[:, cols], in0=gu[:, 1, cols],
                                scalar=meta[:, bass.ds(s, 1), 1 + e:2 + e].rearrange("p o w -> p (o w)"),
                                in1=act_g[:, cols], op0=ALU.mult, op1=ALU.mult)
                        op.then_inc(hid_done, 1)
                        if not (isinstance(s, int) and s == T - 1):
                            x_low(s + 1, 1 - b)

                dve.sem_inc(w_split, 1)
                dve.sem_inc(residual, 2)
                x_low(0, 0)
                steps(dve, step)


def hybrid_decoder_layer(nc, x, ln_in_g, ln_in_b, w_in, b_gate, conv_w, sg_w, sg_b, sg_ln_g, sg_ln_b,
                         w_br, w_o, ln_mix_g, ln_mix_b, w_router, router_bias, gu_w, dn_w,
                         ln_ffn_g, ln_ffn_b, out):
    scratch = lambda name, shape: nc.dram_tensor(name, shape, F32).ap()
    h_dram = scratch("h_scratch", [S, D])
    projT = scratch("projT_scratch", [COLS, P, S])
    v_nat = scratch("v_scratch", [S, W])
    yT = scratch("yT_scratch", [P, 3 * W // P, S])
    mergedT = scratch("mergedT_scratch", [KT, P, S])
    h2_dram = scratch("h2_scratch", [S + P, D])
    order = scratch("order_scratch", [E_TILES * P, META])
    with ExitStack() as ctx:
        sems = {}

        def sem(name):
            if name not in sems:
                sems[name] = ctx.enter_context(nc.semaphore(name))
            return sems[name]

        ident = ctx.enter_context(nc.sbuf_tensor("ident", [P, P], F32))
        logits = ctx.enter_context(nc.sbuf_tensor("logits", [P, TILES, E], F32))
        with ExitStack() as phase:
            hT_hi = phase.enter_context(nc.sbuf_tensor("hT_hi", [P, KT, S], F32R))
            hT_lo = phase.enter_context(nc.sbuf_tensor("hT_lo", [P, KT, S], F32R))
            input_norm(nc, sem, x, ln_in_g, ln_in_b, h_dram, hT_hi, hT_lo, ident)
            project(nc, sem, w_in, projT, hT_hi, hT_lo)
            gates_and_local_mixers(nc, sem, w_in, b_gate, projT, hT_hi, hT_lo, conv_w, sg_w, sg_b, sg_ln_g, sg_ln_b,
                                   v_nat, yT, ident)
        attention(nc, sem, projT, v_nat, yT)
        with nc.sbuf_tensor("w_o_raw", [P, KT, D], F32) as w_o_raw:
            w_o_loaded = sem("w_o_loaded")
            merge_branches(nc, sem, projT, yT, w_br, mergedT, w_o, w_o_raw, w_o_loaded)
            mix_out(nc, sem, mergedT, w_o_raw, w_o_loaded, h_dram, ln_mix_g, ln_mix_b, w_router, h2_dram,
                    logits, ident)
        meta = ctx.enter_context(nc.sbuf_tensor("meta", [P, E_TILES, META], F32))
        table = ctx.enter_context(nc.sbuf_tensor("table", [1, E_TILES + EG], U32))
        gu_raw = ctx.enter_context(nc.sbuf_tensor("gu_raw", [P, 2, GUC, 2 * EG * FF], F32))
        dn_raw = ctx.enter_context(nc.sbuf_tensor("dn_raw", [P, 2, DNC, D], F32))
        gu_loaded, dn_loaded = sem("gu_loaded"), sem("dn_loaded")
        dispatch(nc, sem, logits, router_bias, order, meta, table, gu_w, dn_w, gu_raw, dn_raw, gu_loaded, dn_loaded)
        experts(nc, sem, h2_dram, meta, table, gu_w, dn_w, gu_raw, dn_raw, gu_loaded, dn_loaded,
                ln_ffn_g, ln_ffn_b, out, ident)


def kernel(**inputs):
    import numpy as np
    import concourse.bacc as bacc
    from concourse.bass_utils import run_bass_kernel_spmd

    w = {name: np.asarray(a) for name, a in inputs.items()}
    by_rows = lambda a: a.reshape(-1, P, a.shape[-1]).transpose(1, 0, 2)
    ffn_in = lambda a: a.reshape(EG, EG, KT, P, FF).transpose(0, 3, 2, 1, 4).reshape(EG, P, KT, EG * FF)
    arrays = {
        "x": w["x"].reshape(S, D),
        "ln_in_g": w["ln_in_g"],
        "ln_in_b": w["ln_in_b"],
        "w_in": w["w_in"].reshape(KT, P, COLS, P).transpose(2, 1, 0, 3).reshape(COLS, P, D),
        "b_gate": w["b_gate"].reshape(COLS - GATES, P).T,
        "conv_w": w["conv_w"].reshape(3, W // P, P).transpose(2, 1, 0),
        "sg_w": w["sg_w"][0].transpose(2, 0, 1),
        "sg_b": w["sg_b"][0],
        "sg_ln_g": w["sg_ln_g"][0],
        "sg_ln_b": w["sg_ln_b"][0],
        "w_br": by_rows(w["w_br"].reshape(3 * W, D)),
        "w_o": by_rows(w["w_o"][0]),
        "ln_mix_g": w["ln_mix_g"][0],
        "ln_mix_b": w["ln_mix_b"][0],
        "w_router": by_rows(w["w_router"]),
        "router_bias": w["router_bias"],
        "gu_w": np.concatenate([ffn_in(w["w_gate"][0]), ffn_in(w["w_up"][0])], axis=-1),
        "dn_w": w["w_down"].reshape(EG, EG, FF, D).transpose(0, 2, 1, 3),
        "ln_ffn_g": w["ln_ffn_g"][0],
        "ln_ffn_b": w["ln_ffn_b"][0],
    }
    arrays = {f"{name}_in": np.ascontiguousarray(a) for name, a in arrays.items()}
    nc = bacc.Bacc("TRN2", target_bir_lowering=False, num_devices=1)
    args = [nc.dram_tensor(name, a.shape, mybir.dt.from_np(a.dtype), kind="ExternalInput").ap()
            for name, a in arrays.items()]
    out = nc.dram_tensor("layer_out", (1, S, D), F32, kind="ExternalOutput").ap()
    hybrid_decoder_layer(nc, *args, out.rearrange("o s d -> (o s) d"))
    r = run_bass_kernel_spmd(nc, [arrays], core_ids=[0])
    return r.results[0]["layer_out"]
```

```python
from contextlib import ExitStack

import concourse.bass as bass
from concourse import mybir

ALU = mybir.AluOpType
ACT = mybir.ActivationFunctionType
AX_X = mybir.AxisListType.X
F32 = mybir.dt.float32
F32R = mybir.dt.float32r
U32 = mybir.dt.uint32

P = 128
D = 1024
KT = D // P
S = 2048
TILES = S // P
NT = 512
TT = S // NT
H, DH = 4, 64
G_C, CHUNK = 4, 128
W = 256
EPS = 1e-5
ALPHA = 2.0 ** 0.25

HA, BG, CG, Q, K, V, U_C, V_C, GATES = 0, 2, 4, 6, 8, 10, 12, 14, 16
COLS = 40


def f32(ap):
    return ap.bitcast(F32)


def load_weights(sp, w_tiles, w_raw, w_loaded, m, b):
    sp.dma_start(w_raw[:, b], w_tiles[bass.ds(m % COLS, 1)].rearrange("o p n -> p (o n)")).then_inc(w_loaded[b], 16)


def high_weights(nc, act, w_raw, w_hi, w_loaded, w_high, b, count):
    act.wait_ge(w_loaded[b], 16 * count)
    nc.scalar.copy(w_hi[:, b], w_raw[:, b]).then_inc(w_high, 1)


def low_weights(nc, dve, w_raw, w_hi, w_lo, w_high, w_split, b, m):
    dve.wait_ge(w_high, m + 1)
    nc.vector.tensor_tensor(w_lo[:, b], w_raw[:, b], f32(w_hi[:, b]), ALU.subtract).then_inc(w_split, 1)


def product_unit(nc, out, w_hi, w_lo, hT_hi, hT_lo, b, x, ks=range(KT)):
    for k in ks:
        w = slice(k * P, (k + 1) * P)
        nc.tensor.matmul(out, w_hi[:, b, w], hT_hi[:, k, x], start=k == 0, stop=False)
        nc.tensor.matmul(out, w_hi[:, b, w], hT_lo[:, k, x], start=False, stop=False)
        last = nc.tensor.matmul(out, w_lo[:, b, w], hT_hi[:, k, x], start=False, stop=k == KT - 1)
    return last


def norm_and_project(nc, sem, x, ln_g, ln_b, h_dram, w_tiles, w_raw, w_hi, w_lo, w_loaded, w_high, w_split,
                     projT, hT_hi, hT_lo, ident):
    EARLY = 2
    GT = NT // P
    with ExitStack() as ctx:
        sb = lambda n, s, dt=F32: ctx.enter_context(nc.sbuf_tensor(n, s, dt))
        ps = lambda n, s, dt=F32: ctx.enter_context(nc.psum_tensor(n, s, dt))
        xt = sb("np_x", [P, 2, D])
        hn = sb("np_h", [P, 2, D])
        g_row = sb("np_g", [P, D])
        b_row = sb("np_b", [P, D])
        ot = sb("np_out", [P, TT, NT])
        stats = sb("np_stats", [P, 2, 12])
        mv = sb("np_mv", [P, 2, 4])
        half = sb("np_half", [P, 1])
        acc = ps("np_acc", [P, TT, NT])
        tp = ps("np_tp", [P, 2, KT, P])
        rows_loaded = sem("np_rows_loaded")
        x_loaded = [sem(f"np_x_loaded{b}") for b in range(2)]
        consts = sem("np_consts")
        passed = sem("passed")
        stat_chain = sem("np_stat_chain")
        rstd_done = sem("np_rstd_done")
        normed = sem("np_normed")
        scaled = sem("np_scaled")
        h_done = sem("np_h_done")
        h_stored = [sem(f"np_h_stored{b}") for b in range(2)]
        turned = sem("np_turned")
        hi_done = sem("np_hi_done")
        lo_done = sem("np_lo_done")
        product_done = sem("np_product_done")
        evacuated = sem("np_evacuated")
        stored = [sem(f"np_stored{t}") for t in range(TT)]
        x_t = x.rearrange("(t p) d -> p t d", p=P)
        h_t = h_dram.rearrange("(t p) d -> p t d", p=P)
        rows = projT.rearrange("m p s -> p m s")
        flat = lambda a: a.rearrange("p o d -> p (o d)")

        def groups(eng, tile, early):
            for i in range(GT):
                tile(0, i)
            with eng.Fori(1, TILES // GT) as q:
                for i in range(GT):
                    tile(q, i)
                    if i >= GT - EARLY:
                        early(q - 1, i - (GT - EARLY))

        def uses(m, t):
            return m - EARLY + (TT if t < EARLY else 0)

        with nc.Block() as block:

            @block.sync
            def _(sp):
                def load_x(t, b):
                    sp.dma_start(xt[:, b], flat(x_t[:, bass.ds(t % TILES, 1)])).then_inc(x_loaded[b], 16)

                def tile(q, i):
                    t, b = GT * q + i, i % 2
                    sp.wait_ge(scaled, t + 1)
                    load_x(t + 2, b)
                    sp.wait_ge(h_done, t + 1)
                    sp.dma_start(flat(h_t[:, bass.ds(t, 1)]), hn[:, b]).then_inc(h_stored[b], 16)
                    if isinstance(t, int) and t < EARLY:
                        sp.wait_ge(w_split, t + 1)
                        load_weights(sp, w_tiles, w_raw, w_loaded, t + 2, b)

                def early(q, m):
                    sp.wait_ge(evacuated, EARLY * q + m + 1 + EARLY)
                    sp.dma_start(rows[:, m, bass.ds(q * NT, NT)], ot[:, m]).then_inc(stored[m], 16)

                load_x(0, 0)
                load_x(1, 1)
                sp.dma_start(g_row[:], ln_g.partition_broadcast(P)).then_inc(rows_loaded, 16)
                sp.dma_start(b_row[:], ln_b.partition_broadcast(P)).then_inc(rows_loaded, 16)
                for b in range(2):
                    load_weights(sp, w_tiles, w_raw, w_loaded, b, b)
                    sp.sem_inc(h_stored[b], 16)
                for t in range(TT):
                    sp.sem_inc(stored[t], 16)
                groups(sp, tile, early)
                for m in range(EARLY):
                    early(TT - 1, m)
                with sp.Fori(EARLY // 2, GATES // 2) as j:
                    for b in range(2):
                        m = 2 * j + b
                        sp.wait_ge(w_split, m + 1)
                        load_weights(sp, w_tiles, w_raw, w_loaded, m + 2, b)
                        for t in range(TT):
                            sp.wait_ge(evacuated, TT * m + t + 1 + EARLY)
                            sp.dma_start(flat(rows[:, bass.ds(m, 1), t * NT:(t + 1) * NT]), ot[:, t]
                                         ).then_inc(stored[t], 16)
                for t in range(TT):
                    sp.wait_ge(stored[t], 16 * (uses(GATES, t) + 1))
                for b in range(2):
                    sp.wait_ge(h_stored[b], 16 * (TILES // 2 + 1))
                    sp.wait_ge(x_loaded[b], 16 * (TILES // 2 + 1))

            @block.gpsimd
            def _(pool):
                nc.gpsimd.memset(ident[:], 0.0).then_inc(consts, 1)
                pool.wait_ge(consts, 1)
                nc.gpsimd.affine_select(out=ident[:], in_=ident[:], compare_op=ALU.not_equal, fill=1.0, base=0,
                                        pattern=[[-1, P]], channel_multiplier=1).then_inc(consts, 1)
                nc.gpsimd.memset(half[:], -0.5).then_inc(consts, 1)
                pool.wait_ge(consts, 3)

                def tile(q, i):
                    t, b = GT * q + i, i % 2
                    pool.wait_ge(stat_chain, 4 * t + 4)
                    nc.gpsimd.tensor_tensor(mv[:, b, 3:4], mv[:, b, 2:3], half[:], ALU.pow).then_inc(rstd_done, 1)
                    pool.wait_ge(h_stored[b], 16 * (GT // 2 * q + i // 2) + 16)
                    pool.wait_ge(turned, t + 1)
                    pool.wait_ge(rows_loaded, 32)
                    pool.wait_ge(normed, t + 1)
                    nc.gpsimd.tensor_tensor(hn[:, b], xt[:, b], g_row[:], ALU.mult).then_inc(scaled, 1)

                groups(pool, tile, lambda q, m: None)

            @block.scalar
            def _(act):
                def high_w(b, count):
                    high_weights(nc, act, w_raw, w_hi, w_loaded, w_high, b, count)

                def evacuate(slot, count, before):
                    act.wait_ge(stored[slot], 16 * before + 16)
                    act.wait_ge(product_done, count)
                    nc.scalar.copy(ot[:, slot], acc[:, slot]).then_inc(evacuated, 1)

                def tile(q, i):
                    t, b = GT * q + i, i % 2
                    act.wait_ge(turned, t + 1 + 2)
                    act.sem_inc(passed, 1)
                    nc.scalar.copy(hT_hi[:, :, bass.ds(t * P, P)], tp[:, b]).then_inc(hi_done, 1)

                def early(q, m):
                    evacuate(m, EARLY * q + m + 1, q)

                act.sem_inc(evacuated, EARLY)
                high_w(0, 1)
                high_w(1, 1)
                groups(act, tile, early)
                early(TT - 1, 0)
                high_w(0, 2)
                early(TT - 1, 1)
                with act.Fori(EARLY // 2, GATES // 2) as j:
                    for b in range(2):
                        m = 2 * j + b
                        high_w(1 - b, j + 1 + b)
                        for t in range(TT):
                            evacuate(t, TT * m + t + 1, uses(m, t))

            @block.vector
            def _(dve):
                def low_w(b, m):
                    low_weights(nc, dve, w_raw, w_hi, w_lo, w_high, w_split, b, m)

                def shift(t, b):
                    dve.wait_ge(rows_loaded, 32)
                    dve.wait_ge(scaled, t + 1)
                    nc.vector.tensor_tensor(hn[:, b], hn[:, b], b_row[:], ALU.add).then_inc(h_done, 1)

                def low_part(t, b):
                    dve.wait_ge(hi_done, t + 1)
                    cols = bass.ds(t * P, P)
                    nc.vector.tensor_tensor(hT_lo[:, :, cols], tp[:, b], f32(hT_hi[:, :, cols]),
                                            ALU.subtract).then_inc(lo_done, 1)

                def tile(q, i):
                    t, b = GT * q + i, i % 2
                    dve.wait_ge(x_loaded[b], 16 * (GT // 2 * q + i // 2 + 1))
                    for c in range(2):
                        nc.vector.bn_stats(stats[:, b, 6 * c:6 * c + 6], xt[:, b, NT * c:NT * c + NT]
                                           ).then_inc(stat_chain, 1)
                    dve.wait_ge(stat_chain, 4 * t + 2)
                    dve.sem_inc(passed, 1)
                    nc.vector.bn_aggr(mv[:, b, 0:2], stats[:, b]).then_inc(stat_chain, 1)
                    dve.wait_ge(stat_chain, 4 * t + 3)
                    nc.vector.tensor_scalar(mv[:, b, 2:3], mv[:, b, 1:2], EPS, None, ALU.add).then_inc(stat_chain, 1)
                    if not (isinstance(t, int) and t < 1):
                        shift(t - 1, 1 - b)
                    dve.wait_ge(rstd_done, t + 1)
                    nc.vector.tensor_scalar(xt[:, b], xt[:, b], mv[:, b, 0:1], mv[:, b, 3:4],
                                            ALU.subtract, ALU.mult).then_inc(normed, 1)
                    if isinstance(t, int) and t < EARLY:
                        low_w(b, t)
                    else:
                        low_part(t - 2, b)

                dve.sem_inc(lo_done, 2)
                groups(dve, tile, lambda q, m: None)
                shift(TILES - 1, 1)
                low_part(TILES - 2, 0)
                low_part(TILES - 1, 1)
                low_w(0, EARLY)
                with dve.Fori(EARLY // 2, GATES // 2) as j:
                    for b in range(2):
                        low_w(1 - b, 2 * j + b + 1)

            @block.tensor
            def _(pe):
                def turn(q, i):
                    t, b = GT * q + i, i % 2
                    pe.wait_ge(lo_done, t + 1)
                    pe.wait_ge(h_done, t + 1)
                    for k in range(KT):
                        last = nc.tensor.transpose(tp[:, b, k], hn[:, b, k * P:(k + 1) * P], ident[:])
                    last.then_inc(turned, 1)

                def early_half(q, m, half):
                    if half == 0:
                        pe.wait_ge(lo_done, GT * q + GT + 2)
                        pe.wait_ge(evacuated, EARLY * q + m + 1)
                    last = product_unit(nc, acc[:, m], w_hi, w_lo, hT_hi, hT_lo, m, bass.ds(q * NT, NT),
                                        range(KT // 2 * half, KT // 2 * (half + 1)))
                    if half == 1:
                        last.then_inc(product_done, 1)

                pe.sem_inc(turned, 2)
                pe.wait_ge(consts, 2)
                for i in range(GT):
                    turn(0, i)
                pe.wait_ge(w_split, EARLY)
                with pe.Fori(1, TT) as q:
                    for i in range(GT):
                        turn(q, i)
                        early_half(q - 1, i // 2, i % 2)
                for i in range(GT):
                    early_half(TT - 1, i // 2, i % 2)
                pe.wait_ge(evacuated, EARLY * TT + EARLY)
                with pe.Fori(EARLY // 2, GATES // 2) as j:
                    for b in range(2):
                        m = 2 * j + b
                        pe.wait_ge(w_split, m + 1)
                        for t in range(TT):
                            pe.wait_ge(evacuated, TT * m + t + 1 - TT + EARLY)
                            product_unit(nc, acc[:, t], w_hi, w_lo, hT_hi, hT_lo, b, slice(t * NT, (t + 1) * NT)
                                         ).then_inc(product_done, 1)


def gates_and_local_mixers(nc, sem, w_tiles, w_raw, w_hi, w_lo, w_loaded, w_high, w_split, b_gate, projT,
                           hT_hi, hT_lo, conv_w, sg_w, sg_b, sg_g, sg_bb,
                           v_nat, yT, ident):
    N_GATES = COLS - GATES
    PER = N_GATES // TT
    CH = NT // CHUNK
    HALO = 2
    with ExitStack() as ctx:
        sb = lambda n, s, dt=F32: ctx.enter_context(nc.sbuf_tensor(n, s, dt))
        ps = lambda n, s, dt=F32: ctx.enter_context(nc.psum_tensor(n, s, dt))
        ot = sb("gm_out", [P, TT, NT])
        bg = sb("gm_b_gate", [P, N_GATES])
        conv_u = sb("gm_conv_u", [P, 2, HALO + NT])
        conv_c = sb("gm_conv_c", [P, 2, NT])
        conv_b = sb("gm_conv_b", [P, 2, NT])
        vT = sb("gm_vT", [P, 2, NT])
        uT = sb("gm_uT", [P, 2, NT])
        vcT = sb("gm_vcT", [P, 2, NT])
        cw = sb("gm_cw", [P, 2, 3])
        wsT = sb("gm_wsT", [P, G_C, CHUNK])
        bias = sb("gm_bias", [P, 2, CHUNK])
        g_row = sb("gm_g", [P, W])
        b_row = sb("gm_b", [P, W])
        half = sb("gm_half", [P, 1])
        stats = sb("gm_stats", [P, 6])
        mv = sb("gm_mv", [P, 4])
        vn = sb("gm_vn", [P, W])
        vs = sb("gm_v", [P, W])
        fb = sb("gm_fb", [P, 2, CHUNK])
        acc = ps("gm_acc", [P, TT, NT])
        vc_ps = ps("gm_vc_ps", [P, 4, P])
        v_ps = ps("gm_v_ps", [P, 4, P])
        fT = ps("gm_fT", [P, 4, P])
        small_loaded = sem("gm_small_loaded")
        passed = sem("passed")
        product_done = sem("gm_product_done")
        evacuated = sem("gm_evacuated")
        stored = [sem(f"gm_stored{t}") for t in range(TT)]
        v_loaded = sem("gm_v_loaded")
        u_loaded = sem("gm_u_loaded")
        conv_loaded = sem("gm_conv_loaded")
        consts = sem("gm_consts")
        gelu_done = sem("gm_gelu_done")
        turned = sem("gm_turned")
        stat_chain = sem("gm_stat_chain")
        rstd_done = sem("gm_rstd_done")
        normed = sem("gm_normed")
        scaled = sem("gm_scaled")
        vn_done = sem("gm_vn_done")
        v_copied = sem("gm_v_copied")
        v_stored = sem("gm_v_stored")
        mixed = sem("gm_mixed")
        biased = sem("gm_biased")
        yc_done = sem("gm_yc_done")
        conv_chain = sem("gm_conv_chain")
        y_stored = sem("gm_y_stored")
        CONV_STEPS = 9
        rows = projT.rearrange("m p s -> p m s")
        v_t = v_nat.rearrange("(n p) c -> p n c", p=P)

        with nc.Block() as block:

            @block.sync
            def _(sp):
                sp.dma_start(bg[:], b_gate).then_inc(small_loaded, 16)
                sp.dma_start(wsT[:], sg_w).then_inc(small_loaded, 16)
                for g in range(G_C):
                    sp.dma_start(bias[64 * (g % 2):64 * (g % 2) + 64, g // 2], sg_b[g].partition_broadcast(64)
                                 ).then_inc(small_loaded, 16)
                sp.dma_start(g_row[:], sg_g.partition_broadcast(P)).then_inc(small_loaded, 16)
                sp.dma_start(b_row[:], sg_bb.partition_broadcast(P)).then_inc(small_loaded, 16)
                sp.dma_start(cw[:], conv_w).then_inc(small_loaded, 16)
                for t in range(TT):
                    sp.sem_inc(stored[t], 16)
                sp.sem_inc(v_stored, 16)
                sp.sem_inc(y_stored, 16)
                with sp.Fori(0, TT) as q:
                    block_cols = bass.ds(q * NT, NT)
                    sp.wait_ge(turned, CH * q + 1)
                    sp.wait_ge(y_stored, 32 * q + 16)
                    for x, m, s in ((vcT[:], V_C, v_loaded), (vT[:], V, v_loaded),
                                    (conv_u[:, :, HALO:], HA, conv_loaded), (conv_c[:], CG, conv_loaded),
                                    (conv_b[:], BG, conv_loaded), (uT[:], U_C, u_loaded)):
                        sp.dma_start(x, rows[:, m:m + 2, block_cols]).then_inc(s, 16)
                    for i in range(PER):
                        g, b = PER * q + i, i % 2
                        sp.wait_ge(w_split, GATES + g + 1)
                        load_weights(sp, w_tiles, w_raw, w_loaded, GATES + g + 2, b)
                        for t in range(TT):
                            sp.wait_ge(evacuated, TT * g + t + 1 + TT)
                            sp.dma_start(rows[:, bass.ds(GATES + g, 1), t * NT:(t + 1) * NT
                                              ].rearrange("p o s -> p (o s)"), ot[:, t]).then_inc(stored[t], 16)
                        if 1 <= i <= CH:
                            chunk = CH * q + i - 1
                            sp.wait_ge(v_copied, chunk + 2)
                            sp.dma_start(v_t[:, bass.ds(chunk, 1)].rearrange("p o c -> p (o c)"), vs[:]
                                         ).then_inc(v_stored, 16)
                        if i == 1:
                            sp.wait_ge(conv_chain, CONV_STEPS * (q + 1))
                            sp.dma_start(yT[:, 0:2, block_cols], conv_c[:]).then_inc(y_stored, 16)
                        if i == PER - 1:
                            sp.wait_ge(yc_done, CH * (q + 1))
                            sp.dma_start(yT[:, 4:6, block_cols], uT[:]).then_inc(y_stored, 16)
                for b in range(2):
                    sp.wait_ge(w_loaded[b], 16 * (COLS // 2 + 1))
                for t in range(TT):
                    sp.wait_ge(stored[t], 16 * (N_GATES + 1))
                sp.wait_ge(v_stored, 16 * (CH * TT + 1))
                sp.wait_ge(y_stored, 16 * (2 * TT + 1))

            @block.gpsimd
            def _(pool):
                nc.gpsimd.memset(half[:], -0.5).then_inc(consts, 1)
                nc.gpsimd.memset(conv_u[:, :, 0:HALO], 0.0).then_inc(consts, 1)
                pool.wait_ge(small_loaded, 9 * 16)
                nc.gpsimd.affine_select(out=wsT[:], in_=wsT[:], compare_op=ALU.is_ge, fill=0.0, base=0,
                                        pattern=[[0, G_C], [1, CHUNK]], channel_multiplier=-1
                                        ).then_inc(consts, 1)
                pool.wait_ge(consts, 2)
                with pool.Fori(0, TT) as q:
                    for k in range(CH):
                        chunk = CH * q + k
                        pool.wait_ge(stat_chain, 3 * chunk + 3)
                        nc.gpsimd.tensor_tensor(mv[:, 3:4], mv[:, 2:3], half[:], ALU.pow).then_inc(rstd_done, 1)
                        pool.wait_ge(normed, chunk + 2)
                        nc.gpsimd.tensor_tensor(vn[:], vn[:], g_row[:], ALU.mult).then_inc(scaled, 1)
                        pool.wait_ge(scaled, chunk + 1)
                        nc.gpsimd.tensor_tensor(vn[:], vn[:], b_row[:], ALU.add).then_inc(vn_done, 1)

            @block.scalar
            def _(act):
                act.sem_inc(evacuated, TT)
                act.sem_inc(v_copied, 1)
                act.wait_ge(small_loaded, 9 * 16)
                with act.Fori(0, TT) as q:
                    for i in range(PER):
                        g = PER * q + i
                        high_weights(nc, act, w_raw, w_hi, w_loaded, w_high, (i + 1) % 2,
                                     GATES // 2 + PER // 2 * q + (i + 1) // 2 + 1)
                        for t in range(TT):
                            act.wait_ge(stored[t], 16 * g + 16)
                            act.wait_ge(product_done, TT * g + t + 1)
                            act.sem_inc(passed, 1)
                            nc.scalar.activation(ot[:, t], acc[:, t], ACT.Sigmoid, bias=bg[:, bass.ds(g, 1)]
                                                 ).then_inc(evacuated, 1)
                            if i == 0 and t == TT - 2:
                                act.wait_ge(v_loaded, 32 * q + 32)
                                nc.scalar.activation(vcT[:], vcT[:], ACT.Gelu_apprx_tanh).then_inc(gelu_done, 1)
                                act.wait_ge(u_loaded, 16 * q + 16)
                                nc.scalar.activation(uT[:], uT[:], ACT.Gelu_apprx_tanh).then_inc(gelu_done, 1)
                        if 1 <= i <= CH:
                            chunk = CH * q + i - 1
                            act.wait_ge(v_stored, 16 * chunk + 16)
                            act.wait_ge(turned, chunk + 2)
                            nc.scalar.copy(vs[:], v_ps[:, 0:2].rearrange("p c t -> p (c t)")).then_inc(v_copied, 1)

            @block.tensor
            def _(pe):
                pe.sem_inc(turned, 1)
                pe.sem_inc(mixed, 1)
                with pe.Fori(0, TT) as q:
                    for i in range(PER):
                        g, b = PER * q + i, i % 2
                        if i >= 2:
                            chunk = CH * q + i - 2
                            pe.wait_ge(biased, chunk + 1)
                            pe.wait_ge(consts, 3)
                            pe.wait_ge(vn_done, chunk + 1)
                            for gr in range(G_C):
                                r = 64 * (gr % 2)
                                last = nc.tensor.matmul(fT[r:r + 64, gr // 2], vn[:, gr * 64:(gr + 1) * 64],
                                                        wsT[:, gr], start=True, stop=True)
                            last.then_inc(mixed, 1)
                        if 1 <= i <= CH:
                            k = i - 1
                            chunk = CH * q + k
                            pe.wait_ge(gelu_done, 2 * q + 1)
                            pe.wait_ge(v_copied, chunk + 1)
                            pe.wait_ge(normed, chunk + 1)
                            cols = slice(k * CHUNK, (k + 1) * CHUNK)
                            for c in range(2):
                                nc.tensor.transpose(vc_ps[:, c], vcT[:, c, cols], ident[:])
                                last = nc.tensor.transpose(v_ps[:, c], vT[:, c, cols], ident[:])
                            last.then_inc(turned, 1)
                        pe.wait_ge(w_split, GATES + g + 1)
                        for t in range(TT):
                            pe.wait_ge(evacuated, TT * g + t + 1)
                            product_unit(nc, acc[:, t], w_hi, w_lo, hT_hi, hT_lo, b, slice(t * NT, (t + 1) * NT)
                                         ).then_inc(product_done, 1)

            @block.vector
            def _(dve):
                def convolve(q):
                    step = [0]

                    def chained(op):
                        step[0] += 1
                        op.then_inc(conv_chain, 1)
                        dve.wait_ge(conv_chain, CONV_STEPS * q + step[0])

                    u = conv_u[:, :, HALO:]
                    dve.wait_ge(conv_loaded, 48 * q + 48)
                    chained(nc.vector.tensor_tensor(u, conv_c[:], u, ALU.mult))
                    for tap in range(3):
                        for c in range(2):
                            y, x = conv_c[:, c], conv_u[:, c, tap:tap + NT]
                            if tap == 0:
                                op = nc.vector.tensor_scalar(y, x, cw[:, c, 0:1], None, ALU.mult)
                            else:
                                op = nc.vector.scalar_tensor_tensor(out=y, in0=x, scalar=cw[:, c, tap:tap + 1],
                                                                    in1=y, op0=ALU.mult, op1=ALU.add)
                            chained(op)
                    chained(nc.vector.tensor_tensor(conv_c[:], conv_c[:], conv_b[:], ALU.mult))
                    chained(nc.vector.tensor_copy(conv_u[:, :, 0:HALO], conv_u[:, :, NT:NT + HALO]))

                def gate(q, k):
                    chunk = CH * q + k
                    dve.wait_ge(mixed, chunk + 2)
                    nc.vector.tensor_tensor(fb[:], fT[:, 0:2], bias[:], ALU.add).then_inc(biased, 1)
                    dve.wait_ge(biased, chunk + 2)
                    dve.wait_ge(gelu_done, 2 * q + 2)
                    u = uT[:, :, k * CHUNK:(k + 1) * CHUNK]
                    nc.vector.tensor_tensor(u, u, fb[:], ALU.mult).then_inc(yc_done, 1)

                def normalise(q, k):
                    chunk = CH * q + k
                    vc = vc_ps[:, 0:2].rearrange("p c t -> p (c t)")
                    dve.wait_ge(turned, chunk + 2)
                    nc.vector.bn_stats(stats[:], vc).then_inc(stat_chain, 1)
                    dve.wait_ge(stat_chain, 3 * chunk + 1)
                    dve.sem_inc(passed, 1)
                    nc.vector.bn_aggr(mv[:, 0:2], stats[:]).then_inc(stat_chain, 1)
                    dve.wait_ge(stat_chain, 3 * chunk + 2)
                    nc.vector.tensor_scalar(mv[:, 2:3], mv[:, 1:2], EPS, None, ALU.add).then_inc(stat_chain, 1)
                    dve.wait_ge(rstd_done, chunk + 1)
                    dve.wait_ge(mixed, chunk + 1)
                    nc.vector.tensor_scalar(vn[:], vc, mv[:, 0:1], mv[:, 3:4], ALU.subtract, ALU.mult
                                            ).then_inc(normed, 1)

                dve.sem_inc(normed, 1)
                dve.sem_inc(biased, 1)
                dve.wait_ge(small_loaded, 9 * 16)
                dve.wait_ge(consts, 2)
                with dve.Fori(0, TT) as q:
                    for i in range(PER):
                        low_weights(nc, dve, w_raw, w_hi, w_lo, w_high, w_split, (i + 1) % 2,
                                    GATES + PER * q + i + 1)
                        if i == 0:
                            convolve(q)
                        if i >= 2:
                            gate(q, i - 2)
                        if 1 <= i <= CH:
                            normalise(q, i - 1)



def attention(nc, sem, projT, v_nat, yT, w_br, w_br_raw, w_br_loaded):
    SCALE = DH ** -0.5
    R = 8
    RS = 4
    RZ = 4
    HEADS = 2
    SP_CAP = 44.0

    LN, SP, HI, LO, OWN, SUM, REST, EXP, MASK, AV, OUT = 1, 2, 3, 3, 4, 5, 6, 6, 7, 8, 9

    chain = [[], []]
    for c, tiles in enumerate(((3, 0), (2, 1))):
        for qt in tiles:
            blocks = list(range(4 * qt + 3, -1, -1))
            for kb in blocks:
                d = kb - 4 * qt
                chain[c].append((c, qt, kb, d, min(P * max(d, 0), NT // 2), kb == blocks[0], kb == 0))
    head_items = [x for pair in zip(*chain) for x in pair]
    PER_HEAD = len(head_items)
    items = [(s,) + x for s in range(HEADS) for x in head_items]
    N = len(items)

    with ExitStack() as ctx:
        sb = lambda n, s, dt=F32: ctx.enter_context(nc.sbuf_tensor(n, s, dt))
        ps = lambda n, s, dt=F32: ctx.enter_context(nc.psum_tensor(n, s, dt))
        q_raw = sb("at_q_raw", [P, S])
        k_raw = sb("at_k_raw", [P, S])
        q_hi = sb("at_q_hi", [P, HEADS, S], F32R)
        q_lo = sb("at_q_lo", [P, HEADS, S], F32R)
        k_st = sb("at_k", [P, HEADS, S], F32R)
        v_sb = sb("at_v", [P, HEADS, TILES, DH])
        neg_own = sb("at_neg_own", [P, P], F32R)
        neg_rest = sb("at_neg_rest", [P, P], F32R)
        z_sb = sb("at_z", [P, R, NT])
        e_sb = sb("at_e", [P, RS, NT])
        sp_sb = sb("at_sp", [P, R, NT])
        sp_hi = sb("at_sp_hi", [P, R, NT], F32R)
        sp_lo = sb("at_sp_lo", [P, R, NT], F32R)
        t_sb = sb("at_t", [P, RS, NT])
        a_sb = sb("at_a", [P, RS, NT])
        y_sb = sb("at_y", [DH, 2, NT])
        z_ps = ps("at_z_ps", [P, RZ, NT])
        sum_ps = ps("at_sum_ps", [P, 2, NT])
        y_ps = ps("at_y_ps", [P, 2, NT])

        consts = sem("at_consts")
        passed = sem("passed")
        q_loaded = sem("at_q_loaded")
        k_loaded = sem("at_k_loaded")
        v_loaded = sem("at_v_loaded")
        prep = sem("at_prep")
        z_done = sem("at_z_done")
        z_copied = sem("at_z_copied")
        e_done = sem("at_e_done")
        l_done = sem("at_l_done")
        sp_done = sem("at_sp_done")
        masked = sem("at_masked")
        hi_done = sem("at_hi_done")
        lo_done = sem("at_lo_done")
        own_done = sem("at_own_done")
        t_done = sem("at_t_done")
        rest_done = sem("at_rest_done")
        a_done = sem("at_a_done")
        a_masked = sem("at_a_masked")
        av_done = sem("at_av_done")
        y_done = sem("at_y_done")
        y_stored = [sem(f"at_y_stored{c}") for c in range(2)]

        proj_rows = projT.rearrange("m p s -> (m p) s")
        v_heads = v_nat.rearrange("(n p) (h d) -> p n h d", p=P, d=DH)
        y_heads = yT[:, 2:4].rearrange("(r p) m s -> m r p s", p=DH)
        diag_before = [sum(1 for x in items[:n] if x[4] >= 0) for n in range(N + 1)]
        last_before = [sum(1 for x in items[:n] if x[7]) for n in range(N + 1)]
        DIAG, LASTS = diag_before[N], last_before[N]
        lasts = [n for n in range(N) if items[n][7]]
        chain_tile = lambda n: sum(1 for m in lasts if m < n and items[m][1] == items[n][1])

        def tile_before(n):
            own = [x for x, m in enumerate(lasts) if items[m][1] == items[n][1]]
            k = chain_tile(n)
            return own[k - 1] if k else own[-1] - LASTS

        PARTS = S // NT
        PREP = 4 * PARTS

        ringed = dict(act=(z_copied, e_done, l_done, a_done, y_done), dve=(sp_done, hi_done, t_done),
                      pe=(z_done, own_done, av_done))
        done = lambda n: R + n + 1
        freed = lambda n: n + 1

        with nc.Block() as block:

            @block.sync
            def _(sp):
                def load(h, slot, first):
                    for half in range(2):
                        r = slice(half * DH, half * DH + DH)
                        sp.dma_start(q_raw[r], proj_rows[bass.ds(Q * P + h * DH, DH)]).then_inc(q_loaded, 16)
                        sp.dma_start(k_raw[r], proj_rows[bass.ds(K * P + h * DH, DH)]).then_inc(k_loaded, 16)
                    sp.dma_start(v_sb[:, slot], v_heads[:, :, bass.ds(h, 1)].rearrange("p n o d -> p n (o d)")
                                 ).then_inc(v_loaded, 16)

                def store(n, count, pair):
                    slot, c, qt = items[n][0:3]
                    sp.wait_ge(y_done, count)
                    sp.dma_start(y_heads[bass.ds(pair, 1), slot, :, qt * NT:(qt + 1) * NT
                                         ].rearrange("o p s -> p (o s)"), y_sb[:, c]).then_inc(y_stored[c], 16)

                for c in range(2):
                    sp.sem_inc(y_stored[c], 16)
                load(0, 0, True)
                sp.dma_start(w_br_raw[:], w_br).then_inc(w_br_loaded, 16)
                with sp.Fori(0, H // HEADS) as j:
                    sp.wait_ge(prep, PREP * (HEADS * j + 1))
                    load(HEADS * j + 1, 1, False)
                    for x, n in enumerate(lasts):
                        if x == LASTS // 2:
                            sp.wait_ge(prep, PREP * (HEADS * j + 2))
                            load((HEADS * j + 2) % H, 0, False)
                        store(n, j * LASTS + done(x), j)
                sp.wait_ge(w_br_loaded, 16)
                for c in range(2):
                    sp.wait_ge(y_stored[c], 16 * (H // HEADS) * (LASTS // 2) + 16)

            @block.gpsimd
            def _(pool):
                nc.gpsimd.memset(e_sb[:, 0, 0:P], -1.0).then_inc(consts, 1)
                pool.wait_ge(consts, 1)
                nc.gpsimd.affine_select(out=z_sb[:, 0, 0:P], in_=e_sb[:, 0, 0:P], compare_op=ALU.is_ge, fill=0.0,
                                        base=0, pattern=[[-1, P]], channel_multiplier=1).then_inc(consts, 1)
                nc.gpsimd.affine_select(out=z_sb[:, 0, P:2 * P], in_=e_sb[:, 0, 0:P], compare_op=ALU.is_gt, fill=0.0,
                                        base=0, pattern=[[1, P]], channel_multiplier=-1).then_inc(consts, 1)

                def causal(tile, d, c0):
                    return nc.gpsimd.affine_select(out=tile, in_=tile, compare_op=ALU.is_gt, fill=0.0,
                                                   base=c0 - d * P, pattern=[[1, NT - c0]], channel_multiplier=-1)

                pool.sem_inc(lo_done, R)
                with pool.Fori(0, H // HEADS) as j:
                    for s in range(N + MASK):
                        if LO <= s < N + LO:
                            n = s - LO
                            c0 = items[n][5]
                            pool.wait_ge(hi_done, j * N + done(n))
                            nc.gpsimd.tensor_tensor(sp_lo[:, n % R, c0:NT], sp_sb[:, n % R, c0:NT],
                                                    f32(sp_hi[:, n % R, c0:NT]), ALU.subtract).then_inc(lo_done, 1)
                        if SP <= s < N + SP:
                            n = s - SP
                            slot, c, qt, kb, d, c0, first, last = items[n]
                            tile = sp_sb[:, n % R, c0:NT]
                            if d >= 0:
                                pool.wait_ge(sp_done, j * N + done(n))
                                pool.sem_inc(passed, 1)
                                causal(tile, d, c0).then_inc(masked, 1)
                        if MASK <= s + 1 < N + MASK and items[s + 1 - MASK][4] >= 0:
                            n = s + 1 - MASK
                            slot, c, qt, kb, d, c0, first, last = items[n]
                            pool.wait_ge(a_done, j * N + done(n))
                            pool.sem_inc(passed, 1)
                            causal(a_sb[:, n % RS, c0:NT], d, c0).then_inc(a_masked, 1)

            @block.scalar
            def _(act):
                for s in ringed["act"]:
                    act.sem_inc(s, R)
                nc.scalar.preload_act_table_set("natural_log_exp_and_others")
                act.wait_ge(consts, 5)
                with act.Fori(0, H // HEADS) as j:
                    for s in range(N + OUT):
                        if s < N:
                            n = s
                            c0 = items[n][5]
                            z = z_ps[:, n % RZ, c0:NT]
                            act.wait_ge(z_done, j * N + done(n))
                            act.wait_ge(t_done, j * N + freed(n))
                            nc.scalar.copy(z_sb[:, n % R, c0:NT], z).then_inc(z_copied, 1)
                        if LN <= s < N + LN:
                            n = s - LN
                            e = e_sb[:, n % RS, items[n][5]:NT]
                            act.wait_ge(e_done, j * N + done(n))
                            nc.scalar.activation(e, e, ACT.Ln, bias=1.0).then_inc(l_done, 1)
                        if s < N:
                            n = s
                            c0 = items[n][5]
                            act.wait_ge(sp_done, j * N + done(n - RS))
                            nc.scalar.activation(e_sb[:, n % RS, c0:NT], z_ps[:, n % RZ, c0:NT], ACT.Exp
                                                 ).then_inc(e_done, 1)
                        if EXP <= s < N + EXP:
                            n = s - EXP
                            c0 = items[n][5]
                            act.wait_ge(t_done, j * N + done(n))
                            act.wait_ge(av_done, j * N + done(n - RS))
                            nc.scalar.activation(a_sb[:, n % RS, c0:NT], t_sb[:, n % RS, c0:NT], ACT.Exp
                                                 ).then_inc(a_done, 1)
                        if s >= OUT and items[s - OUT][7]:
                            n = s - OUT
                            c = items[n][1]
                            act.wait_ge(av_done, j * N + done(n))
                            act.wait_ge(y_stored[c], 16 * (j * (LASTS // 2) + chain_tile(n) + 1))
                            nc.scalar.copy(y_sb[:, c], y_ps[0:DH, c]).then_inc(y_done, 1)

            @block.tensor
            def _(pe):
                for s in ringed["pe"]:
                    pe.sem_inc(s, R)
                pe.sem_inc(rest_done, R)
                pe.wait_ge(consts, 5)
                parts_seen = [PARTS]
                with pe.Fori(0, H // HEADS) as j:
                    for s in range(-1, N + AV):
                        if s + 1 < N:
                            n = s + 1
                            slot, c, qt, kb, d, c0, first, last = items[n]
                            if n % PER_HEAD == 0 or kb // PARTS < parts_seen[0]:
                                parts_seen[0] = kb // PARTS
                                pe.wait_ge(prep, PREP * (HEADS * j + slot) + 4 * (PARTS - kb // PARTS))
                            pe.wait_ge(e_done, j * N + done(n - RZ))
                            qs = slice(qt * NT + c0, (qt + 1) * NT)
                            out = z_ps[:, n % RZ, c0:NT]
                            kw = k_st[:, slot, kb * P:(kb + 1) * P]
                            nc.tensor.matmul(out, kw, q_hi[:, slot, qs], start=True, stop=False)
                            nc.tensor.matmul(out, kw, q_lo[:, slot, qs], start=False, stop=True).then_inc(z_done, 1)
                        if REST <= s < N + REST:
                            n = s - REST
                            slot, c, qt, kb, d, c0, first, last = items[n]
                            out = sum_ps[:, c, c0:NT]
                            pe.wait_ge(t_done, j * N + done(n))
                            for part in (sp_hi, sp_lo):
                                mm = nc.tensor.matmul(out, neg_rest[:], part[:, n % R, c0:NT], start=False,
                                                      stop=last and part is sp_lo, skip_group_check=True)
                            mm.then_inc(rest_done, 1)
                        if OWN <= s < N + OWN:
                            n = s - OWN
                            slot, c, qt, kb, d, c0, first, last = items[n]
                            out = sum_ps[:, c, c0:NT]
                            pe.wait_ge(lo_done, j * N + done(n))
                            for part in (sp_hi, sp_lo):
                                mm = nc.tensor.matmul(out, neg_own[:], part[:, n % R, c0:NT],
                                                      start=first and part is sp_hi, stop=False,
                                                      skip_group_check=True)
                            mm.then_inc(own_done, 1)
                        if AV <= s < N + AV:
                            n = s - AV
                            slot, c, qt, kb, d, c0, first, last = items[n]
                            if n % PER_HEAD == 0:
                                pe.wait_ge(prep, PREP * (HEADS * j + slot + 1))
                            pe.wait_ge(a_done, j * N + done(n))
                            if d >= 0:
                                pe.wait_ge(a_masked, j * DIAG + diag_before[n] + 1)
                            if first:
                                pe.wait_ge(y_done, j * LASTS + done(tile_before(n)))
                            nc.tensor.matmul(y_ps[0:DH, c, c0:NT], v_sb[:, slot, kb], a_sb[:, n % RS, c0:NT],
                                             start=first, stop=last, skip_group_check=True).then_inc(av_done, 1)

            @block.vector
            def _(dve):
                for s in ringed["dve"]:
                    dve.sem_inc(s, R)
                dve.wait_ge(consts, 3)
                nc.vector.tensor_copy(neg_own[:], z_sb[:, 0, 0:P]).then_inc(consts, 1)
                nc.vector.tensor_copy(neg_rest[:], z_sb[:, 0, P:2 * P]).then_inc(consts, 1)

                def split(i, head, slot):
                    k, step = divmod(i, 4)
                    x = slice((PARTS - 1 - k) * NT, (PARTS - k) * NT)
                    lower = slice(DH, P)
                    if i == 0:
                        dve.wait_ge(q_loaded, 32 * (head + 1))
                        dve.wait_ge(k_loaded, 32 * (head + 1))
                    if i == PREP - 1:
                        dve.wait_ge(v_loaded, 16 * (head + 1))
                    if step == 0:
                        op = nc.vector.tensor_scalar(q_hi[:, slot, x], q_raw[:, x], SCALE, None, ALU.mult)
                    elif step == 1:
                        op = nc.vector.tensor_copy(k_st[:, slot, x], k_raw[:, x])
                    elif step == 2:
                        dve.wait_ge(prep, PREP * head + 4 * k + 1)
                        op = nc.vector.scalar_tensor_tensor(out=q_lo[:, slot, x], in0=q_raw[:, x], scalar=SCALE,
                                                            in1=f32(q_hi[:, slot, x]), op0=ALU.mult,
                                                            op1=ALU.subtract)
                    else:
                        dve.wait_ge(prep, PREP * head + 4 * k + 2)
                        op = nc.vector.tensor_tensor(k_st[lower, slot, x], k_raw[lower, x],
                                                     f32(k_st[lower, slot, x]), ALU.subtract)
                    op.then_inc(prep, 1)

                for i in range(PREP):
                    split(i, 0, 0)
                with dve.Fori(0, H // HEADS) as j:
                    for s in range(N + SUM):
                        if HI <= s < N + HI:
                            n = s - HI
                            d, c0 = items[n][4:6]
                            if d >= 0:
                                dve.wait_ge(masked, j * DIAG + diag_before[n] + 1)
                            dve.wait_ge(sp_done, j * N + done(n))
                            dve.wait_ge(rest_done, j * N + freed(n))
                            nc.vector.tensor_copy(sp_hi[:, n % R, c0:NT], sp_sb[:, n % R, c0:NT]
                                                  ).then_inc(hi_done, 1)
                        if SP <= s < N + SP:
                            n = s - SP
                            c0 = items[n][5]
                            dve.wait_ge(l_done, j * N + done(n))
                            dve.wait_ge(z_copied, j * N + done(n))
                            dve.wait_ge(lo_done, j * N + freed(n))
                            nc.vector.scalar_tensor_tensor(out=sp_sb[:, n % R, c0:NT], in0=e_sb[:, n % RS, c0:NT],
                                                           scalar=SP_CAP, in1=z_sb[:, n % R, c0:NT], op0=ALU.min,
                                                           op1=ALU.max).then_inc(sp_done, 1)
                        if SUM <= s < N + SUM:
                            n = s - SUM
                            slot, c, qt, kb, d, c0, first, last = items[n]
                            dve.wait_ge(own_done, j * N + done(n))
                            dve.wait_ge(a_done, j * N + done(n - RS))
                            nc.vector.tensor_tensor(t_sb[:, n % RS, c0:NT], sum_ps[:, c, c0:NT],
                                                    z_sb[:, n % R, c0:NT], ALU.add).then_inc(t_done, 1)
                        for slot in range(HEADS):
                            i = s - slot * PER_HEAD - 16
                            if 0 <= i < PREP:
                                split(i, HEADS * j + slot + 1, 1 - slot)


E = 16


def merge_branches(nc, sem, projT, yT, w_raw, w_loaded, mergedT, w_o, w_o_raw, w_o_loaded):
    B = 3
    KB = W // P
    WP = 4
    rows_of = lambda i: slice(i * KB, (i + 1) * KB)
    part_of = lambda i: slice(i * (D // WP), (i + 1) * (D // WP))
    with ExitStack() as ctx:
        sb = lambda n, s, dt=F32: ctx.enter_context(nc.sbuf_tensor(n, s, dt))
        w_hi = sb("mb_w_hi", [P, B * KB, D], F32R)
        w_lo = sb("mb_w_lo", [P, B * KB, D], F32R)
        y_raw = sb("mb_y_raw", [P, B * KB, NT])
        y_hi = sb("mb_y_hi", [P, 2, B * KB, NT], F32R)
        y_lo = sb("mb_y_lo", [P, 2, B * KB, NT], F32R)
        gate = sb("mb_gate", [P, 4, B, NT])
        part = sb("mb_part", [P, 2, B, NT])
        acc = ctx.enter_context(nc.psum_tensor("mb_acc", [P, 2, B, NT], F32))
        y_loaded = [sem(f"mb_y_loaded{i}") for i in range(B)]
        gate_loaded = [sem(f"mb_gate_loaded{b}") for b in range(4)]
        w_hi_done = sem("mb_w_hi_done")
        w_lo_done = sem("mb_w_lo_done")
        y_hi_done = sem("mb_y_hi_done")
        y_lo_done = sem("mb_y_lo_done")
        product_done = sem("mb_product_done")
        gated = sem("mb_gated")
        summed = sem("mb_summed")
        stored = [sem(f"mb_stored{b}") for b in range(2)]
        gates_dram = projT[GATES:COLS].rearrange("(i m) p s -> m p i s", i=B)
        n_items = TT * KT

        with nc.Block() as block:

            @block.sync
            def _(sp):
                def load_y(t):
                    for i in range(B):
                        sp.dma_start(y_raw[:, rows_of(i)], yT[:, rows_of(i), bass.ds(t * NT, NT)]
                                     ).then_inc(y_loaded[i], 16)

                def load_gates(t, m):
                    sp.dma_start(gate[:, m % 4], gates_dram[m, :, :, bass.ds(t * NT, NT)]
                                 ).then_inc(gate_loaded[m % 4], 16)

                load_y(0)
                for m in range(4):
                    load_gates(0, m)
                for b in range(2):
                    sp.sem_inc(stored[b], 16)
                with sp.Fori(0, TT // 2) as j:
                    for b in range(2):
                        t = 2 * j + b
                        for m in range(KT):
                            n = t * KT + m
                            if m == 0:
                                sp.wait_ge(y_lo_done, B * (t + 1))
                                load_y((t + 1) % TT)
                            sp.wait_ge(summed, 2 * n + 2)
                            sp.dma_start(mergedT[m, :, bass.ds(t * NT, NT)], part[:, m % 2, 0]
                                         ).then_inc(stored[m % 2], 16)
                            if m % 4 == 3:
                                row = bass.ds(KT // TT * t + m // 4, 1)
                                sp.dma_start(w_o_raw[:, row], w_o[:, row]).then_inc(w_o_loaded, 16)
                            ahead = t if m < KT - 4 else (t + 1) % TT
                            load_gates(ahead, (m + 4) % KT)
                for b in range(2):
                    sp.wait_ge(stored[b], 16 * (n_items // 2) + 16)
                for b in range(4):
                    sp.wait_ge(gate_loaded[b], 16 * (n_items // 4 + 1))
                for i in range(B):
                    sp.wait_ge(y_loaded[i], 16 * (TT + 1))
                sp.wait_ge(w_o_loaded, 16 * KT)

            @block.scalar
            def _(act):
                def y_high(t, b):
                    for i in range(B):
                        act.wait_ge(y_loaded[i], 16 * (t + 1))
                        nc.scalar.copy(y_hi[:, b, rows_of(i)], y_raw[:, rows_of(i)]).then_inc(y_hi_done, 1)

                act.wait_ge(w_loaded, 16)
                for i in range(WP):
                    nc.scalar.copy(w_hi[:, :, part_of(i)], w_raw[:, :, part_of(i)]).then_inc(w_hi_done, 1)
                    if i == 0:
                        y_high(0, 0)
                with act.Fori(0, TT // 2) as j:
                    for b in range(2):
                        t = 2 * j + b
                        act.wait_ge(product_done, t * KT + 1)
                        y_high(t + 1, 1 - b)

            @block.vector
            def _(dve):
                def y_low(t, b):
                    for i in range(B):
                        r = rows_of(i)
                        dve.wait_ge(y_hi_done, B * t + i + 1)
                        nc.vector.tensor_tensor(y_lo[:, b, r], y_raw[:, r], f32(y_hi[:, b, r]), ALU.subtract
                                                ).then_inc(y_lo_done, 1)

                dve.sem_inc(gated, 2 * B)
                for i in range(WP):
                    r = part_of(i)
                    if i == 1:
                        y_low(0, 0)
                    dve.wait_ge(w_hi_done, i + 1)
                    nc.vector.tensor_tensor(w_lo[:, :, r], w_raw[:, :, r], f32(w_hi[:, :, r]), ALU.subtract
                                            ).then_inc(w_lo_done, 1)
                with dve.Fori(0, TT // 2) as j:
                    for b in range(2):
                        t = 2 * j + b
                        for m in range(KT):
                            n = t * KT + m
                            if m == 3:
                                y_low(t + 1, 1 - b)
                            dve.wait_ge(gate_loaded[m % 4], 16 * (t * (KT // 4) + m // 4 + 1))
                            dve.wait_ge(product_done, n + 2)
                            dve.wait_ge(stored[m % 2], 16 * (t * (KT // 2) + m // 2 + 1))
                            for i in range(B):
                                nc.vector.tensor_tensor(part[:, m % 2, i], acc[:, m % 2, i], gate[:, m % 4, i],
                                                        ALU.mult).then_inc(gated, 1)
                            for i in range(1, B):
                                dve.wait_ge(gated, B * (n + 2) + i + 1)
                                if i > 1:
                                    dve.wait_ge(summed, 2 * n + 1)
                                nc.vector.tensor_tensor(part[:, m % 2, 0], part[:, m % 2, 0], part[:, m % 2, i],
                                                        ALU.add).then_inc(summed, 1)

            @block.tensor
            def _(pe):
                pe.sem_inc(product_done, 1)
                with pe.Fori(0, TT // 2) as j:
                    for b in range(2):
                        t = 2 * j + b
                        for m in range(KT):
                            n = t * KT + m
                            pe.wait_ge(w_lo_done, m * WP // KT + 1)
                            pe.wait_ge(gated, B * n + B)
                            for i in range(B):
                                if m == 0:
                                    pe.wait_ge(y_lo_done, B * t + i + 1)
                                for k in range(KB):
                                    ik = i * KB + k
                                    out, c = acc[:, m % 2, i], slice(m * P, (m + 1) * P)
                                    nc.tensor.matmul(out, w_hi[:, ik, c], y_hi[:, b, ik], start=k == 0, stop=False)
                                    nc.tensor.matmul(out, w_hi[:, ik, c], y_lo[:, b, ik], start=False, stop=False)
                                    last = nc.tensor.matmul(out, w_lo[:, ik, c], y_hi[:, b, ik],
                                                            start=False, stop=k == KB - 1)
                            last.then_inc(product_done, 1)


def mix_out(nc, sem, mergedT, w_raw, w_loaded, h_dram, ln_g, ln_b, w_router, h2_dram, logits, ident):
    HR = 4
    with ExitStack() as ctx:
        sb = lambda n, s, dt=F32: ctx.enter_context(nc.sbuf_tensor(n, s, dt))
        ps = lambda n, s, dt=F32: ctx.enter_context(nc.psum_tensor(n, s, dt))
        w_hi = sb("mo_w_hi", [P, KT, D], F32R)
        w_lo = sb("mo_w_lo", [P, KT, D], F32R)
        wr = sb("mo_w_router", [P, KT, E])
        m_raw = sb("mo_m_raw", [P, 2, KT, P])
        m_hi = sb("mo_m_hi", [P, 2, KT, P], F32R)
        m_lo = sb("mo_m_lo", [P, 2, KT, P], F32R)
        h = sb("mo_h", [P, 2, D])
        g_row = sb("mo_g", [P, D])
        b_row = sb("mo_b", [P, D])
        x2 = sb("mo_x2", [P, 2, D])
        h2 = sb("mo_h2", [P, HR, D])
        h2T = sb("mo_h2T", [P, KT, P])
        zeros = sb("mo_zeros", [P, D])
        stats = sb("mo_stats", [P, 2, 12])
        mv = sb("mo_mv", [P, 2, 4])
        half = sb("mo_half", [P, 1])
        out = ps("mo_out", [P, 2, 2, NT])
        tp = ps("mo_tp", [P, KT, P])
        lg = ps("mo_lg", [P, 2, NT])
        rows_loaded = sem("mo_rows_loaded")
        m_loaded = [sem(f"mo_m_loaded{b}") for b in range(2)]
        h_loaded = [sem(f"mo_h_loaded{b}") for b in range(2)]
        w_hi_done = sem("mo_w_hi_done")
        w_lo_done = sem("mo_w_lo_done")
        m_hi_done = sem("mo_m_hi_done")
        m_lo_done = sem("mo_m_lo_done")
        product_done = sem("mo_product_done")
        residual = sem("mo_residual")
        stat_chain = sem("mo_stat_chain")
        passed = sem("passed")
        consts = sem("mo_consts")
        rstd_done = sem("mo_rstd_done")
        normed = sem("mo_normed")
        scaled = sem("mo_scaled")
        h2_done = sem("mo_h2_done")
        h2_stored = [sem(f"mo_h2_stored{q}") for q in range(HR)]
        pad_stored = sem("mo_pad_stored")
        turned = sem("mo_turned")
        h2T_done = sem("mo_h2T_done")
        logit_done = sem("mo_logit_done")
        logits_copied = sem("mo_logits_copied")
        m_t = mergedT.rearrange("m p (t c) -> p t m c", c=P)
        h_t = h_dram.rearrange("(t p) d -> p t d", p=P)
        h2_t = h2_dram.rearrange("(t p) d -> p t d", p=P)
        flat = lambda a: a.rearrange("p o d -> p (o d)")

        def steps(eng, step):
            for s in range(HR):
                step(s, s, True)
            with eng.Fori(1, TILES // HR) as j:
                for q in range(HR):
                    step(HR * j + q, q, True)
            for s in range(TILES, TILES + 3):
                step(s, s % HR, False)

        def first(s, lag):
            return isinstance(s, int) and s < lag

        def past(s, lag):
            return isinstance(s, int) and s - lag >= TILES

        with nc.Block() as block:

            @block.sync
            def _(sp):
                def step(s, q, product):
                    if product:
                        b = q % 2
                        if not first(s, 2):
                            sp.wait_ge(residual, 2 * s - 2)
                        sp.dma_start(m_raw[:, b], m_t[:, bass.ds(s, 1)].rearrange("p o m c -> p (o m) c")
                                     ).then_inc(m_loaded[b], 16)
                        sp.dma_start(h[:, b], flat(h_t[:, bass.ds(s, 1)])).then_inc(h_loaded[b], 16)
                    if isinstance(s, int) and s == 0:
                        sp.dma_start(g_row[:], ln_g.partition_broadcast(P)).then_inc(rows_loaded, 16)
                        sp.dma_start(b_row[:], ln_b.partition_broadcast(P)).then_inc(rows_loaded, 16)
                        sp.dma_start(wr[:], w_router).then_inc(rows_loaded, 16)
                    if not first(s, 3):
                        sp.wait_ge(h2_done, s - 2)
                        sp.dma_start(flat(h2_t[:, bass.ds(s - 3, 1)]), h2[:, (q + 1) % HR]
                                     ).then_inc(h2_stored[(q + 1) % HR], 16)

                steps(sp, step)
                sp.wait_ge(consts, 2)
                sp.dma_start(flat(h2_t[:, TILES:TILES + 1]), zeros[:]).then_inc(pad_stored, 16)
                for q in range(HR):
                    sp.wait_ge(h2_stored[q], 16 * (TILES // HR))
                sp.wait_ge(pad_stored, 16)

            @block.gpsimd
            def _(pool):
                nc.gpsimd.memset(half[:], -0.5).then_inc(consts, 1)
                nc.gpsimd.memset(zeros[:], 0.0).then_inc(consts, 1)
                pool.wait_ge(consts, 2)
                pool.wait_ge(rows_loaded, 48)

                def step(s, q, product):
                    if first(s, 1) or past(s, 1):
                        return
                    q, b = (q - 1) % HR, (q - 1) % 2
                    pool.wait_ge(stat_chain, 4 * s)
                    nc.gpsimd.tensor_tensor(mv[:, b, 3:4], mv[:, b, 2:3], half[:], ALU.pow).then_inc(rstd_done, 1)
                    if not first(s, HR + 1):
                        pool.wait_ge(h2_stored[q], 16 * ((s - 1) // HR))
                        pool.wait_ge(turned, s - HR)
                    pool.wait_ge(normed, s)
                    nc.gpsimd.tensor_tensor(h2[:, q], x2[:, b], g_row[:], ALU.mult).then_inc(scaled, 1)
                    pool.wait_ge(scaled, s)
                    nc.gpsimd.tensor_tensor(h2[:, q], h2[:, q], b_row[:], ALU.add).then_inc(h2_done, 1)

                steps(pool, step)

            @block.scalar
            def _(act):
                def high_rows(ks):
                    act.wait_ge(w_loaded, 16 * KT)
                    for k in ks:
                        nc.scalar.copy(w_hi[:, k], w_raw[:, k]).then_inc(w_hi_done, 1)

                def step(s, q, product):
                    if isinstance(s, int) and s == 0:
                        high_rows(range(KT // 2))
                    if product:
                        b = q % 2
                        act.wait_ge(m_loaded[b], 16 * (s // 2 + 1))
                        if not first(s, 2):
                            act.wait_ge(product_done, 2 * s - 2)
                        nc.scalar.copy(m_hi[:, b], m_raw[:, b]).then_inc(m_hi_done, 1)
                    if isinstance(s, int) and s == 0:
                        high_rows(range(KT // 2, KT))
                    if not first(s, 3):
                        if not first(s, 4):
                            act.wait_ge(logit_done, s - 3)
                        act.wait_ge(turned, s - 2)
                        nc.scalar.copy(h2T[:], tp[:]).then_inc(h2T_done, 1)

                steps(act, step)
                act.wait_ge(logit_done, TILES)
                for b in range(2):
                    nc.scalar.copy(logits[:, b::2], lg[:, b, 0:TILES // 2 * E].rearrange("p (t e) -> p t e", e=E)
                                   ).then_inc(logits_copied, 1)

            @block.vector
            def _(dve):
                def low_rows(ks):
                    for k in ks:
                        dve.wait_ge(w_hi_done, k + 1)
                        nc.vector.tensor_tensor(w_lo[:, k], w_raw[:, k], f32(w_hi[:, k]), ALU.subtract
                                                ).then_inc(w_lo_done, 1)

                def step(s, q, product):
                    if isinstance(s, int) and s == 0:
                        low_rows(range(KT // 2))
                    if product:
                        b = q % 2
                        if not first(s, 2):
                            dve.wait_ge(product_done, 2 * s - 2)
                        dve.wait_ge(m_hi_done, s + 1)
                        nc.vector.tensor_tensor(m_lo[:, b], m_raw[:, b], f32(m_hi[:, b]), ALU.subtract
                                                ).then_inc(m_lo_done, 1)
                    if isinstance(s, int) and s == 0:
                        low_rows(range(KT // 2, KT))
                    if first(s, 1) or past(s, 1):
                        return
                    b = (q - 1) % 2
                    dve.wait_ge(h_loaded[b], 16 * ((s - 1) // 2 + 1))
                    if not first(s, 3):
                        dve.wait_ge(scaled, s - 2)
                    for c in range(2):
                        x = slice(c * NT, (c + 1) * NT)
                        dve.wait_ge(product_done, 2 * s - 1 + c)
                        nc.vector.scalar_tensor_tensor(out=x2[:, b, x], in0=h[:, b, x], scalar=ALPHA,
                                                       in1=out[:, b, c], op0=ALU.mult, op1=ALU.add
                                                       ).then_inc(residual, 1)
                    for c in range(2):
                        dve.wait_ge(residual, 2 * s - 1 + c)
                        nc.vector.bn_stats(stats[:, b, 6 * c:6 * c + 6], x2[:, b, c * NT:(c + 1) * NT]
                                           ).then_inc(stat_chain, 1)
                    dve.wait_ge(stat_chain, 4 * s - 2)
                    dve.sem_inc(passed, 1)
                    nc.vector.bn_aggr(mv[:, b, 0:2], stats[:, b]).then_inc(stat_chain, 1)
                    dve.wait_ge(stat_chain, 4 * s - 1)
                    nc.vector.tensor_scalar(mv[:, b, 2:3], mv[:, b, 1:2], EPS, None, ALU.add).then_inc(stat_chain, 1)
                    dve.wait_ge(rstd_done, s)
                    nc.vector.tensor_scalar(x2[:, b], x2[:, b], mv[:, b, 0:1], mv[:, b, 3:4],
                                            ALU.subtract, ALU.mult).then_inc(normed, 1)

                steps(dve, step)

            @block.tensor
            def _(pe):
                def product_half(s, b, c):
                    if not first(s, 2):
                        pe.wait_ge(residual, 2 * s - 3 + c)
                    for k in range(KT):
                        if isinstance(s, int) and s == 0 and c == 0:
                            pe.wait_ge(w_lo_done, k + 1)
                        o, x = out[:, b, c], slice(c * NT, (c + 1) * NT)
                        nc.tensor.matmul(o, m_hi[:, b, k], w_hi[:, k, x], start=k == 0, stop=False)
                        nc.tensor.matmul(o, m_lo[:, b, k], w_hi[:, k, x], start=False, stop=False)
                        last = nc.tensor.matmul(o, m_hi[:, b, k], w_lo[:, k, x], start=False, stop=k == KT - 1)
                    last.then_inc(product_done, 1)

                def step(s, q, product):
                    if product:
                        pe.wait_ge(m_lo_done, s + 1)
                        product_half(s, q % 2, 0)
                    if not first(s, 3):
                        pe.wait_ge(h2T_done, s - 2)
                        cols = bass.ds((s - 3) // 2 * E, E)
                        for k in range(KT):
                            last = nc.tensor.matmul(lg[:, (q + 1) % 2, cols], h2T[:, k], wr[:, k], start=k == 0,
                                                    stop=k == KT - 1, skip_group_check=True)
                        last.then_inc(logit_done, 1)
                    if product:
                        product_half(s, q % 2, 1)
                    if not first(s, 2) and not past(s, 2):
                        pe.wait_ge(h2_done, s - 1)
                        if not first(s, 3):
                            pe.wait_ge(h2T_done, s - 2)
                        for k in range(KT):
                            last = nc.tensor.transpose(tp[:, k], h2[:, (q + 2) % HR, k * P:(k + 1) * P], ident[:])
                        last.then_inc(turned, 1)

                steps(pe, step)


EG = 4
FF = 128
GUC, DNC = KT, EG
E_TILES = TILES + EG - 1
DSLOTS = 3
META = 8


def dispatch(nc, sem, logits, router_bias, order, meta, table, gu_w, dn_w, gu_raw, dn_raw, gu_loaded, dn_loaded):
    with ExitStack() as ctx:
        sb = lambda n, s, dt=F32: ctx.enter_context(nc.sbuf_tensor(n, s, dt))
        TG = TILES * EG
        bias = sb("dp_bias", [P, E])
        score = sb("dp_score", [P, TG, EG])
        sel = sb("dp_sel", [P, TG, EG])
        rank = sb("dp_rank", [P, TG, EG])
        ahead = sb("dp_ahead", [P, TG, EG, EG])
        taken = sb("dp_taken", [P, TG, EG])
        g_score = sb("dp_g_score", [P, TG])
        g_rank = sb("dp_g_rank", [P, TG])
        best = sb("dp_best", [P, TG])
        before = sb("dp_before", [P, P])
        ones = sb("dp_ones", [P, P])
        tile_sum = sb("dp_tile_sum", [P, TG])
        upto = sb("dp_upto", [P, TG])
        place = sb("dp_place", [P, TG])
        slot = sb("dp_slot", [P, TILES])
        slot_u = sb("dp_slot_u", [P, TILES], U32)
        denom = sb("dp_denom", [P, TILES])
        rdenom = sb("dp_rdenom", [P, TILES])
        weight = sb("dp_weight", [P, TILES, EG])
        steps = sb("dp_steps", [P, TILES])
        over = sb("dp_over", [P, EG, TILES])
        g_tiles = sb("dp_g_tiles", [P, EG])
        start = sb("dp_start", [P, EG])
        tile_no = sb("dp_tile_no", [P, E_TILES])
        past = sb("dp_past", [P, 3, E_TILES])
        group = sb("dp_group", [P, E_TILES])
        need = sb("dp_need", [P, 3])
        pad = sb("dp_pad", [P, E_TILES, META])
        row = sb("dp_row", [P, TILES, META])
        ps = ctx.enter_context(nc.psum_tensor("dp_ps", [P, 2, NT], F32))
        loaded = sem("dp_loaded")
        consts = sem("dp_consts")
        scored = sem("dp_scored")
        chain = sem("dp_chain")
        counted = sem("dp_counted")
        padded = sem("dp_padded")
        row_done = sem("dp_row_done")
        scattered = sem("dp_scattered")
        meta_loaded = sem("dp_meta_loaded")
        order_t = order.rearrange("(t p) w -> p t w", p=P)

        with nc.Block() as block:

            @block.sync
            def _(sp):
                sp.dma_start(bias[:], router_bias.partition_broadcast(P)).then_inc(loaded, 16)
                sp.wait_ge(consts, 7)
                sp.dma_start(order_t, pad[:]).then_inc(padded, 16)
                for c in range(GUC):
                    sp.dma_start(gu_raw[:, 0, c], gu_w[0, :, c]).then_inc(gu_loaded, 16)
                sp.dma_start(dn_raw[:, 0], dn_w[0]).then_inc(dn_loaded, 16)
                sp.wait_ge(scattered, 16 * TILES)
                sp.dma_start(meta[:], order_t).then_inc(meta_loaded, 16)
                sp.wait_ge(meta_loaded, 16)

            @block.gpsimd
            def _(pool):
                nc.gpsimd.memset(ahead[:], 0.0).then_inc(consts, 1)
                nc.gpsimd.memset(pad[:], 0.0).then_inc(consts, 1)
                nc.gpsimd.memset(row[:], 0.0).then_inc(consts, 1)
                nc.gpsimd.memset(ones[:], 1.0).then_inc(consts, 1)
                pool.wait_ge(consts, 4)
                nc.gpsimd.affine_select(out=before[:], in_=ones[:], compare_op=ALU.is_gt, fill=0.0, base=0,
                                        pattern=[[1, P]], channel_multiplier=-1).then_inc(consts, 1)
                nc.gpsimd.iota(pad[:, :, 0].bitcast(U32), [[0, E_TILES]], base=S, channel_multiplier=1
                               ).then_inc(consts, 1)
                nc.gpsimd.iota(row[:, :, 0].bitcast(U32), [[P, TILES]], base=0, channel_multiplier=1
                               ).then_inc(consts, 1)
                nc.gpsimd.iota(steps[:], [[P, TILES]], base=0, channel_multiplier=0,
                               allow_small_or_imprecise_dtypes=True).then_inc(consts, 1)
                nc.gpsimd.iota(tile_no[:], [[1, E_TILES]], base=0, channel_multiplier=0,
                               allow_small_or_imprecise_dtypes=True).then_inc(consts, 1)
                pool.wait_ge(padded, 16)
                pool.wait_ge(row_done, 2)
                for t in range(TILES):
                    nc.gpsimd.indirect_dma_start(out=order, out_offset=bass.IndirectOffsetOnAxis(slot_u[:, t:t + 1], 0),
                                                 in_=row[:, t], in_offset=None).then_inc(scattered, 16)

            @block.scalar
            def _(act):
                nc.scalar.activation(score[:].rearrange("p (t g) e -> p t (g e)", g=EG), logits[:], ACT.Sigmoid
                                     ).then_inc(scored, 1)

            @block.tensor
            def _(pe):
                pe.wait_ge(consts, 5)
                pe.wait_ge(counted, 1)
                nc.tensor.matmul(ps[:, 0, 0:TG], before[:], best[:], start=True, stop=True)
                nc.tensor.matmul(ps[:, 1, 0:TG], ones[:], best[:], start=True, stop=True).then_inc(counted, 1)

            @block.vector
            def _(dve):
                count = [0]

                def link(op):
                    count[0] += 1
                    op.then_inc(chain, 1)
                    dve.wait_ge(chain, count[0])

                def ranks(out, x, ahead):
                    for i in range(EG):
                        for js, op in ((slice(0, i), ALU.is_ge), (slice(i + 1, EG), ALU.is_gt)):
                            if js.start < js.stop:
                                mine = x[:, :, i:i + 1].to_broadcast([P, x.shape[1], js.stop - js.start])
                                count[0] += 1
                                nc.vector.tensor_tensor(ahead[:, :, i, js], x[:, :, js], mine, op).then_inc(chain, 1)
                    dve.wait_ge(chain, count[0])
                    link(nc.vector.tensor_reduce(out, ahead, AX_X, ALU.add))

                by_token = lambda a: a.rearrange("p (t g) e -> p t (g e)", g=EG)
                by_group = lambda a: a.rearrange("p (t g) -> p t g", g=EG)
                dve.wait_ge(loaded, 16)
                dve.wait_ge(consts, 4)
                dve.wait_ge(scored, 1)
                link(nc.vector.tensor_tensor(by_token(sel[:]), by_token(score[:]),
                                             bias[:].unsqueeze(1).to_broadcast([P, TILES, E]), ALU.add))
                ranks(rank[:], sel[:], ahead[:])
                link(nc.vector.tensor_scalar(taken[:], rank[:], 2.0, None, ALU.is_lt))
                link(nc.vector.tensor_tensor(rank[:], sel[:], taken[:], ALU.mult))
                link(nc.vector.tensor_reduce(g_score[:], rank[:], AX_X, ALU.add))
                ranks(by_group(g_rank[:]), by_group(g_score[:]), ahead[:, 0:TILES])
                nc.vector.tensor_scalar(best[:], g_rank[:], 1.0, None, ALU.is_lt).then_inc(counted, 1)
                dve.wait_ge(counted, 1)
                link(nc.vector.tensor_tensor(taken[:], taken[:], score[:], ALU.mult))
                link(nc.vector.tensor_tensor(taken[:], taken[:], best[:].unsqueeze(2).to_broadcast([P, TG, EG]),
                                             ALU.mult))
                link(nc.vector.tensor_reduce(denom[:], by_token(taken[:]), AX_X, ALU.add))
                link(nc.vector.reciprocal(rdenom[:], denom[:]))
                link(nc.vector.tensor_reduce(weight[:], taken[:].rearrange("p (t g) e -> p t e g", g=EG),
                                             AX_X, ALU.add))
                dve.wait_ge(consts, 9)
                nc.vector.tensor_tensor(row[:, :, 1:1 + EG], weight[:],
                                        rdenom[:].unsqueeze(2).to_broadcast([P, TILES, EG]), ALU.mult
                                        ).then_inc(row_done, 1)
                dve.wait_ge(counted, 2)
                link(nc.vector.tensor_copy(tile_sum[:], ps[:, 1, 0:TG]))
                for g in range(EG):
                    x = by_group(tile_sum[:])[:, :, g]
                    link(nc.vector.tensor_tensor_scan(by_group(upto[:])[:, :, g], ones[:, 0:TILES], x, 0.0,
                                                      ALU.mult, ALU.add))
                link(nc.vector.tensor_tensor(place[:], upto[:], tile_sum[:], ALU.subtract))
                link(nc.vector.tensor_tensor(place[:], place[:], ps[:, 0, 0:TG], ALU.add))
                total = by_group(upto[:])[:, TILES - 1]
                link(nc.vector.tensor_tensor(over[:], total.unsqueeze(2).to_broadcast([P, EG, TILES]),
                                             steps[:].unsqueeze(1).to_broadcast([P, EG, TILES]), ALU.is_gt))
                link(nc.vector.tensor_reduce(g_tiles[:], over[:], AX_X, ALU.add))
                link(nc.vector.memset(start[:, 0:1], 0.0))
                for g in range(1, EG):
                    link(nc.vector.tensor_tensor(start[:, g:g + 1], start[:, g - 1:g], g_tiles[:, g - 1:g], ALU.add))
                link(nc.vector.scalar_tensor_tensor(out=by_group(place[:]),
                                                    in0=start[:].unsqueeze(1).to_broadcast([P, TILES, EG]),
                                                    scalar=float(P), in1=by_group(place[:]), op0=ALU.mult, op1=ALU.add))
                link(nc.vector.tensor_tensor(place[:], place[:], best[:], ALU.mult))
                link(nc.vector.tensor_reduce(slot[:], by_group(place[:]), AX_X, ALU.add))
                nc.vector.tensor_copy(slot_u[:], slot[:]).then_inc(row_done, 1)
                link(nc.vector.tensor_tensor(past[:], tile_no[:].unsqueeze(1).to_broadcast([P, 3, E_TILES]),
                                             start[:, 1:EG].unsqueeze(2).to_broadcast([P, 3, E_TILES]), ALU.is_ge))
                link(nc.vector.tensor_reduce(group[:], past[:].rearrange("p g t -> p t g"), AX_X, ALU.add))
                link(nc.vector.tensor_copy(table[:, 0:E_TILES], group[0:1, :]))
                link(nc.vector.tensor_scalar(need[:, 0:2], start[:, 1:3], float(GUC), 1.0, ALU.mult, ALU.add))
                link(nc.vector.tensor_scalar(need[:, 2:3], start[:, 1:2], 1.0, None, ALU.add))
                link(nc.vector.tensor_copy(table[:, E_TILES:E_TILES + 3], need[0:1, :]))


def experts(nc, sem, h2_dram, meta, table, gu_w, dn_w, gu_raw, dn_raw, gu_loaded, dn_loaded, ln_g, ln_b, out, ident):
    RING = 4
    XR = 4
    with ExitStack() as ctx:
        sb = lambda n, s, dt=F32: ctx.enter_context(nc.sbuf_tensor(n, s, dt))
        ps = lambda n, s, dt=F32: ctx.enter_context(nc.psum_tensor(n, s, dt))
        w_hi = sb("ex_w_hi", [P, RING, D], F32R)
        w_lo = sb("ex_w_lo", [P, RING, D], F32R)
        x = sb("ex_x", [P, XR, D])
        o = sb("ex_o", [P, 2, D])
        xT_hi = sb("ex_xT_hi", [P, 2, KT, P], F32R)
        xT_lo = sb("ex_xT_lo", [P, 2, KT, P], F32R)
        act_g = sb("ex_gate", [P, EG * FF])
        hid = sb("ex_hid", [P, EG * FF])
        hT_sb = sb("ex_hT_sb", [P, EG, P])
        g_row = sb("ex_g", [P, D])
        b_row = sb("ex_b", [P, D])
        stats = sb("ex_stats", [P, 12])
        mv = sb("ex_mv", [P, 4])
        half = sb("ex_half", [P, 1])
        gather_ids = sb("ex_gather_ids", [P, XR, 1], U32)
        store_ids = sb("ex_store_ids", [P, 2, 1], U32)
        gu = ps("ex_gu", [P, 2, NT])
        y = ps("ex_y", [P, 2, NT])
        xT = ps("ex_xT", [P, KT, P])
        hT = ps("ex_hT", [P, EG, P])
        rows_loaded = sem("ex_rows_loaded")
        consts = sem("ex_consts")
        passed = sem("passed")
        gather_ids_done = sem("ex_gather_ids_done")
        store_ids_done = sem("ex_store_ids_done")
        x_loaded = [sem(f"ex_x_loaded{q}") for q in range(XR)]
        w_high = sem("ex_w_high")
        w_split = sem("ex_w_split")
        w_used = sem("ex_w_used")
        x_turned = sem("ex_x_turned")
        x_high = sem("ex_x_high")
        x_split = sem("ex_x_split")
        gate_done = sem("ex_gate_done")
        hid_done = sem("ex_hid_done")
        h_turned = sem("ex_h_turned")
        h_copied = sem("ex_h_copied")
        down_done = sem("ex_down_done")
        residual = sem("ex_residual")
        stat_chain = sem("ex_stat_chain")
        rstd_done = sem("ex_rstd_done")
        normed = sem("ex_normed")
        scaled = sem("ex_scaled")
        shifted = sem("ex_shifted")
        stored = sem("ex_stored")
        o_free = sem("ex_o_free")
        T = E_TILES

        def steps(eng, step):
            step(0, 0, True, False, False)
            step(1, 1, True, True, False)
            with eng.Fori(0, (T - 3) // XR) as j:
                for i in range(XR):
                    step(XR * j + 2 + i, (2 + i) % XR, True, True, True)
            step(T - 1, (T - 1) % XR, True, True, True)
            step(T, T % XR, False, True, True)
            step(T + 1, (T + 1) % XR, False, False, True)

        def chunk(s, i):
            return GUC * s + i

        def group_of(eng, t):
            return eng.value_load(table[0:1, bass.ds(t, 1)], min_val=0, max_val=EG - 1)

        meta_ids = meta[:, :, 0].bitcast(U32)

        with nc.Block() as block:

            @block.sync
            def _(sp):
                need = [sp.value_load(table[0:1, E_TILES + i:E_TILES + i + 1], min_val=1,
                                      max_val=GUC * T + 1) for i in range(3)]
                sp.dma_start(g_row[:], ln_g.partition_broadcast(P)).then_inc(rows_loaded, 16)
                sp.dma_start(b_row[:], ln_b.partition_broadcast(P)).then_inc(rows_loaded, 16)
                def load_gu(g):
                    for c in range(GUC):
                        sp.wait_ge(gu_loaded, 16 * (GUC * g + c))
                        sp.dma_start(gu_raw[:, g % 2, c], gu_w[g, :, c]).then_inc(gu_loaded, 16)

                sp.wait_ge(x_loaded[1], 16)
                for g in range(1, DSLOTS):
                    sp.wait_ge(dn_loaded, 16 * g)
                    if g < 2:
                        load_gu(1)
                    sp.dma_start(dn_raw[:, g], dn_w[g]).then_inc(dn_loaded, 16)
                for g in (2, 3):
                    sp.wait_ge(w_split, need[g - 2])
                    load_gu(g)
                sp.wait_ge(dn_loaded, 16 * DSLOTS)
                sp.wait_ge(down_done, need[2])
                sp.dma_start(dn_raw[:, 0], dn_w[3]).then_inc(dn_loaded, 16)
                sp.wait_ge(gu_loaded, 16 * EG * GUC)
                sp.wait_ge(dn_loaded, 16 * EG)

            @block.gpsimd
            def _(pool):
                def gather(t, q):
                    nc.gpsimd.tensor_copy(gather_ids[:, q], meta_ids[:, bass.ds(t, 1)]).then_inc(gather_ids_done, 1)
                    pool.wait_ge(gather_ids_done, t + 1)
                    pool.sem_inc(passed, 1)
                    nc.gpsimd.indirect_dma_start(out=x[:, q], out_offset=None, in_=h2_dram,
                                                 in_offset=bass.IndirectOffsetOnAxis(gather_ids[:, q], 0)
                                                 ).then_inc(x_loaded[q], 16)

                nc.gpsimd.memset(half[:], -0.5).then_inc(consts, 1)
                pool.wait_ge(consts, 1)
                pool.sem_inc(o_free, 2)
                gather(0, 0)

                def step(s, q, has_gu, has_dn, has_norm):
                    b = q % 2
                    if has_gu and not (isinstance(s, int) and s == T - 1):
                        if has_norm:
                            pool.wait_ge(residual, 2 * (s - 1))
                        gather(s + 1, (q + 1) % XR)
                    if has_norm:
                        t = s - 2
                        pool.wait_ge(stat_chain, 4 * t + 4)
                        nc.gpsimd.tensor_tensor(mv[:, 3:4], mv[:, 2:3], half[:], ALU.pow).then_inc(rstd_done, 1)
                        pool.wait_ge(rows_loaded, 32)
                        pool.wait_ge(normed, t + 1)
                        nc.gpsimd.tensor_tensor(o[:, b], o[:, b], g_row[:], ALU.mult).then_inc(scaled, 1)
                        nc.gpsimd.tensor_copy(store_ids[:, b], meta_ids[:, bass.ds(t, 1)]).then_inc(store_ids_done, 1)
                        pool.wait_ge(scaled, t + 1)
                        nc.gpsimd.tensor_tensor(o[:, b], o[:, b], b_row[:], ALU.add).then_inc(shifted, 1)
                        pool.wait_ge(store_ids_done, t + 1)
                        pool.wait_ge(shifted, t + 1)
                        pool.sem_inc(passed, 1)
                        nc.gpsimd.indirect_dma_start(out=out, out_offset=bass.IndirectOffsetOnAxis(store_ids[:, b], 0),
                                                     in_=o[:, b], in_offset=None, bounds_check=S - 1,
                                                     oob_is_err=False).then_inc(stored, 16)
                        pool.wait_ge(stored, 16 * t + 16)
                        pool.sem_inc(o_free, 1)

                steps(pool, step)

            @block.scalar
            def _(act):
                def high_part(s, i, group):
                    n = chunk(s, i)
                    act.wait_ge(gu_loaded, group * (16 * GUC) + 16 * (i + 1))
                    act.wait_ge(w_used, n + 1)
                    nc.scalar.copy(w_hi[:, i % RING], gu_raw[:, bass.ds(group % 2, 1), i
                                                             ].rearrange("p o n -> p (o n)")).then_inc(w_high, 1)

                def turned_x(t, b):
                    act.wait_ge(x_turned, t + 1)
                    nc.scalar.copy(xT_hi[:, b], xT[:]).then_inc(x_high, 1)

                def step(s, q, has_gu, has_dn, has_norm):
                    b = q % 2
                    if has_gu:
                        group = group_of(act, s)
                        if not (isinstance(s, int) and s == 0):
                            for i in range(RING):
                                high_part(s, i, group)
                    if has_dn:
                        act.wait_ge(h_turned, s)
                        act.wait_ge(down_done, s)
                        nc.scalar.copy(hT_sb[:], hT[:]).then_inc(h_copied, 1)
                    if has_gu:
                        for i in range(RING, GUC):
                            high_part(s, i, group)
                        act.wait_ge(w_used, chunk(s, GUC - 1) + RING + 1)
                        if has_dn:
                            act.wait_ge(hid_done, s)
                        nc.scalar.activation(act_g[:], gu[:, 0], ACT.Silu).then_inc(gate_done, 1)
                        if not (isinstance(s, int) and s == T - 1):
                            turned_x(s + 1, 1 - b)

                first_group = group_of(act, 0)
                for i in range(RING):
                    high_part(0, i, first_group)
                turned_x(0, 0)
                steps(act, step)

            @block.tensor
            def _(pe):
                def turn_x(t, q):
                    pe.wait_ge(x_loaded[q], 16 * (t // XR + 1))
                    if not (isinstance(t, int) and t == 0):
                        pe.wait_ge(x_split, t)
                    for k in range(KT):
                        last = nc.tensor.transpose(xT[:, k], x[:, q, k * P:(k + 1) * P], ident[:])
                    last.then_inc(x_turned, 1)

                def gate_up(s, b, i):
                    pe.wait_ge(w_split, chunk(s, i) + 2)
                    r = i % RING
                    for c in range(2):
                        cols = slice(c * NT, (c + 1) * NT)
                        nc.tensor.matmul(gu[:, c], xT_hi[:, b, i], w_hi[:, r, cols], start=i == 0, stop=False)
                        nc.tensor.matmul(gu[:, c], xT_lo[:, b, i], w_hi[:, r, cols], start=False, stop=False)
                        last = nc.tensor.matmul(gu[:, c], xT_hi[:, b, i], w_lo[:, r, cols],
                                                start=False, stop=i == GUC - 1)
                    last.then_inc(w_used, 1)

                def step(s, q, has_gu, has_dn, has_norm):
                    b = q % 2
                    if has_gu:
                        pe.wait_ge(x_split, s + 1)
                        if has_dn:
                            pe.wait_ge(hid_done, s)
                        for i in range(2):
                            gate_up(s, b, i)
                    if has_dn:
                        pe.wait_ge(hid_done, s)
                        if has_norm:
                            pe.wait_ge(h_copied, s - 1)
                        for e in range(EG):
                            last = nc.tensor.transpose(hT[:, e], hid[:, e * FF:(e + 1) * FF], ident[:])
                        last.then_inc(h_turned, 1)
                    if has_gu:
                        for i in range(2, GUC):
                            gate_up(s, b, i)
                        if not (isinstance(s, int) and s == T - 1):
                            turn_x(s + 1, (q + 1) % XR)
                    if has_dn:
                        group = group_of(pe, s - 1)
                        pe.wait_ge(dn_loaded, group * 16 + 16)
                        pe.wait_ge(h_copied, s)
                        if has_norm:
                            pe.wait_ge(residual, 2 * s)
                        for e in range(EG):
                            for c in range(2):
                                w = dn_raw[:, bass.ds(group % DSLOTS, 1), e, c * NT:(c + 1) * NT]
                                last = nc.tensor.matmul(y[:, c], hT_sb[:, e], w.rearrange("p o n -> p (o n)"),
                                                        start=e == 0, stop=e == EG - 1)
                        last.then_inc(down_done, 1)

                pe.sem_inc(w_used, RING)
                pe.sem_inc(down_done, 1)
                turn_x(0, 0)
                steps(pe, step)

            @block.vector
            def _(dve):
                def low_part(s, i, group):
                    n = chunk(s, i)
                    dve.wait_ge(w_high, n + 1)
                    nc.vector.tensor_tensor(w_lo[:, i % RING], gu_raw[:, bass.ds(group % 2, 1), i
                                                                      ].rearrange("p o n -> p (o n)"),
                                            f32(w_hi[:, i % RING]), ALU.subtract).then_inc(w_split, 1)

                def x_low(t, b):
                    dve.wait_ge(x_high, t + 1)
                    nc.vector.tensor_tensor(xT_lo[:, b], xT[:], f32(xT_hi[:, b]), ALU.subtract).then_inc(x_split, 1)

                def step(s, q, has_gu, has_dn, has_norm):
                    b = q % 2

                    def low_parts(chunks):
                        if has_gu:
                            for i in chunks:
                                low_part(s, i, group)

                    if has_gu:
                        group = group_of(dve, s)
                    low_parts(range(0 if has_dn or has_norm else RING, RING))
                    if has_norm:
                        t = s - 2
                        dve.wait_ge(down_done, t + 2)
                        dve.wait_ge(o_free, t + 1)
                        for c in range(2):
                            cols = slice(c * NT, (c + 1) * NT)
                            nc.vector.scalar_tensor_tensor(out=o[:, b, cols], in0=x[:, (q + 2) % XR, cols], scalar=ALPHA,
                                                           in1=y[:, c], op0=ALU.mult, op1=ALU.add
                                                           ).then_inc(residual, 1)
                        for c in range(2):
                            dve.wait_ge(residual, 2 * t + c + 3)
                            nc.vector.bn_stats(stats[:, 6 * c:6 * c + 6], o[:, b, c * NT:(c + 1) * NT]
                                               ).then_inc(stat_chain, 1)
                    low_parts(range(4, 5))
                    if has_norm:
                        dve.wait_ge(stat_chain, 4 * t + 2)
                        dve.sem_inc(passed, 1)
                        nc.vector.bn_aggr(mv[:, 0:2], stats[:]).then_inc(stat_chain, 1)
                        dve.wait_ge(stat_chain, 4 * t + 3)
                        nc.vector.tensor_scalar(mv[:, 2:3], mv[:, 1:2], EPS, None, ALU.add).then_inc(stat_chain, 1)
                    low_parts(range(5, 6))
                    if has_norm:
                        dve.wait_ge(rstd_done, t + 1)
                        nc.vector.tensor_scalar(o[:, b], o[:, b], mv[:, 0:1], mv[:, 3:4],
                                                ALU.subtract, ALU.mult).then_inc(normed, 1)
                    low_parts(range(6, GUC))
                    if has_gu:
                        dve.wait_ge(gate_done, s + 1)
                        if has_dn:
                            dve.wait_ge(h_turned, s)
                        for e in range(EG):
                            cols = slice(e * FF, (e + 1) * FF)
                            op = nc.vector.scalar_tensor_tensor(
                                out=hid[:, cols], in0=gu[:, 1, cols],
                                scalar=meta[:, bass.ds(s, 1), 1 + e:2 + e].rearrange("p o w -> p (o w)"),
                                in1=act_g[:, cols], op0=ALU.mult, op1=ALU.mult)
                        op.then_inc(hid_done, 1)
                        if not (isinstance(s, int) and s == T - 1):
                            x_low(s + 1, 1 - b)

                dve.sem_inc(w_split, 1)
                dve.sem_inc(residual, 2)
                first_group = group_of(dve, 0)
                for i in range(RING):
                    low_part(0, i, first_group)
                x_low(0, 0)
                steps(dve, step)


def hybrid_decoder_layer(nc, x, ln_in_g, ln_in_b, w_in, b_gate, conv_w, sg_w, sg_b, sg_ln_g, sg_ln_b,
                         w_br, w_o, ln_mix_g, ln_mix_b, w_router, router_bias, gu_w, dn_w,
                         ln_ffn_g, ln_ffn_b, out):
    scratch = lambda name, shape: nc.dram_tensor(name, shape, F32).ap()
    h_dram = scratch("h_scratch", [S, D])
    projT = scratch("projT_scratch", [COLS, P, S])
    v_nat = scratch("v_scratch", [S, W])
    yT = scratch("yT_scratch", [P, 3 * W // P, S])
    mergedT = scratch("mergedT_scratch", [KT, P, S])
    h2_dram = scratch("h2_scratch", [S + P, D])
    order = scratch("order_scratch", [E_TILES * P, META])
    with ExitStack() as ctx:
        sems = {}

        def sem(name):
            if name not in sems:
                sems[name] = ctx.enter_context(nc.semaphore(name))
            return sems[name]

        ident = ctx.enter_context(nc.sbuf_tensor("ident", [P, P], F32))
        logits = ctx.enter_context(nc.sbuf_tensor("logits", [P, TILES, E], F32))
        with ExitStack() as phase:
            hT_hi = phase.enter_context(nc.sbuf_tensor("hT_hi", [P, KT, S], F32R))
            hT_lo = phase.enter_context(nc.sbuf_tensor("hT_lo", [P, KT, S], F32R))
            w_raw = phase.enter_context(nc.sbuf_tensor("w_raw", [P, 2, KT * P], F32))
            w_hi = phase.enter_context(nc.sbuf_tensor("w_hi", [P, 2, KT * P], F32R))
            w_lo = phase.enter_context(nc.sbuf_tensor("w_lo", [P, 2, KT * P], F32R))
            w_loaded = [sem(f"w_loaded{b}") for b in range(2)]
            w_high, w_split = sem("w_high"), sem("w_split")
            weights = (w_raw, w_hi, w_lo, w_loaded, w_high, w_split)
            norm_and_project(nc, sem, x, ln_in_g, ln_in_b, h_dram, w_in, *weights, projT, hT_hi, hT_lo, ident)
            gates_and_local_mixers(nc, sem, w_in, *weights, b_gate, projT, hT_hi, hT_lo, conv_w,
                                   sg_w, sg_b, sg_ln_g, sg_ln_b, v_nat, yT, ident)
        with nc.sbuf_tensor("w_br_raw", [P, 3 * W // P, D], F32) as w_br_raw:
            w_br_loaded = sem("w_br_loaded")
            attention(nc, sem, projT, v_nat, yT, w_br, w_br_raw, w_br_loaded)
            with nc.sbuf_tensor("w_o_raw", [P, KT, D], F32) as w_o_raw:
                w_o_loaded = sem("w_o_loaded")
                merge_branches(nc, sem, projT, yT, w_br_raw, w_br_loaded, mergedT, w_o, w_o_raw, w_o_loaded)
                mix_out(nc, sem, mergedT, w_o_raw, w_o_loaded, h_dram, ln_mix_g, ln_mix_b, w_router, h2_dram,
                        logits, ident)
        meta = ctx.enter_context(nc.sbuf_tensor("meta", [P, E_TILES, META], F32))
        table = ctx.enter_context(nc.sbuf_tensor("table", [1, E_TILES + 3], U32))
        gu_raw = ctx.enter_context(nc.sbuf_tensor("gu_raw", [P, 2, GUC, 2 * EG * FF], F32))
        dn_raw = ctx.enter_context(nc.sbuf_tensor("dn_raw", [P, DSLOTS, DNC, D], F32))
        gu_loaded, dn_loaded = sem("gu_loaded"), sem("dn_loaded")
        dispatch(nc, sem, logits, router_bias, order, meta, table, gu_w, dn_w, gu_raw, dn_raw, gu_loaded, dn_loaded)
        experts(nc, sem, h2_dram, meta, table, gu_w, dn_w, gu_raw, dn_raw, gu_loaded, dn_loaded,
                ln_ffn_g, ln_ffn_b, out, ident)


def kernel(**inputs):
    import numpy as np
    import concourse.bacc as bacc
    from concourse.bass_utils import run_bass_kernel_spmd

    w = {name: np.asarray(a) for name, a in inputs.items()}
    by_rows = lambda a: a.reshape(-1, P, a.shape[-1]).transpose(1, 0, 2)
    ffn_in = lambda a: a.reshape(EG, EG, KT, P, FF).transpose(0, 3, 2, 1, 4).reshape(EG, P, KT, EG * FF)
    arrays = {
        "x": w["x"].reshape(S, D),
        "ln_in_g": w["ln_in_g"],
        "ln_in_b": w["ln_in_b"],
        "w_in": w["w_in"].reshape(KT, P, COLS, P).transpose(2, 1, 0, 3).reshape(COLS, P, D),
        "b_gate": w["b_gate"].reshape(COLS - GATES, P).T,
        "conv_w": w["conv_w"].reshape(3, W // P, P).transpose(2, 1, 0),
        "sg_w": w["sg_w"][0].transpose(2, 0, 1),
        "sg_b": w["sg_b"][0],
        "sg_ln_g": w["sg_ln_g"][0],
        "sg_ln_b": w["sg_ln_b"][0],
        "w_br": by_rows(w["w_br"].reshape(3 * W, D)),
        "w_o": by_rows(w["w_o"][0]),
        "ln_mix_g": w["ln_mix_g"][0],
        "ln_mix_b": w["ln_mix_b"][0],
        "w_router": by_rows(w["w_router"]),
        "router_bias": w["router_bias"],
        "gu_w": np.concatenate([ffn_in(w["w_gate"][0]), ffn_in(w["w_up"][0])], axis=-1),
        "dn_w": w["w_down"].reshape(EG, EG, FF, D).transpose(0, 2, 1, 3),
        "ln_ffn_g": w["ln_ffn_g"][0],
        "ln_ffn_b": w["ln_ffn_b"][0],
    }
    arrays = {f"{name}_in": np.ascontiguousarray(a) for name, a in arrays.items()}
    nc = bacc.Bacc("TRN2", target_bir_lowering=False, num_devices=1)
    args = [nc.dram_tensor(name, a.shape, mybir.dt.from_np(a.dtype), kind="ExternalInput").ap()
            for name, a in arrays.items()]
    out = nc.dram_tensor("layer_out", (1, S, D), F32, kind="ExternalOutput").ap()
    hybrid_decoder_layer(nc, *args, out.rearrange("o s d -> (o s) d"))
    r = run_bass_kernel_spmd(nc, [arrays], core_ids=[0])
    return r.results[0]["layer_out"]
```
